# Optimizing a Trainium2 kernel written in Bass

```python
import jax
import jax.numpy as jnp
from jax import lax
import numpy as np

D_MODEL = 1024
BATCH = 1
SEQ = 256
DEPTH = 2

GRID_W = 64
CTX_LEN = 256
BLOCK = 128
HEAD_DIM = 64
ROPE_THETA = 10000.0
EPS = 1e-6
NEG_INF = -1e30

A_Q_HEADS = 8
A_KV_HEADS = 2
A_WINDOW = 128
B_HEADS = 8
B_NOPE = 64
B_ROPE = 32
B_QK = B_NOPE + B_ROPE
B_V = 64
B_Q_RANK = 256
B_KV_RANK = 256
C_HEADS = 4
C_DK = 64
C_DV = 128
D_Q_HEADS = 8
D_KV_HEADS = 2
PEER_HEADS = 8
PEER_N_KEYS = 128
PEER_N_EXPERTS = PEER_N_KEYS * PEER_N_KEYS
PEER_D_KEY = 256
PEER_TOPK = 16
PEER_BLOCK = 128

N_AB = (DEPTH + 1) // 2
N_CD = DEPTH // 2

A_Q_W = A_Q_HEADS * HEAD_DIM
A_KV_W = A_KV_HEADS * HEAD_DIM
AB_SPLITS = (A_Q_W, A_KV_W, A_KV_W, B_Q_RANK, B_KV_RANK, B_ROPE)
AB_IN = sum(AB_SPLITS)
AB_OUT = A_Q_W + B_HEADS * B_V
C_QK_W = C_HEADS * C_DK
C_V_W = C_HEADS * C_DV
D_Q_W = D_Q_HEADS * HEAD_DIM
D_KV_W = D_KV_HEADS * HEAD_DIM
CD_SPLITS = (C_QK_W, C_QK_W, C_V_W, C_V_W, D_Q_W, D_KV_W, D_KV_W)
CD_IN = sum(CD_SPLITS)
CD_OUT = C_V_W + D_Q_W

kernel_name = "hybrid_dit_window_mla_retention_axialgqa_peer"

def rms_norm(x, w):
    xf = x.astype(jnp.float32)
    y = xf * lax.rsqrt(jnp.mean(xf * xf, axis=-1, keepdims=True) + EPS)
    return (y * w.astype(jnp.float32)).astype(x.dtype)

def modulate(x, w, shift, scale):
    return rms_norm(x, w) * (1 + scale) + shift

def split_cols(z, widths):
    offsets = [int(o) for o in np.cumsum(widths)[:-1]]
    return jnp.split(z, offsets, axis=-1)

def grid_positions(n_tokens):
    rows = n_tokens // GRID_W
    row = jnp.repeat(jnp.arange(rows, dtype=jnp.int32), GRID_W)
    col = jnp.tile(jnp.arange(GRID_W, dtype=jnp.int32), rows)
    return row, col

def rope_1d(x, pos):
    half = x.shape[-1] // 2
    freqs = ROPE_THETA ** (-jnp.arange(half, dtype=jnp.float32) / half)
    ang = pos.astype(jnp.float32)[:, None] * freqs[None, :]
    cos = jnp.cos(ang)[:, None, :]
    sin = jnp.sin(ang)[:, None, :]
    xf = x.astype(jnp.float32)
    x1, x2 = xf[..., :half], xf[..., half:]
    return jnp.concatenate([x1 * cos - x2 * sin, x2 * cos + x1 * sin], axis=-1).astype(x.dtype)

def axial_rope(x, row, col):
    d = x.shape[-1] // 2
    return jnp.concatenate([rope_1d(x[..., :d], row), rope_1d(x[..., d:], col)], axis=-1)

def attend(q, k, v, sink=None):
    B, Q, Hq, d = q.shape
    Hkv = k.shape[2]
    G = Hq // Hkv
    qg = q.reshape(B, Q, Hkv, G, d)
    s = jnp.einsum('bqhgd,bkhd->bhgqk', qg, k).astype(jnp.float32) * d ** -0.5
    if sink is not None:
        s_sink = jnp.broadcast_to(sink.astype(jnp.float32).reshape(1, Hkv, G, 1, 1), s.shape[:-1] + (1,))
        p = jax.nn.softmax(jnp.concatenate([s, s_sink], axis=-1), axis=-1)[..., :-1]
    else:
        p = jax.nn.softmax(s, axis=-1)
    o = jnp.einsum('bhgqk,bkhd->bqhgd', p.astype(v.dtype), v)
    return o.reshape(B, Q, Hq * v.shape[-1])

def blocked_attention(q, k, v):
    B, S = q.shape[:2]
    nb = S // BLOCK
    qb = q.reshape((B, nb, BLOCK) + q.shape[2:]).swapaxes(0, 1)
    o = lax.map(lambda qq: attend(qq, k, v), qb)
    return o.swapaxes(0, 1).reshape(B, S, -1)

def window_attention(q, k, v, kc, vc, sink):
    B, S, Hq, d = q.shape
    Hkv = k.shape[2]
    G = Hq // Hkv
    nb = S // BLOCK
    scale = d ** -0.5
    qb = q.reshape(B, nb, BLOCK, Hkv, G, d)
    pad = ((0, 0), (BLOCK, BLOCK), (0, 0), (0, 0))
    kp = jnp.pad(k, pad).reshape(B, nb + 2, BLOCK, Hkv, d)
    vp = jnp.pad(v, pad).reshape(B, nb + 2, BLOCK, Hkv, v.shape[-1])
    kw = jnp.concatenate([kp[:, :-2], kp[:, 1:-1], kp[:, 2:]], axis=2)
    vw = jnp.concatenate([vp[:, :-2], vp[:, 1:-1], vp[:, 2:]], axis=2)
    qi = jnp.arange(BLOCK)[:, None]
    kj = jnp.arange(3 * BLOCK)[None, :]
    kpos = jnp.arange(nb)[:, None, None] * BLOCK + kj[None] - BLOCK
    valid = (jnp.abs(kj - BLOCK - qi)[None] <= A_WINDOW) & (kpos >= 0) & (kpos < S)
    s_loc = jnp.einsum('bnqhgd,bnkhd->bnhgqk', qb, kw).astype(jnp.float32) * scale
    s_loc = jnp.where(valid[None, :, None, None], s_loc, NEG_INF)
    s_ctx = jnp.einsum('bnqhgd,blhd->bnhgql', qb, kc).astype(jnp.float32) * scale
    s_sink = jnp.broadcast_to(sink.astype(jnp.float32).reshape(1, 1, Hkv, G, 1, 1), s_loc.shape[:-1] + (1,))
    p = jax.nn.softmax(jnp.concatenate([s_loc, s_ctx, s_sink], axis=-1), axis=-1).astype(v.dtype)
    nw = 3 * BLOCK
    o = (jnp.einsum('bnhgqk,bnkhd->bnqhgd', p[..., :nw], vw)
         + jnp.einsum('bnhgql,blhd->bnqhgd', p[..., nw:-1], vc))
    return o.reshape(B, S, Hq * v.shape[-1])

def retention_chunked(q, k, v, log_gamma, s0):
    q = q.astype(jnp.float32)
    k = k.astype(jnp.float32)
    v = v.astype(jnp.float32)
    B, S, H, dk = q.shape
    dv = v.shape[-1]
    nc = S // BLOCK
    idx = jnp.arange(BLOCK, dtype=jnp.float32)
    diff = idx[:, None] - idx[None, :]
    lg = log_gamma[:, None, None]
    decay_in = jnp.exp(lg * jnp.maximum(diff, 0.0)) * (diff >= 0)
    q_dec = jnp.exp(log_gamma[:, None] * (idx[None, :] + 1.0))
    k_dec = jnp.exp(log_gamma[:, None] * (BLOCK - 1.0 - idx[None, :]))
    chunk_dec = jnp.exp(log_gamma * BLOCK)
    qc = q.reshape(B, nc, BLOCK, H, dk).transpose(1, 0, 3, 2, 4)
    kc = k.reshape(B, nc, BLOCK, H, dk).transpose(1, 0, 3, 2, 4)
    vc = v.reshape(B, nc, BLOCK, H, dv).transpose(1, 0, 3, 2, 4)

    def step(state, inp):
        qi, ki, vi = inp
        s = jnp.einsum('bhqd,bhkd->bhqk', qi, ki) * decay_in
        inner = jnp.einsum('bhqk,bhkv->bhqv', s, vi)
        cross = jnp.einsum('bhqd,bhdv->bhqv', qi, state) * q_dec[None, :, :, None]
        new_state = (state * chunk_dec[None, :, None, None]
                     + jnp.einsum('bhkd,bhkv->bhdv', ki * k_dec[None, :, :, None], vi))
        return new_state, inner + cross

    s_fin, o = lax.scan(step, s0, (qc, kc, vc))
    return o.transpose(1, 0, 3, 2, 4).reshape(B, S, H, dv), s_fin

def retention_out(o, g, gn_w):
    mu = jnp.mean(o, axis=-1, keepdims=True)
    var = jnp.mean(jnp.square(o - mu), axis=-1, keepdims=True)
    y = ((o - mu) * lax.rsqrt(var + EPS)).reshape(o.shape[0], o.shape[1], C_V_W) * gn_w.astype(jnp.float32)
    return (jax.nn.silu(g.astype(jnp.float32)) * y).astype(g.dtype)

def flip_seq(t):
    return jnp.flip(t, axis=1)

def mixer_ab(h, hc, w_in, w_o, a_qn, a_kn, a_sink, b_qln, b_kvln, b_wuq, b_wukv, b_qn, b_kn,
             row, col, with_ctx_out):
    def project(z, rotate):
        Bz, n = z.shape[:2]
        qa, ka, va, cq, ckv, kr = split_cols(z @ w_in, AB_SPLITS)
        qa = rms_norm(qa.reshape(Bz, n, A_Q_HEADS, HEAD_DIM), a_qn)
        ka = rms_norm(ka.reshape(Bz, n, A_KV_HEADS, HEAD_DIM), a_kn)
        va = va.reshape(Bz, n, A_KV_HEADS, HEAD_DIM)
        qb = rms_norm((rms_norm(cq, b_qln) @ b_wuq).reshape(Bz, n, B_HEADS, B_QK), b_qn)
        kv = (rms_norm(ckv, b_kvln) @ b_wukv).reshape(Bz, n, B_HEADS, B_NOPE + B_V)
        kb = jnp.concatenate([kv[..., :B_NOPE],
                              jnp.broadcast_to(kr[:, :, None, :], (Bz, n, B_HEADS, B_ROPE))], axis=-1)
        kb = rms_norm(kb, b_kn)
        vb = kv[..., B_NOPE:]
        if rotate:
            qa = axial_rope(qa, row, col)
            ka = axial_rope(ka, row, col)
            qb = jnp.concatenate([qb[..., :B_NOPE], axial_rope(qb[..., B_NOPE:], row, col)], axis=-1)
            kb = jnp.concatenate([kb[..., :B_NOPE], axial_rope(kb[..., B_NOPE:], row, col)], axis=-1)
        return qa, ka, va, qb, kb, vb

    qa, ka, va, qb, kb, vb = project(h, True)
    qac, kac, vac, qbc, kbc, vbc = project(hc, False)
    o_a = window_attention(qa, ka, va, kac, vac, a_sink)
    o_b = blocked_attention(qb, jnp.concatenate([kbc, kb], axis=1), jnp.concatenate([vbc, vb], axis=1))
    y = jnp.concatenate([o_a, o_b], axis=-1) @ w_o
    yc = None
    if with_ctx_out:
        yc = jnp.concatenate([attend(qac, kac, vac, a_sink), attend(qbc, kbc, vbc)], axis=-1) @ w_o
    return y, yc

def mixer_cd(h, hc, w_in, w_o, dec_f, dec_b, gn_w, d_qn, d_kn, row, col, with_ctx_out):
    def project(z, rotate):
        Bz, n = z.shape[:2]
        q_r, k_r, v_r, g_r, q_d, k_d, v_d = split_cols(z @ w_in, CD_SPLITS)
        q_r = q_r.reshape(Bz, n, C_HEADS, C_DK)
        k_r = k_r.reshape(Bz, n, C_HEADS, C_DK) * C_DK ** -0.5
        v_r = v_r.reshape(Bz, n, C_HEADS, C_DV)
        q_d = rms_norm(q_d.reshape(Bz, n, D_Q_HEADS, HEAD_DIM), d_qn)
        k_d = rms_norm(k_d.reshape(Bz, n, D_KV_HEADS, HEAD_DIM), d_kn)
        v_d = v_d.reshape(Bz, n, D_KV_HEADS, HEAD_DIM)
        if rotate:
            q_r = axial_rope(q_r, row, col)
            k_r = axial_rope(k_r, row, col)
            q_d = axial_rope(q_d, row, col)
            k_d = axial_rope(k_d, row, col)
        return q_r, k_r, v_r, g_r, q_d, k_d, v_d

    q_r, k_r, v_r, g_r, q_d, k_d, v_d = project(h, True)
    q_rc, k_rc, v_rc, g_rc, q_dc, k_dc, v_dc = project(hc, False)
    lg_f = jax.nn.log_sigmoid(dec_f.astype(jnp.float32))
    lg_b = jax.nn.log_sigmoid(dec_b.astype(jnp.float32))
    zero = jnp.zeros((h.shape[0], C_HEADS, C_DK, C_DV), jnp.float32)
    oc_f, st_f = retention_chunked(q_rc, k_rc, v_rc, lg_f, zero)
    oc_b, st_b = retention_chunked(flip_seq(q_rc), flip_seq(k_rc), flip_seq(v_rc), lg_b, zero)
    o_f, _ = retention_chunked(q_r, k_r, v_r, lg_f, st_f)
    o_b, _ = retention_chunked(flip_seq(q_r), flip_seq(k_r), flip_seq(v_r), lg_b, st_b)
    y_ret = retention_out(o_f + flip_seq(o_b), g_r, gn_w)
    o_d = blocked_attention(q_d, jnp.concatenate([k_dc, k_d], axis=1), jnp.concatenate([v_dc, v_d], axis=1))
    y = jnp.concatenate([y_ret, o_d], axis=-1) @ w_o
    yc = None
    if with_ctx_out:
        yc_ret = retention_out(oc_f + flip_seq(oc_b), g_rc, gn_w)
        yc = jnp.concatenate([yc_ret, attend(q_dc, k_dc, v_dc)], axis=-1) @ w_o
    return y, yc

def peer(h, w_q, sub_keys, u_tab, v_tab):
    T, D = h.shape
    q = (h @ w_q).reshape(T, PEER_HEADS, 2, PEER_D_KEY // 2)
    scores = jnp.einsum('thpd,hpnd->thpn', q, sub_keys).astype(jnp.float32)
    s_top, i_top = lax.top_k(scores, PEER_TOPK)
    cand = s_top[:, :, 0, :, None] + s_top[:, :, 1, None, :]
    cand_idx = i_top[:, :, 0, :, None] * PEER_N_KEYS + i_top[:, :, 1, None, :]
    best, pos = lax.top_k(cand.reshape(T, PEER_HEADS, PEER_TOPK * PEER_TOPK), PEER_TOPK)
    experts = jnp.take_along_axis(cand_idx.reshape(T, PEER_HEADS, PEER_TOPK * PEER_TOPK), pos, axis=-1)
    gates = jax.nn.softmax(best, axis=-1)
    nblk = T // PEER_BLOCK
    hk = PEER_HEADS * PEER_TOPK

    def one_block(args):
        hb, eb, gb = args
        u = u_tab[eb]
        a = jax.nn.gelu(jnp.einsum('cd,ced->ce', hb, u).astype(jnp.float32))
        return jnp.einsum('ce,ced->cd', (gb * a).astype(hb.dtype), v_tab[eb])

    out = lax.map(one_block, (h.reshape(nblk, PEER_BLOCK, D),
                              experts.reshape(nblk, PEER_BLOCK, hk),
                              gates.reshape(nblk, PEER_BLOCK, hk)))
    return out.reshape(T, D)

def setup_inputs(seed: int = 0) -> dict:
    key = jax.random.key(seed)
    ks = iter(jax.random.split(key, 40))

    def normal(shape, scale):
        return jax.random.normal(next(ks), shape, jnp.float32) * scale

    def gain(shape):
        return 1.0 + normal(shape, 0.02)

    base = 1.0 - 2.0 ** (-5.0 - np.arange(C_HEADS))
    decay_logit = jnp.asarray(np.log(base / (1.0 - base)), jnp.float32)
    return {
        "x": normal((BATCH, SEQ, D_MODEL), 1.0),
        "c": normal((BATCH, D_MODEL), 1.0),
        "ctx": normal((BATCH, CTX_LEN, D_MODEL), 1.0),
        "c_ctx": normal((D_MODEL,), 1.0),
        "ada_w": normal((DEPTH, D_MODEL, 6 * D_MODEL), 0.5 * D_MODEL ** -0.5),
        "ada_b": normal((DEPTH, 6 * D_MODEL), 0.02),
        "norm1_w": gain((DEPTH, D_MODEL)),
        "norm2_w": gain((DEPTH, D_MODEL)),
        "ab_w_in": normal((N_AB, D_MODEL, AB_IN), D_MODEL ** -0.5),
        "ab_w_o": normal((N_AB, AB_OUT, D_MODEL), AB_OUT ** -0.5),
        "a_q_norm": gain((N_AB, HEAD_DIM)),
        "a_k_norm": gain((N_AB, HEAD_DIM)),
        "a_sink": normal((N_AB, A_Q_HEADS), 0.5),
        "b_q_lora_norm": gain((N_AB, B_Q_RANK)),
        "b_kv_lora_norm": gain((N_AB, B_KV_RANK)),
        "b_w_uq": normal((N_AB, B_Q_RANK, B_HEADS * B_QK), B_Q_RANK ** -0.5),
        "b_w_ukv": normal((N_AB, B_KV_RANK, B_HEADS * (B_NOPE + B_V)), B_KV_RANK ** -0.5),
        "b_q_norm": gain((N_AB, B_QK)),
        "b_k_norm": gain((N_AB, B_QK)),
        "cd_w_in": normal((N_CD, D_MODEL, CD_IN), D_MODEL ** -0.5),
        "cd_w_o": normal((N_CD, CD_OUT, D_MODEL), CD_OUT ** -0.5),
        "c_decay_fwd": decay_logit + normal((N_CD, C_HEADS), 0.05),
        "c_decay_bwd": decay_logit + normal((N_CD, C_HEADS), 0.05),
        "c_gn_w": gain((N_CD, C_V_W)),
        "d_q_norm": gain((N_CD, HEAD_DIM)),
        "d_k_norm": gain((N_CD, HEAD_DIM)),
        "peer_w_q": normal((DEPTH, D_MODEL, PEER_HEADS * PEER_D_KEY), D_MODEL ** -0.5),
        "peer_keys": normal((DEPTH, PEER_HEADS, 2, PEER_N_KEYS, PEER_D_KEY // 2), (PEER_D_KEY // 2) ** -0.5),
        "peer_u": normal((DEPTH, PEER_N_EXPERTS, D_MODEL), D_MODEL ** -0.5),
        "peer_v": normal((DEPTH, PEER_N_EXPERTS, D_MODEL), 0.1),
    }

def reference(x, c, ctx, c_ctx, ada_w, ada_b, norm1_w, norm2_w, ab_w_in, ab_w_o, a_q_norm, a_k_norm,
              a_sink, b_q_lora_norm, b_kv_lora_norm, b_w_uq, b_w_ukv, b_q_norm, b_k_norm, cd_w_in, cd_w_o,
              c_decay_fwd, c_decay_bwd, c_gn_w, d_q_norm, d_k_norm, peer_w_q, peer_keys, peer_u, peer_v):
    B, S, D = x.shape
    row, col = grid_positions(S)
    xc = ctx
    for l in range(DEPTH):
        last = l == DEPTH - 1
        i = l // 2
        mod = jax.nn.silu(c) @ ada_w[l] + ada_b[l]
        mod_c = jax.nn.silu(c_ctx) @ ada_w[l] + ada_b[l]
        sh1, sc1, g1, sh2, sc2, g2 = jnp.split(mod[:, None, :], 6, axis=-1)
        sh1c, sc1c, g1c, sh2c, sc2c, g2c = jnp.split(mod_c, 6, axis=-1)
        h = modulate(x, norm1_w[l], sh1, sc1)
        hc = modulate(xc, norm1_w[l], sh1c, sc1c)
        if l % 2 == 0:
            y, yc = mixer_ab(h, hc, ab_w_in[i], ab_w_o[i], a_q_norm[i], a_k_norm[i], a_sink[i],
                             b_q_lora_norm[i], b_kv_lora_norm[i], b_w_uq[i], b_w_ukv[i], b_q_norm[i],
                             b_k_norm[i], row, col, not last)
        else:
            y, yc = mixer_cd(h, hc, cd_w_in[i], cd_w_o[i], c_decay_fwd[i], c_decay_bwd[i], c_gn_w[i],
                             d_q_norm[i], d_k_norm[i], row, col, not last)
        x = x + g1 * y
        h2 = modulate(x, norm2_w[l], sh2, sc2)
        if last:
            f = peer(h2.reshape(B * S, D), peer_w_q[l], peer_keys[l], peer_u[l], peer_v[l])
            x = x + g2 * f.reshape(B, S, D)
        else:
            xc = xc + g1c * yc
            h2c = modulate(xc, norm2_w[l], sh2c, sc2c)
            f = peer(jnp.concatenate([h2.reshape(B * S, D), h2c.reshape(-1, D)], axis=0),
                     peer_w_q[l], peer_keys[l], peer_u[l], peer_v[l])
            x = x + g2 * f[:B * S].reshape(B, S, D)
            xc = xc + g2c * f[B * S:].reshape(xc.shape)
    return x


_drawn_inputs = setup_inputs


def setup_inputs(seed=0):
    import zlib

    import numpy as np

    out = dict(_drawn_inputs(seed))
    spreads = {}
    factors = {'ada_b': 3.17,
     'norm1_w': 8.0,
     'norm2_w': 8.0,
     'a_q_norm': 8.0,
     'a_k_norm': 8.0,
     'a_sink': 8.0,
     'b_q_lora_norm': 8.0,
     'b_kv_lora_norm': 8.0,
     'b_w_uq': 2.945,
     'b_q_norm': 8.0,
     'b_k_norm': 8.0,
     'c_gn_w': 8.0,
     'd_q_norm': 8.0,
     'd_k_norm': 8.0}
    for name, (base, spread) in spreads.items():
        noise = np.random.default_rng([zlib.crc32(name.encode()), seed]).standard_normal(out[name].shape)
        drawn = base * np.exp(spread * noise) if base else spread * noise
        out[name] = jnp.asarray(drawn.astype(out[name].dtype))
    for name, factor in factors.items():
        out[name] = (out[name] * factor).astype(out[name].dtype)
    return out
```

```python
from contextlib import ExitStack

import numpy as np
import concourse.bass as bass
from concourse import mybir

F32 = mybir.dt.float32
U32 = mybir.dt.uint32
ACT = mybir.ActivationFunctionType
ALU = mybir.AluOpType
AXX = mybir.AxisListType.X

P = 128
D = 1024
KC = D // P
X = 256
T = 512
GRID_W = 64
HD = 64
EPS = 1e-6
NEG = -1e30
LOWEST = -3.0e38
HEADS = 8
NSEL = 128
SLOTS = 8
GRP = 256
GRP_TILES = GRP // P
MODS = 6 * KC

PR = {}
_at = 0
for _name, _n in (("n1", 16), ("n2", 16), ("ada_b", 96), ("aq", 1), ("ak", 1), ("bql", 2), ("bkvl", 2),
                  ("bq", 1), ("bk", 1), ("gn", 4), ("dq", 1), ("dk", 1), ("c", 16), ("sink", 8),
                  ("decf", 4), ("decb", 4), ("eps", 1), ("one", 1)):
    PR[_name] = _at
    _at += _n
NPR = _at

TAB = [{}, {}]
TABW = [0, 0]
for _l, _spec in enumerate(((("cosA", 512), ("sinA", 512), ("bo64", 128), ("rot64", 128), ("ones", 128),
                             ("cosB", 512), ("sinB", 512), ("bo96", 128), ("rot96", 128),
                             ("m01", 128), ("m10", 128)),
                            (("cosA", 512), ("sinA", 512), ("bo64", 128), ("rot64", 128), ("ones", 128),
                             ("df", 1024), ("db", 1024), ("mf", 512), ("mb", 512)))):
    for _name, _n in _spec:
        TAB[_l][_name] = (TABW[_l], _n)
        TABW[_l] += _n


class Step:

    def __init__(self, eng, sem):
        self.eng, self.sem, self.n = eng, sem, 0

    def inc(self, ins):
        ins.then_inc(self.sem, 1)
        self.n = self.n + 1

    def wait(self):
        self.eng.wait_ge(self.sem, self.n)

    def do(self, ins):
        self.inc(ins)
        self.wait()


def build(nc, A, out):
    with ExitStack() as ctx:
        def sb(name, shape, dt=F32):
            return ctx.enter_context(nc.sbuf_tensor(name, shape, dt))

        def sem(name):
            return ctx.enter_context(nc.semaphore(name))

        xt = sb("xt", [P, KC, T])
        ht = sb("ht", [P, KC, T])
        ring = sb("ring", [P, SLOTS, D])
        sel = sb("sel", [P, 2, T])
        sel2 = sb("sel2", [P, T], mybir.dt.bfloat16)
        scr = sb("scr", [P, 2048])
        cst = sb("cst", [P, 2, P])
        par = sb("par", [P, NPR])
        cs = sb("cs", [P, KC, 2])
        mod = sb("mod", [P, 2, MODS, 2])
        gain = sb("gain", [P, 4, KC, 2])
        arena = sb("arena", [P, P * GRP])
        ident, iota = cst[:, 0, :], cst[:, 1, :]
        oha = scr[:, 0:1024].rearrange("p (b t n) -> p b t n", b=2, t=4)
        ohb = scr[:, 1024:2048].rearrange("p (b t n) -> p b t n", b=2, t=4)
        gel = scr[:, 0:512].rearrange("p (b t) -> p b t", b=2)
        wt = scr[:, 512:1024].rearrange("p (b t) -> p b t", b=2)
        gates = arena[:, :].rearrange("p (i t) -> p i t", t=GRP)
        ps = ctx.enter_context(nc.psum_tensor("ps", [P, 8, 512], F32))

        def carve(spec):
            at, got = 0, {}
            for name, dims in spec:
                n = int(np.prod(dims))
                v = arena[:, at:at + n]
                if len(dims) == 2:
                    v = v.rearrange("p (a b) -> p a b", a=dims[0])
                if len(dims) == 3:
                    v = v.rearrange("p (a b c) -> p a b c", a=dims[0], b=dims[1])
                got[name] = v
                at += n
            assert at <= P * GRP, at
            return got

        common = [("tab", (max(TABW),)), ("nrt", (T,)), ("nrb", (T,)),
                  ("zw", (2, T)), ("zsq", (2, T)), ("rt", (2, T)), ("ri", (T,)), ("ta", (T,)), ("tb", (T,)),
                  ("dg", (2, P)), ("st", (5, 64))]
        m0 = carve(common + [("qa", (4, T)), ("ka", (T,)), ("va", (4, P)), ("qb", (8, T)), ("kb", (8, T)),
                             ("vb", (4, T)), ("lq", (2, T)), ("lkv", (2, T)), ("zk", (2, T)), ("zks", (2, T)),
                             ("oa", (8, T))])
        m1 = carve(common + [("qr", (2, X)), ("kr", (2, T)), ("qd", (4, X)), ("kd", (T,)), ("vr", (4, T)),
                             ("vd", (4, P)), ("sg", (4, X)), ("oa", (8, X)), ("dt", (4, 4, X)),
                             ("de", (2, 4 * X)), ("sd", (2, 4, X)), ("lg", (16,)), ("orr", (4, X)),
                             ("osq", (4, X)), ("ort", (4 * X,))])
        tk = carve([("qt", (16, T)), ("sc", (2, 16, P)), ("cd", (HEADS, 256)), ("eq", (P, 16)),
                    ("v", (16, 16)), ("if", (16, 16)), ("bv", (HEADS, 16)), ("pf", (2, P)),
                    ("g", (2, 3, P)), ("sm", (2, HEADS)), ("i", (16, 16)), ("pi", (3, P))])
        keys = arena[:, P * GRP - 16 * P:P * GRP].rearrange("p (a b) -> p a b", a=16)
        iu = tk["i"].bitcast(U32)
        piu = tk["pi"].bitcast(U32)
        mix = [m0, m1]
        for m in mix:
            m["sq8"], m["nt"] = m["zsq"], m["zw"]
            m["pr"], m["pts"] = m["zw"], m["zsq"]

        def tab(l, name):
            a, n = TAB[l][name]
            return mix[l]["tab"][:, a:a + n]

        def pcol(name, i=0, n=1, rows=slice(0, P)):
            return par[rows, PR[name] + i:PR[name] + i + n]

        s_par = sem("s_par")
        s_x = sem("s_x")
        s_tab = [sem(f"s_tab{l}") for l in range(2)]
        s_key = sem("s_key")
        s_slot = [sem(f"s_slot{i}") for i in range(SLOTS)]
        s_cs = sem("s_cs")
        s_ada = sem("s_ada")
        s_mod = sem("s_mod")
        s_nsq = sem("s_nsq")
        s_nss = sem("s_nss")
        s_nrt = sem("s_nrt")
        s_nt = sem("s_nt")
        s_nh = sem("s_nh")
        s_xt = sem("s_xt")
        s_z = [sem(f"s_z{l}") for l in range(2)]
        s_zw = [sem(f"s_zw{l}") for l in range(2)]
        s_rx = [sem(f"s_rx{l}") for l in range(2)]
        s_rt = [sem(f"s_rt{l}") for l in range(2)]
        s_it = [sem(f"s_it{l}") for l in range(2)]
        s_s = [sem(f"s_s{l}") for l in range(2)]
        s_nm = [sem(f"s_nm{l}") for l in range(2)]
        s_p = [sem(f"s_p{l}") for l in range(2)]
        s_dg = [sem(f"s_dg{l}") for l in range(2)]
        s_pt = [sem(f"s_pt{l}") for l in range(2)]
        s_pe = [sem(f"s_pe{l}") for l in range(2)]
        s_pv = [sem(f"s_pv{l}") for l in range(2)]
        s_oe = [sem(f"s_oe{l}") for l in range(2)]
        s_wo = sem("s_wo")
        s_q = sem("s_q")
        s_qe = sem("s_qe")
        s_sc = sem("s_sc")
        s_sce = sem("s_sce")
        s_best = sem("s_best")
        s_bexp = sem("s_bexp")
        s_tk = sem("s_tk")
        s_tt = sem("s_tt")
        s_sel = sem("s_sel")
        s_oh = sem("s_oh")
        s_g = sem("s_g")
        s_ge = sem("s_ge")
        s_a = sem("s_a")
        s_gel = sem("s_gel")
        s_w = sem("s_w")
        s_y = sem("s_y")
        s_ye = sem("s_ye")
        s_yt = sem("s_yt")
        s_ex = sem("s_ex")
        s_dt = sem("s_dt")
        s_rs = sem("s_rs")
        s_rd = sem("s_rd")
        s_ro = sem("s_ro")
        s_roe = sem("s_roe")
        s_mu = sem("s_mu")
        s_oc = sem("s_oc")
        s_osq = sem("s_osq")
        s_yr = sem("s_yr")
        s_out = sem("s_out")
        s_act = sem("s_act")
        s_dve = sem("s_dve")

        loads, freed = [], {}

        def load(key, src, freed_by):
            loads.append((key, src))
            freed[key] = freed_by

        adas = [(0, 0, 16), (0, 16, 40), (0, 40, 48), (1, 0, 48)]
        ada_done = [sum(b - a for _, a, b in adas[:g]) for g in range(len(adas))]

        def load_ada(g):
            l, a, b = adas[g]
            for m in range(a, b):
                load(("ada", l, m), A["ada"][l, m].rearrange("p k m -> p (k m)"), (s_ada, ada_done[g] + m - a + 1))

        def hk(k, a=0, b=T):
            return ht[:, k, a:b]

        def item(kind, groups, rows=slice(0, P), n=T, **kw):
            return dict(kind=kind, groups=groups, rows=rows, n=n, **kw)

        def feat(key, rows=slice(0, P), cols=slice(0, P), n=T, w=P):
            return (rows, slice(0, n), [(key, (k, w, cols), hk(k, 0, n)) for k in range(KC)])

        items0 = []
        for j in range(4):
            items0.append(item("rope", [feat(("w0", j))], w=pcol("aq"), dest=m0["qa"][:, j, :], tb="A"))
        items0.append(item("rope", [feat(("w0", 4))], w=pcol("ak"), dest=m0["ka"], tb="A"))
        for name, c0, dst in (("bql", 5, "lq"), ("bkvl", 7, "lkv")):
            items0.append(item("lora0", [feat(("w0", c0))], w=pcol(name, 0), dest=m0[dst]))
            items0.append(item("lora1", [feat(("w0", c0 + 1))], w=pcol(name, 1), dest=m0[dst]))
        items0.append(item("kr", [feat(("kr", 0), rows=slice(64, 96), cols=slice(0, 32), w=32)],
                           rows=slice(64, 96), w=pcol("bk", rows=slice(64, 96))))
        items0.append(item("plain", [(slice(0, P), slice(t * P, t * P + P),
                                      [(("w0", 9), (k, P, None), hk(k, t * P, t * P + P)) for k in range(KC)])
                                     for t in range(4)], dest=m0["va"].rearrange("p a b -> p (a b)")))
        for h in range(HEADS):
            items0.append(item("rope", [(slice(0, 96), slice(0, T),
                                         [(("uq", h // 4), (k, 384, slice((h % 4) * 96, (h % 4) * 96 + 96)),
                                           m0["lq"][:, k, :]) for k in range(2)])],
                               rows=slice(0, 96), w=pcol("bq", rows=slice(0, 96)), dest=m0["qb"][0:96, h, :], tb="B"))
        for h in range(HEADS):
            items0.append(item("ropek", [(slice(0, 64), slice(0, T),
                                          [(("ukvk", 0), (k, 512, slice(h * 64, h * 64 + 64)), m0["lkv"][:, k, :])
                                           for k in range(2)])],
                               rows=slice(0, 96), w=pcol("bk", rows=slice(0, 64)), dest=m0["kb"][0:96, h, :], tb="B"))
        for t in range(4):
            items0.append(item("plain", [(slice(0, P), slice(0, T),
                                          [(("ukvv", 0), (k, 512, None), m0["lkv"][:, k, t * P:t * P + P])
                                           for k in range(2)])], dest=m0["vb"][:, t, :]))
        items1 = []
        for j in range(4):
            items1.append(item("rope", [feat(("w1", 4 + j), n=X)], n=X, w=pcol("dq"), dest=m1["qd"][:, j, :], tb="A"))
        items1.append(item("rope", [feat(("w1", 8))], w=pcol("dk"), dest=m1["kd"], tb="A"))
        for j in range(2):
            items1.append(item("rope0", [feat(("w1", j), n=X)], n=X, w=pcol("one"), dest=m1["qr"][:, j, :], tb="A"))
        for j in range(2):
            items1.append(item("rope0", [feat(("w1", 2 + j))], w=pcol("one"), dest=m1["kr"][:, j, :], tb="A"))
        items1.append(item("plain", [(slice(0, P), slice(t * P, t * P + P),
                                      [(("w1", 9), (k, P, None), hk(k, t * P, t * P + P)) for k in range(KC)])
                                     for t in range(4)], dest=m1["vd"].rearrange("p a b -> p (a b)")))
        for t in range(4):
            items1.append(item("plain", [(slice(0, P), slice(0, T),
                                          [(("vr", k // 2), (k % 2, 512, None), hk(k, t * P, t * P + P))
                                           for k in range(KC)])], dest=m1["vr"][:, t, :]))
        for j in range(4):
            items1.append(item("silu", [feat(("w1", 10 + j), n=X)], n=X, dest=m1["sg"][:, j, :]))
        items = [items0, items1]

        def has_rx(it):
            return it["kind"] in ("rope", "ropek", "rope0", "lora1")

        def has_norm(it):
            return it["kind"] in ("rope", "ropek", "lora1")

        rx_upto = [[sum(has_rx(i) for i in its[:c + 1]) for c in range(len(its))] for its in items]
        rt_upto = [[sum(has_norm(i) for i in its[:c + 1]) for c in range(len(its))] for its in items]

        def load_items(l):
            last = {}
            for c, it in enumerate(items[l]):
                for _, _, mms in it["groups"]:
                    for key, _, _ in mms:
                        last[key] = c
            seen = set()
            for it in items[l]:
                for _, _, mms in it["groups"]:
                    for key, _, _ in mms:
                        if key not in seen:
                            seen.add(key)
                            s = A[key[0]][key[1]].rearrange("p k m -> p (k m)")
                            load(key, s, (s_z[l], last[key] + 1))

        def heads(l):
            m, got = mix[l], []
            kinds = ("A", "B") if l == 0 else ("A",)
            nq = 4 if l == 0 else 2
            pair = 0
            for kind in kinds:
                for j in range(4):
                    for qt in range(nq):
                        for half in range(2):
                            po = 64 * half
                            r = slice(po, po + 64)
                            ks, blk = (slice(0, T), range(4)) if qt < 2 else (slice(X, T), range(2, 4))
                            if kind == "A":
                                qn, kn, vn = ("qa", "ka", "va") if l == 0 else ("qd", "kd", "vd")
                                q = m[qn][r, j, qt * P:qt * P + P]
                                k = m[kn][r, ks]
                                v = [m[vn][:, b, po:po + 64] for b in blk]
                                h, sc = j + 4 * half, HD ** -0.5
                            else:
                                h, sc = 2 * j + half, 96 ** -0.5
                                q = m["qb"][0:96, h, qt * P:qt * P + P]
                                k = m["kb"][0:96, h, ks]
                                v = [m["vb"][:, b, h * 64:h * 64 + 64] for b in blk]
                            mask = None
                            if l == 0 and kind == "A" and qt < 2:
                                mask = (1 - qt, tab(0, "m01" if qt == 0 else "m10"))
                            got.append(dict(q=q, k=k, v=v, nb=len(v), mask=mask, sc=float(sc),
                                            sink=pcol("sink", h) if l == 0 and kind == "A" else None,
                                            rows=r, col=qt * P, pair=pair, first=qt == 0 and half == 0,
                                            last=qt == nq - 1 and half == 1,
                                            dest=m["oa"][:, (4 if (kind == "B" or l == 1) else 0) + j, :]))
                    pair += 1
            return got

        att = [heads(0), heads(1)]
        pairs = [8, 4]
        nq_cols = [T, X]
        wo_base = [0, 8]
        xt_base = {"wo0": 0, "peer0": 8, "wo1": 24, "peer1": 32}

        def load_wo(l):
            for m in range(KC):
                load(("wo", l, m), A["wo"][l, m].rearrange("p k m -> p (k m)"), (s_wo, wo_base[l] + m + 1))

        tiles = [4, 2]
        tile_base = [0, 4]
        groups = [(0, 0), (0, 1), (1, 0)]

        def load_peer(l):
            for m in range(16):
                load(("wq", l, m), A["wq"][l, m].rearrange("p k m -> p (k m)"), (s_q, 16 * l + m + 1))

        load_ada(0)
        load_items(0)
        load_ada(1)
        load_wo(0)
        load_peer(0)
        load_ada(2)
        load_ada(3)
        loads.append(("experts", 0))
        loads.append(("experts", 1))
        load_items(1)
        load_wo(1)
        load_peer(1)
        loads.append(("experts", 2))
        slot_of, before, owner, count, pos = {}, {}, [None] * SLOTS, [0] * SLOTS, 0
        expert_count = {}
        for key, src in loads:
            if key == "experts":
                pos = 0
                expert_count[src] = list(count)
                before[("experts", src)] = list(owner)
                for s in range(SLOTS):
                    count[s] += P // 4
                    j = s // 2
                    owner[s] = (s_a, P * src + P - 3 + j) if s % 2 == 0 else (s_y, P * src + P - 3 + j)
                continue
            slot_of[key] = (pos, count[pos])
            before[key] = owner[pos]
            owner[pos] = freed[key]
            count[pos] += 1
            pos = (pos + 1) % SLOTS

        def landed(eng, key):
            slot, n = slot_of[key]
            eng.wait_ge(s_slot[slot], 16 * (n + 1))
            return ring[:, slot, :]

        def tab_dst(l):
            return mix[l]["tab"][:, 0:TABW[l]]

        ys = arena[:, 0:2 * D].rearrange("p (t d) -> p t d", t=GRP_TILES)

        def group_xt(n):
            return [xt_base["peer0"], xt_base["peer0"] + KC, xt_base["peer1"]][n]

        def sc_view(b):
            return tk["sc"][:, b, :, :]

        block = ctx.enter_context(nc.Block())

        @block.sync
        def _(sp):
            sp.dma_start(cst[:, :, :], A["cst"]).then_inc(s_par, 16)
            sp.dma_start(par[:, :], A["par"]).then_inc(s_par, 16)
            for key, src in loads:
                if key == "experts":
                    n = src
                    l, g = groups[n]

                    def pair_load(i, j, c, first):
                        u = A["ut"][l, c].rearrange("a p k m -> p (a k m)") if not first else \
                            A["ut"][l, j].rearrange("p k m -> p (k m)")
                        v = A["vt"][l, c].rearrange("a p d -> p (a d)") if not first else A["vt"][l, j]
                        if first:
                            w = before[("experts", n)][2 * j]
                            sp.wait_ge(w[0], w[1])
                        else:
                            sp.wait_ge(s_a, i * 4 + (P * n + j - 3))
                        sp.dma_start(ring[:, 2 * j, :], u).then_inc(s_slot[2 * j], 16)
                        if first:
                            w = before[("experts", n)][2 * j + 1]
                            sp.wait_ge(w[0], w[1])
                        else:
                            sp.wait_ge(s_y, i * 4 + (P * n + j - 3))
                        sp.dma_start(ring[:, 2 * j + 1, :], v).then_inc(s_slot[2 * j + 1], 16)

                    for j in range(4):
                        pair_load(0, j, None, True)
                    with sp.Fori(1, P // 4) as i:
                        for j in range(4):
                            pair_load(i, j, bass.ds(i * 4 + j, 1), False)
                    continue
                slot, n = slot_of[key]
                if before[key] is not None:
                    sp.wait_ge(before[key][0], before[key][1])
                sp.dma_start(ring[:, slot, 0:src.shape[-1]], src).then_inc(s_slot[slot], 16)
            sp.wait_ge(s_xt, xt_base["peer1"] + KC)
            sp.dma_start(out, xt[:, :, 0:X]).then_inc(s_out, 16)
            sp.wait_ge(s_out, 16)

        @block.gpsimd
        def _(pool):
            pool.dma_start(xt[:, :, :], A["x"]).then_inc(s_x, 16)
            pool.dma_start(tab_dst(0), A["tab0"]).then_inc(s_tab[0], 16)
            pool.wait_ge(s_xt, xt_base["wo0"] + KC)
            pool.dma_start(keys, A["keys"][0]).then_inc(s_key, 16)
            pool.wait_ge(s_xt, xt_base["wo1"])
            pool.dma_start(tab_dst(1), A["tab1"]).then_inc(s_tab[1], 16)
            pool.wait_ge(s_xt, xt_base["peer1"])
            pool.dma_start(keys, A["keys"][1]).then_inc(s_key, 16)

        @block.tensor
        def _(pe):
            mm = pe.matmul

            def modulation(g):
                l, a, b = adas[g]
                if g == 0:
                    pe.wait_ge(s_cs, 1)
                else:
                    pe.wait_ge(s_mod, 2 * g)
                for m in range(a, b):
                    w = landed(pe, ("ada", l, m)).rearrange("p (k m) -> p k m", k=KC)
                    for k in range(KC):
                        last = mm(ps[:, 7, 2 * m:2 * m + 2], w[:, k, :], cs[:, k, :], start=k == 0, stop=k == KC - 1)
                    last.then_inc(s_ada, 1)

            def norm(n):
                width = T if n < 3 else X
                pe.wait_ge(s_tab[n // 2], 16)
                for k in range(KC):
                    pe.wait_ge(s_nsq, KC * n + k + 1)
                    mm(ps[:, 6, 0:width], tab(n // 2, "ones"), mix[n // 2]["sq8"][:, k % 2, 0:width],
                       start=k == 0, stop=k == KC - 1).then_inc(s_nss, 1)

            def project(l, c):
                it = items[l][c]
                if c >= 3:
                    pe.wait_ge(s_zw[l], c - 2)
                if l == 0 and it["kind"] in ("rope", "ropek", "plain") and c >= 11:
                    pe.wait_ge(s_it[0], rx_upto[0][8])
                for rows, cols, mms in it["groups"]:
                    for i, (key, (k, w, wcols), act) in enumerate(mms):
                        wr = landed(pe, key)
                        if wcols is None:
                            lhs, rhs = act, wr[:, k * w:k * w + w]
                        else:
                            lhs, rhs = wr[:, k * w + wcols.start:k * w + wcols.stop], act
                        last = mm(ps[rows, c % 3, cols], lhs, rhs, start=i == 0, stop=i == len(mms) - 1)
                last.then_inc(s_z[l], 1)

            def reduce_rotate(l, c):
                it, m = items[l][c], mix[l]
                if not has_rx(it):
                    return
                pe.wait_ge(s_zw[l], c + 1)
                if c == 0:
                    pe.wait_ge(s_tab[l], 16)
                if c >= 2 and rx_upto[l][c - 2]:
                    pe.wait_ge(s_it[l], rx_upto[l][c - 2])
                r, n = it["rows"], it["n"]
                if it["kind"] == "lora1":
                    mm(ps[:, 3 + c % 2, :], tab(l, "ones"), m["zsq"][:, (c - 1) % 2, :], start=True, stop=False)
                    mm(ps[:, 3 + c % 2, :], tab(l, "ones"), m["zsq"][:, c % 2, :], start=False, stop=True).then_inc(s_rx[l], 1)
                    return
                zw, zsq = (m["zk"], m["zks"]) if it["kind"] == "ropek" else (m["zw"], m["zsq"])
                w = 96 if it["tb"] == "B" else P
                bo, rot = ("bo96", "rot96") if it["tb"] == "B" else ("bo64", "rot64")
                if has_norm(it):
                    mm(ps[r, 3 + c % 2, 0:n], tab(l, bo)[r, 0:w], zsq[r, c % 2, 0:n], start=True, stop=True)
                mm(ps[r, 5 + c % 2, 0:n], tab(l, rot)[r, 0:w], zw[r, c % 2, 0:n], start=True,
                   stop=True).then_inc(s_rx[l], 1)

            def projections(l):
                pe.wait_ge(s_nh, KC * (2 * l + 1))
                project(l, 0)
                for c in range(len(items[l])):
                    if c + 1 < len(items[l]):
                        project(l, c + 1)
                    reduce_rotate(l, c)

            def scores(l, a):
                it = att[l][a]
                if a >= 3:
                    pe.wait_ge(s_p[l], a - 2)
                n = it["nb"] * P
                last = mm(ps[:, a % 3, 0:n], it["q"], it["k"], start=True, stop=it["mask"] is None)
                if it["mask"]:
                    b, mk = it["mask"]
                    last = mm(ps[:, a % 3, b * P:b * P + P], ident, mk, start=False, stop=True)
                last.then_inc(s_s[l], 1)

            def transpose_probs(l, a):
                it, m = att[l][a], mix[l]
                pe.wait_ge(s_p[l], a + 1)
                pe.wait_ge(s_dg[l], a + 1)
                if a >= 2:
                    pe.wait_ge(s_pe[l], a - 1)
                for b in range(it["nb"]):
                    last = mm(ps[:, 3 + a % 2, b * P:b * P + P], m["pr"][:, a % 2, b * P:b * P + P],
                              m["dg"][:, a % 2, :], start=True, stop=True)
                last.then_inc(s_pt[l], 1)

            def values(l, a):
                it, m = att[l][a], mix[l]
                pe.wait_ge(s_pe[l], a + 1)
                if it["first"] and it["pair"] >= 2:
                    pe.wait_ge(s_oe[l], it["pair"] - 1)
                for b in range(it["nb"]):
                    last = mm(ps[it["rows"], 5 + it["pair"] % 2, it["col"]:it["col"] + P], it["v"][b],
                              m["pts"][:, a % 2, b * P:b * P + P], start=b == 0, stop=b == it["nb"] - 1)
                last.then_inc(s_pv[l], 1)

            def attention(l):
                n = len(att[l])
                pe.wait_ge(s_zw[l], len(items[l]))
                pe.wait_ge(s_it[l], rx_upto[l][-1])
                if l == 1:
                    pe.wait_ge(s_yr, 1)
                scores(l, 0)
                scores(l, 1)
                for a in range(n):
                    transpose_probs(l, a)
                    if a + 2 < n:
                        scores(l, a + 2)
                    if a >= 1:
                        values(l, a - 1)
                values(l, n - 1)

            def retention():
                pe.wait_ge(s_zw[1], len(items1))
                pe.wait_ge(s_it[1], rx_upto[1][-1])
                m = m1

                def rscores(h):
                    r = slice(64 * (h % 2), 64 * (h % 2) + 64)
                    for kt in range(4):
                        last = mm(ps[:, 2 * (h % 2) + kt // 2, (kt % 2) * X:(kt % 2) * X + X],
                                  m["kr"][r, h // 2, kt * P:kt * P + P], m["qr"][r, h // 2, :], start=True, stop=True)
                    last.then_inc(s_rs, 1)

                rscores(0)
                rscores(1)
                for h in range(4):
                    pe.wait_ge(s_rd, h + 1)
                    for kt in range(4):
                        last = mm(ps[:, 4 + h // 2, (h % 2) * X:(h % 2) * X + X], m["vr"][:, kt, h * P:h * P + P],
                                  m["sd"][:, h % 2, kt, :],
                                  start=kt == 0, stop=kt == 3)
                    last.then_inc(s_ro, 1)
                    if h + 2 < 4:
                        rscores(h + 2)
                pe.wait_ge(s_roe, 1)
                for b in range(2):
                    last = mm(ps[:, b, :], tab(1, "ones"), m["orr"][:, 2 * b:2 * b + 2, :].rearrange("p a b -> p (a b)"), start=True, stop=True)
                last.then_inc(s_mu, 1)
                pe.wait_ge(s_osq, 1)
                for b in range(2):
                    last = mm(ps[:, 2 + b, :], tab(1, "ones"), m["osq"][:, 2 * b:2 * b + 2, :].rearrange("p a b -> p (a b)"), start=True, stop=True)
                last.then_inc(s_mu, 1)

            def output(l):
                pe.wait_ge(s_oe[l], pairs[l])
                n = nq_cols[l]
                for m in range(KC):
                    w = landed(pe, ("wo", l, m)).rearrange("p (k m) -> p k m", k=KC)
                    if m >= 3:
                        pe.wait_ge(s_xt, xt_base[f"wo{l}"] + m - 2)
                    for k in range(KC):
                        last = mm(ps[:, m % 3, 0:n], w[:, k, :], mix[l]["oa"][:, k, :], start=k == 0, stop=k == KC - 1)
                    last.then_inc(s_wo, 1)

            def queries(l):
                n = tiles[l] * P
                pe.wait_ge(s_nh, KC * (2 * l + 2))
                for m in range(16):
                    w = landed(pe, ("wq", l, m)).rearrange("p (k m) -> p k m", k=KC)
                    if m >= 3:
                        pe.wait_ge(s_qe, 16 * l + m - 2)
                    for k in range(KC):
                        last = mm(ps[:, m % 3, 0:n], w[:, k, :], hk(k, 0, n), start=k == 0, stop=k == KC - 1)
                    last.then_inc(s_q, 1)
                pe.wait_ge(s_qe, 16 * l + 16)
                pe.wait_ge(s_key, 16 * (l + 1))

            def key_scores(l, t):
                for u in range(4):
                    q = (tile_base[l] + t) * 4 + u
                    if t * 4 + u >= 3:
                        pe.wait_ge(s_sce, q - 2)
                    for j in range(4):
                        hp = 4 * u + j
                        last = mm(ps[:, 3 + q % 3, j * P:j * P + P], tk["qt"][:, hp, t * P:t * P + P],
                                  keys[:, hp, :], start=True, stop=True)
                    last.then_inc(s_sc, 1)

            def select_transpose(l, t):
                n = tile_base[l] + t
                pe.wait_ge(s_tk, n + 1)
                if t >= 2:
                    pe.wait_ge(s_sel, n - 1)
                for j in range(3):
                    last = pe.transpose(ps[:, t % 2, j * P:j * P + P], tk["g"][:, t % 2, j, :], ident)
                last.then_inc(s_tt, 1)

            def selection(l):
                key_scores(l, 0)
                key_scores(l, 1)
                for t in range(tiles[l]):
                    if l == 0 and t < 2:
                        modulation(2 + t)
                    select_transpose(l, t)
                    if t + 2 < tiles[l]:
                        key_scores(l, t + 2)

            def gate_matrices(n):
                l, g = groups[n]
                pe.wait_ge(s_sel, tile_base[l] + tiles[l])
                if n == 1:
                    pe.wait_ge(s_xt, xt_base["peer0"] + KC)

                def steps(i, first):
                    for j in range(2):
                        pe.wait_ge(s_oh, i * 2 + (64 * n + j + 1))
                        if not first:
                            pe.wait_ge(s_ge, i * 2 + (64 * n + j - 1))
                        for t in range(4):
                            last = mm(ps[:, j, t * P:t * P + P], oha[:, j, t, :], ohb[:, j, t, :], start=True, stop=True)
                        last.then_inc(s_g, 1)

                steps(0, True)
                with pe.Fori(1, 32) as i:
                    steps(i, False)

            def experts(n):
                l, g = groups[n]
                cnt = expert_count[n]

                def up(i, j, first):
                    pe.wait_ge(s_slot[2 * j], i * 16 + 16 * (cnt[2 * j] + 1))
                    if not first:
                        pe.wait_ge(s_gel, i * 4 + (P * n + j - 1))
                    for k in range(KC):
                        last = mm(ps[:, 4 + j % 2, 0:GRP], ring[:, 2 * j, k * P:k * P + P], hk(k, g * GRP, g * GRP + GRP),
                                  start=k == 0, stop=k == KC - 1)
                    last.then_inc(s_a, 1)

                def down(i, j, start, stop):
                    pe.wait_ge(s_slot[2 * j + 1], i * 16 + 16 * (cnt[2 * j + 1] + 1))
                    pe.wait_ge(s_w, i * 4 + (P * n + j + 1))
                    for tt in range(GRP_TILES):
                        for half in range(2):
                            last = mm(ps[:, 2 * tt + half, :], wt[:, j % 2, tt * P:tt * P + P],
                                      ring[:, 2 * j + 1, half * 512:half * 512 + 512], start=start, stop=stop)
                    last.then_inc(s_y, 1)

                pe.wait_ge(s_ge, 64 * (n + 1))
                up(0, 0, True)
                up(0, 1, True)
                down(0, 0, True, False)
                up(0, 2, False)
                down(0, 1, False, False)
                up(0, 3, False)
                down(0, 2, False, False)
                with pe.Fori(1, 32) as i:
                    up(i, 0, False)
                    down(i - 1, 3, False, False)
                    for j in range(1, 4):
                        up(i, j, False)
                        down(i, j - 1, False, False)
                down(31, 3, False, True)
                pe.wait_ge(s_ye, 2 * n + 2)
                for m in range(KC):
                    if m >= 2:
                        pe.wait_ge(s_xt, group_xt(n) + m - 1)
                    for tt in range(GRP_TILES):
                        last = pe.transpose(ps[:, 4 + m % 2, tt * P:tt * P + P], ys[:, tt, m * P:m * P + P], ident)
                    last.then_inc(s_yt, 1)

            pe.wait_ge(s_par, 32)
            modulation(0)
            norm(0)
            projections(0)
            attention(0)
            modulation(1)
            output(0)
            norm(1)
            queries(0)
            selection(0)
            for n in range(2):
                gate_matrices(n)
                experts(n)
            norm(2)
            projections(1)
            retention()
            attention(1)
            output(1)
            norm(3)
            queries(1)
            selection(1)
            gate_matrices(2)
            experts(2)

        @block.scalar
        def _(act):
            own = Step(act, s_act)
            af = act.activation

            def norm(n):
                width = T if n < 3 else X
                m, l, w = mix[n // 2], n // 2, n % 2
                for k in range(KC):
                    if n == 0:
                        act.wait_ge(s_x, 16)
                    else:
                        act.wait_ge(s_xt, {1: 0, 2: xt_base["peer0"] + KC, 3: xt_base["wo1"]}[n] + k + 1)
                    if KC * n + k >= 2:
                        act.wait_ge(s_nss, KC * n + k - 1)
                    af(m["sq8"][:, k % 2, 0:width], xt[:, k, 0:width], ACT.Square).then_inc(s_nsq, 1)
                act.wait_ge(s_nss, KC * n + KC)
                af(m["nrt"][:, 0:width], ps[:, 6, 0:width], ACT.Sqrt, bias=pcol("eps"), scale=1.0 / D).then_inc(s_nrt, 1)
                for k in range(KC):
                    act.wait_ge(s_nt, KC * n + k + 1)
                    for st in range(width // X):
                        last = af(ht[:, k, st * X:st * X + X], m["nt"][:, k % 2, st * X:st * X + X], ACT.Identity,
                                  bias=mod[:, l, 24 * w + k, st:st + 1])
                    last.then_inc(s_nh, 1)

            def projections(l):
                m = mix[l]

                def read(c):
                    it = items[l][c]
                    kind, r, n = it["kind"], it["rows"], it["n"]
                    z = ps[r, c % 3, 0:n]
                    act.wait_ge(s_z[l], c + 1)
                    if kind == "plain":
                        af(it["dest"], z, ACT.Copy).then_inc(s_zw[l], 1)
                        return
                    if kind == "silu":
                        af(it["dest"], z, ACT.Silu).then_inc(s_zw[l], 1)
                        return
                    if c >= 2:
                        b = c - 2
                        if kind != "kr" and items[l][b]["kind"] == "lora0":
                            b = c - 1
                        if rx_upto[l][b]:
                            act.wait_ge(s_rx[l], rx_upto[l][b])
                        if rx_upto[l][c - 2]:
                            act.wait_ge(s_it[l], rx_upto[l][c - 2])
                    if kind == "kr":
                        for b in range(2):
                            own.inc(af(m["zk"][r, b, :], z, ACT.Copy, scale=it["w"]))
                            last = af(m["zks"][r, b, :], z, ACT.Square)
                        last.then_inc(s_zw[l], 1)
                        return
                    if kind == "ropek":
                        r = slice(0, 64)
                        z = ps[r, c % 3, 0:n]
                        af(m["zk"][r, c % 2, 0:n], z, ACT.Copy, scale=it["w"])
                        af(m["zks"][r, c % 2, 0:n], z, ACT.Square).then_inc(s_zw[l], 1)
                        return
                    zw = m["zw"][r, c % 2, 0:n] if kind in ("rope", "rope0") else it["dest"][:, int(kind == "lora1"), :]
                    if kind == "rope0":
                        af(zw, z, ACT.Copy, scale=1.0).then_inc(s_zw[l], 1)
                        return
                    af(zw, z, ACT.Copy, scale=it["w"])
                    af(m["zsq"][r, c % 2, 0:n], z, ACT.Square).then_inc(s_zw[l], 1)

                def root(c):
                    it = items[l][c]
                    if not has_norm(it):
                        return
                    r, n = it["rows"], it["n"]
                    act.wait_ge(s_rx[l], rx_upto[l][c])
                    if c >= 2 and rx_upto[l][c - 2]:
                        act.wait_ge(s_it[l], rx_upto[l][c - 2])
                    dim = {"lora1": 256, "rope": 64, "ropek": 96}[it["kind"]]
                    if it["kind"] == "rope" and it["tb"] == "B":
                        dim = 96
                    af(m["rt"][r, c % 2, 0:n], ps[r, 3 + c % 2, 0:n], ACT.Sqrt, bias=pcol("eps", rows=r),
                       scale=1.0 / dim).then_inc(s_rt[l], 1)

                for c in range(len(items[l])):
                    read(c)
                    if c >= 1:
                        root(c - 1)
                root(len(items[l]) - 1)

            def attention(l):
                m = mix[l]

                def exps(a):
                    it = att[l][a]
                    n = it["nb"] * P
                    act.wait_ge(s_nm[l], a + 1)
                    if a >= 2:
                        act.wait_ge(s_pt[l], a - 1)
                    nm = m["st"][:, 0, a % 64:a % 64 + 1]
                    last = af(m["pr"][:, a % 2, 0:n], ps[:, a % 3, 0:n], ACT.Exp, bias=nm, scale=it["sc"],
                              accum_out=m["st"][:, 1, a % 64:a % 64 + 1])
                    if it["sink"] is not None:
                        last = af(m["st"][:, 2, a % 64:a % 64 + 1], it["sink"], ACT.Exp, bias=nm)
                    last.then_inc(s_p[l], 1)

                def evacuate(a):
                    n = att[l][a]["nb"] * P
                    act.wait_ge(s_pt[l], a + 1)
                    if a >= 2:
                        act.wait_ge(s_pv[l], a - 1)
                    af(m["pts"][:, a % 2, 0:n], ps[:, 3 + a % 2, 0:n], ACT.Copy).then_inc(s_pe[l], 1)

                for a in range(len(att[l])):
                    exps(a)
                    if a >= 1:
                        evacuate(a - 1)
                evacuate(len(att[l]) - 1)

            def decays():
                m = m1
                act.wait_ge(s_tab[1], 16)
                own.do(af(m["lg"][:, 0:8], pcol("decf", 0, 8), ACT.Exp, scale=-1.0))
                own.do(af(m["lg"][:, 8:16], m["lg"][:, 0:8], ACT.Ln, bias=pcol("one")))
                own.do(af(m["lg"][:, 0:8], m["lg"][:, 8:16], ACT.Copy, scale=-1.0))
                for h in range(4):
                    if h >= 1:
                        act.wait_ge(s_dt, h)
                    af(m["de"][:, 0, :], tab(1, "df"), ACT.Exp, scale=m["lg"][:, h:h + 1])
                    af(m["de"][:, 1, :], tab(1, "db"), ACT.Exp, scale=m["lg"][:, 4 + h:5 + h]).then_inc(s_ex, 1)

            def retention():
                m = m1
                act.wait_ge(s_ro, 4)
                af(m["orr"].rearrange("p h t -> p (h t)"), ps[:, 4:6, :].rearrange("p a b -> p (a b)"),
                   ACT.Copy).then_inc(s_roe, 1)
                act.wait_ge(s_oc, 1)
                af(m["osq"].rearrange("p h t -> p (h t)"), m["orr"].rearrange("p h t -> p (h t)"),
                   ACT.Square).then_inc(s_osq, 1)
                act.wait_ge(s_mu, 2)
                af(m["ort"], ps[:, 2:4, :].rearrange("p a b -> p (a b)"), ACT.Sqrt, bias=pcol("eps"),
                   scale=1.0 / P).then_inc(s_osq, 1)

            def peer(l):
                n = tiles[l] * P
                for m in range(16):
                    act.wait_ge(s_q, 16 * l + m + 1)
                    af(tk["qt"][:, m, 0:n], ps[:, m % 3, 0:n], ACT.Copy).then_inc(s_qe, 1)

                def score_copy(t):
                    for u in range(4):
                        q = (tile_base[l] + t) * 4 + u
                        act.wait_ge(s_sc, q + 1)
                        af(sc_view(t % 2)[:, 4 * u:4 * u + 4, :].rearrange("p a b -> p (a b)"),
                           ps[:, 3 + q % 3, :], ACT.Copy).then_inc(s_sce, 1)

                score_copy(0)
                score_copy(1)
                for t in range(tiles[l]):
                    k = tile_base[l] + t
                    act.wait_ge(s_best, k + 1)
                    af(tk["bv"].rearrange("p h k -> p (h k)"), tk["bv"].rearrange("p h k -> p (h k)"),
                       ACT.Exp).then_inc(s_bexp, 1)
                    act.wait_ge(s_tt, k + 1)
                    af(sel[:, :, t * P:t * P + P], ps[:, t % 2, 0:2 * P].rearrange("p (a b) -> p a b", a=2), ACT.Copy)
                    af(sel2[:, t * P:t * P + P], ps[:, t % 2, 2 * P:3 * P], ACT.Copy).then_inc(s_sel, 1)
                    if t + 2 < tiles[l]:
                        score_copy(t + 2)

            def gate_matrices(n):
                if n == 0 or n == 2:
                    l = groups[n][0]
                    act.wait_ge(s_tk, tile_base[l] + tiles[l])
                else:
                    act.wait_ge(s_yt, KC * n)

                def steps(i):
                    for j in range(2):
                        act.wait_ge(s_g, i * 2 + (64 * n + j + 1))
                        af(gates[:, :, bass.ds(i * 8 + 4 * j, 4)] if not isinstance(i, int) else
                           gates[:, :, i * 8 + 4 * j:i * 8 + 4 * j + 4],
                           ps[:, j, :].rearrange("p (t i) -> p i t", t=4), ACT.Copy).then_inc(s_ge, 1)

                with act.Fori(0, 32) as i:
                    steps(i)

            def experts(n):
                act.wait_ge(s_g, 64 * (n + 1))

                def gelu(i, j, first):
                    act.wait_ge(s_a, i * 4 + (P * n + j + 1))
                    if not first:
                        act.wait_ge(s_w, i * 4 + (P * n + j - 1))
                    af(gel[:, j % 2, :], ps[:, 4 + j % 2, 0:GRP], ACT.Gelu_apprx_tanh).then_inc(s_gel, 1)

                for j in range(4):
                    gelu(0, j, j < 2)
                with act.Fori(1, 32) as i:
                    for j in range(4):
                        gelu(i, j, False)
                act.wait_ge(s_y, P * (n + 1))
                for tt in range(GRP_TILES):
                    af(ys[:, tt, :], ps[:, 2 * tt:2 * tt + 2, :].rearrange("p a b -> p (a b)"), ACT.Copy).then_inc(s_ye, 1)

            act.wait_ge(s_par, 32)
            af(cs[:, :, :], pcol("c", 0, 16).rearrange("p (k s) -> p k s", s=2), ACT.Silu).then_inc(s_cs, 1)
            norm(0)
            projections(0)
            attention(0)
            norm(1)
            peer(0)
            for n in range(2):
                gate_matrices(n)
                experts(n)
            norm(2)
            decays()
            projections(1)
            retention()
            attention(1)
            norm(3)
            peer(1)
            gate_matrices(2)
            experts(2)

        @block.vector
        def _(dve):
            own = Step(dve, s_dve)
            tt, ts, stt = dve.tensor_tensor, dve.tensor_scalar, dve.scalar_tensor_tensor

            def modulation(g):
                l, a, b = adas[g]
                dve.wait_ge(s_ada, ada_done[g] + b - a)
                n = b - a
                tt(mod[:, l, a:b, :], ps[:, 7, 2 * a:2 * b].rearrange("p (m s) -> p m s", s=2),
                   pcol("ada_b", 48 * l + a, n).unsqueeze(2).broadcast_to([P, n, 2]), ALU.add).then_inc(s_mod, 1)
                dve.wait_ge(s_mod, 2 * g + 1)
                which = [w for w, at in ((0, 8), (1, 32)) if a <= at < b]
                for w in which:
                    at = 8 + 24 * w
                    last = stt(out=gain[:, 2 * l + w, :, :], in0=mod[:, l, at:at + KC, :], scalar=1.0,
                               in1=pcol("n2" if w else "n1", KC * l, KC).unsqueeze(2).broadcast_to([P, KC, 2]),
                               op0=ALU.add, op1=ALU.mult)
                    if w != which[-1]:
                        own.inc(last)
                if which:
                    last.then_inc(s_mod, 1)
                else:
                    dve.sem_inc(s_mod, 1)

            def norm(n):
                width = T if n < 3 else X
                m = mix[n // 2]
                dve.wait_ge(s_nrt, n + 1)
                own.do(dve.reciprocal(m["nrb"][:, 0:width], m["nrt"][:, 0:width]))
                for k in range(KC):
                    if k >= 2:
                        dve.wait_ge(s_nh, KC * n + k - 1)
                    for st in range(width // X):
                        c = slice(st * X, st * X + X)
                        last = stt(out=m["nt"][:, k % 2, c], in0=xt[:, k, c], scalar=gain[:, n, k, st:st + 1],
                                   in1=m["nrb"][:, c], op0=ALU.mult, op1=ALU.mult)
                    last.then_inc(s_nt, 1)

            def projections(l):
                m = mix[l]
                for c, it in enumerate(items[l]):
                    if not has_rx(it):
                        continue
                    r, n = it["rows"], it["n"]
                    if it["kind"] == "lora1":
                        dve.wait_ge(s_rt[l], rt_upto[l][c])
                        own.do(dve.reciprocal(m["ri"], m["rt"][:, c % 2, :]))
                        own.inc(tt(it["dest"][:, 0, :], it["dest"][:, 0, :], m["ri"], ALU.mult))
                        tt(it["dest"][:, 1, :], it["dest"][:, 1, :], m["ri"], ALU.mult).then_inc(s_it[l], 1)
                        continue
                    zw = m["zk"] if it["kind"] == "ropek" else m["zw"]
                    dve.wait_ge(s_rx[l], rx_upto[l][c])
                    own.inc(tt(m["ta"][r, 0:n], zw[r, c % 2, 0:n], tab(l, "cos" + it["tb"])[r, 0:n], ALU.mult))
                    own.do(tt(m["tb"][r, 0:n], ps[r, 5 + c % 2, 0:n], tab(l, "sin" + it["tb"])[r, 0:n], ALU.mult))
                    if not has_norm(it):
                        tt(it["dest"], m["ta"][r, 0:n], m["tb"][r, 0:n], ALU.add).then_inc(s_it[l], 1)
                        dve.wait_ge(s_it[l], rx_upto[l][c])
                        continue
                    own.inc(tt(m["ta"][r, 0:n], m["ta"][r, 0:n], m["tb"][r, 0:n], ALU.add))
                    dve.wait_ge(s_rt[l], rt_upto[l][c])
                    own.do(dve.reciprocal(m["ri"][r, 0:n], m["rt"][r, c % 2, 0:n]))
                    tt(it["dest"], m["ta"][r, 0:n], m["ri"][r, 0:n], ALU.mult).then_inc(s_it[l], 1)
                    dve.wait_ge(s_it[l], rx_upto[l][c])

            def attention(l):
                m = mix[l]
                st = m["st"]

                def finish(a):
                    it = att[l][a]
                    c = slice(a % 64, a % 64 + 1)
                    dve.wait_ge(s_p[l], a + 1)
                    den = st[:, 1, c]
                    if it["sink"] is not None:
                        own.do(tt(st[:, 3, c], st[:, 1, c], st[:, 2, c], ALU.add))
                        den = st[:, 3, c]
                    own.do(dve.reciprocal(st[:, 4, c], den))
                    if a >= 2:
                        dve.wait_ge(s_pt[l], a - 1)
                    ts(m["dg"][:, a % 2, :], ident, st[:, 4, c], None, ALU.mult).then_inc(s_dg[l], 1)

                def gather(pair):
                    n = 2 * (4 if l == 0 else 2)
                    dve.wait_ge(s_pv[l], n * (pair + 1))
                    it = att[l][n * pair]
                    dve.tensor_copy(it["dest"], ps[:, 5 + pair % 2, 0:nq_cols[l]]).then_inc(s_oe[l], 1)

                n = 2 * (4 if l == 0 else 2)
                for a, it in enumerate(att[l]):
                    w = it["nb"] * P
                    dve.wait_ge(s_s[l], a + 1)
                    if a >= 64:
                        dve.wait_ge(s_p[l], a - 63)
                    mx = m["st"][:, 3, a % 64:a % 64 + 1]
                    own.do(dve.tensor_reduce(mx, ps[:, a % 3, 0:w], AXX, ALU.max))
                    nm = m["st"][:, 0, a % 64:a % 64 + 1]
                    if it["sink"] is not None:
                        own.do(ts(nm, mx, it["sc"], it["sink"], ALU.mult, ALU.max))
                        ts(nm, nm, -1.0, None, ALU.mult).then_inc(s_nm[l], 1)
                    else:
                        ts(nm, mx, -it["sc"], None, ALU.mult).then_inc(s_nm[l], 1)
                    if a >= 1:
                        finish(a - 1)
                    if a >= n + 2 and (a - 2) % n == 0:
                        gather((a - 2) // n - 1)
                finish(len(att[l]) - 1)
                gather(pairs[l] - 1)

            def output(l):
                for m in range(KC):
                    dve.wait_ge(s_wo, wo_base[l] + m + 1)
                    for st in range(nq_cols[l] // X):
                        c = slice(st * X, st * X + X)
                        last = stt(out=xt[:, m, c], in0=ps[:, m % 3, c], scalar=mod[:, l, 16 + m, st:st + 1],
                                   in1=xt[:, m, c], op0=ALU.mult, op1=ALU.add)
                    last.then_inc(s_xt, 1)

            def decays():
                m = m1
                for h in range(4):
                    dve.wait_ge(s_ex, h + 1)
                    for b, name in enumerate(("mf", "mb")):
                        last = tt(m["de"][:, b, 0:512], m["de"][:, b, 0:512], tab(1, name), ALU.mult)
                        own.inc(last)
                    own.wait()
                    own.do(tt(m["dt"][:, h, :, :].rearrange("p a b -> p (a b)"), m["de"][:, 0, :], m["de"][:, 1, :], ALU.add))
                    dth = m["dt"][:, h, :, :].rearrange("p a b -> p (a b)")
                    ts(dth, dth, HD ** -0.5, None, ALU.mult).then_inc(s_dt, 1)

            def retention():
                m = m1
                dve.wait_ge(s_dt, 4)
                for h in range(4):
                    dve.wait_ge(s_rs, h + 1)
                    if h >= 2:
                        dve.wait_ge(s_ro, h - 1)
                    b = 2 * (h % 2)
                    tt(m["sd"][:, h % 2, :, :].rearrange("p a b -> p (a b)"),
                       ps[:, b:b + 2, :].rearrange("p a b -> p (a b)"),
                       m["dt"][:, h, :, :].rearrange("p a b -> p (a b)"), ALU.mult).then_inc(s_rd, 1)
                orr = m["orr"].rearrange("p h t -> p (h t)")
                dve.wait_ge(s_mu, 1)
                stt(out=orr, in0=ps[:, 0:2, :].rearrange("p a b -> p (a b)"), scalar=-1.0 / P, in1=orr,
                    op0=ALU.mult, op1=ALU.add).then_inc(s_oc, 1)
                dve.wait_ge(s_osq, 2)
                own.do(dve.reciprocal(m["ort"], m["ort"]))
                own.do(tt(orr, orr, m["ort"], ALU.mult))
                for h in range(4):
                    last = stt(out=m["oa"][:, h, :], in0=m["orr"][:, h, :], scalar=pcol("gn", h),
                               in1=m["sg"][:, h, :], op0=ALU.mult, op1=ALU.mult)
                    if h < 3:
                        own.inc(last)
                last.then_inc(s_yr, 1)

            def topk(l):
                v, f, bv, cd, eq, g3 = tk["v"], tk["if"], tk["bv"], tk["cd"], tk["eq"], tk["g"]
                for t in range(tiles[l]):
                    n = tile_base[l] + t
                    sc = sc_view(t % 2)
                    dve.wait_ge(s_sce, 4 * (n + 1))
                    for half in range(2):
                        s8 = slice(8 * half, 8 * half + 8)
                        for hp in range(16):
                            own.inc(dve.max(v[:, hp, s8], sc[:, hp, :]))
                        own.wait()
                        for hp in range(16):
                            own.inc(dve.max_index(iu[:, hp, s8], v[:, hp, s8], sc[:, hp, :]))
                        own.wait()
                        if half == 0:
                            for hp in range(16):
                                own.inc(dve.match_replace(sc[:, hp, :], v[:, hp, s8], sc[:, hp, :], LOWEST))
                            own.wait()
                    own.inc(dve.tensor_copy(f, iu))
                    vv = v.rearrange("p (h two) a -> p h two a", two=2)
                    own.do(tt(cd.rearrange("p h (a b) -> p h a b", a=16),
                              vv[:, :, 0, :].unsqueeze(3).broadcast_to([P, HEADS, 16, 16]),
                              vv[:, :, 1, :].unsqueeze(2).broadcast_to([P, HEADS, 16, 16]), ALU.add))
                    pi = piu[:, 0, :].rearrange("p (h k) -> p h k", h=HEADS)
                    for half in range(2):
                        s8 = slice(8 * half, 8 * half + 8)
                        for h in range(HEADS):
                            own.inc(dve.max(bv[:, h, s8], cd[:, h, :]))
                        own.wait()
                        for h in range(HEADS):
                            own.inc(dve.max_index(pi[:, h, s8], bv[:, h, s8], cd[:, h, :]))
                        own.wait()
                        if half == 0:
                            for h in range(HEADS):
                                own.inc(dve.match_replace(cd[:, h, :], bv[:, h, s8], cd[:, h, :], LOWEST))
                            own.wait()
                    mx = tk["sm"][:, 0, :]
                    own.do(dve.tensor_copy(mx, bv[:, :, 0]))
                    tt(bv, bv, mx.unsqueeze(2).broadcast_to([P, HEADS, 16]), ALU.subtract).then_inc(s_best, 1)
                    own.inc(ts(piu[:, 1, :], piu[:, 0, :], 4, None, ALU.logical_shift_right))
                    own.do(ts(piu[:, 2, :], piu[:, 0, :], 15, None, ALU.bitwise_and))
                    own.do(dve.tensor_copy(tk["pf"], piu[:, 1:3, :]))
                    if t >= 2:
                        dve.wait_ge(s_tt, n - 1)
                    ff = f.rearrange("p (h two) a -> p h two a", two=2)
                    for half in range(2):
                        own.do(tt(eq, tk["pf"][:, half, :].unsqueeze(2).broadcast_to([P, P, 16]),
                                  iota[:, 0:16].unsqueeze(1).broadcast_to([P, P, 16]), ALU.is_equal))
                        e4 = eq.rearrange("p (h k) a -> p h k a", h=HEADS)
                        own.do(tt(e4, e4, ff[:, :, half, :].unsqueeze(2).broadcast_to([P, HEADS, 16, 16]), ALU.mult))
                        own.do(dve.tensor_reduce(g3[:, t % 2, 1 + half, :], eq, AXX, ALU.add))
                    dve.wait_ge(s_bexp, n + 1)
                    own.do(dve.tensor_reduce(mx, bv, AXX, ALU.add))
                    own.do(dve.reciprocal(tk["sm"][:, 1, :], mx))
                    tt(g3[:, t % 2, 0, :].rearrange("p (h k) -> p h k", h=HEADS), bv,
                       tk["sm"][:, 1, :].unsqueeze(2).broadcast_to([P, HEADS, 16]), ALU.mult).then_inc(s_tk, 1)
                    dve.wait_ge(s_tk, n + 1)
                    if l == 0 and t < 2:
                        modulation(2 + t)

            def one_hots(n):
                l, g = groups[n]
                dve.wait_ge(s_sel, tile_base[l] + tiles[l])
                if n >= 1:
                    dve.wait_ge(s_y, P * n)

                def steps(i, first):
                    for j in range(2):
                        if not first:
                            dve.wait_ge(s_g, i * 2 + (64 * n + j - 1))
                        for t in range(4):
                            at = i * 8 + (g * GRP + 4 * j + t)
                            col = slice(at, at + 1) if isinstance(at, int) else bass.ds(at, 1)
                            ts(oha[:, j, t, :], iota, sel[:, 1, col], sel[:, 0, col], ALU.is_equal, ALU.mult)
                            last = ts(ohb[:, j, t, :], iota, sel2[:, col], None, ALU.is_equal)
                        last.then_inc(s_oh, 1)

                steps(0, True)
                with dve.Fori(1, 32) as i:
                    steps(i, False)

            def experts(n):
                dve.wait_ge(s_g, 64 * (n + 1))
                dve.wait_ge(s_ge, 64 * (n + 1))

                def weigh(i, j, first):
                    dve.wait_ge(s_gel, i * 4 + (P * n + j + 1))
                    if not first:
                        dve.wait_ge(s_y, i * 4 + (P * n + j - 1))
                    at = i * 4 + j
                    g = gates[:, at, :] if isinstance(at, int) else gates[:, bass.ds(at, 1), :].rearrange("p a t -> p (a t)")
                    tt(wt[:, j % 2, :], gel[:, j % 2, :], g, ALU.mult).then_inc(s_w, 1)

                for j in range(4):
                    weigh(0, j, j < 2)
                with dve.Fori(1, 32) as i:
                    for j in range(4):
                        weigh(i, j, False)
                l, g = groups[n]
                c = slice(g * GRP, g * GRP + GRP)
                for m in range(KC):
                    dve.wait_ge(s_yt, KC * n + m + 1)
                    stt(out=xt[:, m, c], in0=ps[:, 4 + m % 2, 0:GRP], scalar=mod[:, l, 40 + m, g:g + 1],
                        in1=xt[:, m, c], op0=ALU.mult, op1=ALU.add).then_inc(s_xt, 1)

            dve.wait_ge(s_par, 32)
            modulation(0)
            norm(0)
            projections(0)
            attention(0)
            modulation(1)
            output(0)
            norm(1)
            topk(0)
            for n in range(2):
                one_hots(n)
                experts(n)
            norm(2)
            decays()
            projections(1)
            retention()
            attention(1)
            output(1)
            norm(3)
            topk(1)
            one_hots(2)
            experts(2)


def _chunks(w, cols):
    w = w[:, cols]
    k = w.shape[0] // P
    return np.ascontiguousarray(w.reshape(k, P, -1, P).transpose(2, 1, 0, 3))


def _rope_tables(head, start, half, rows):
    cos = np.ones((rows, T), np.float32)
    sin = np.zeros((rows, T), np.float32)
    rot = np.zeros((P, P), np.float32)
    t = np.arange(X)
    posn = [t // GRID_W, t % GRID_W]
    fr = (np.float32(10000.0) ** (-np.arange(half, dtype=np.float32) / np.float32(half))).astype(np.float32)
    for r in range(rows):
        f = r % head - start
        if f < 0:
            continue
        ang = posn[f // (2 * half)].astype(np.float32) * fr[f % half]
        low = f % (2 * half) < half
        cos[r, :X] = np.cos(ang)
        sin[r, :X] = -np.sin(ang) if low else np.sin(ang)
        rot[r + half if low else r - half, r] = 1.0
    return cos, sin, rot


def _tables():
    ca, sa, ra = _rope_tables(64, 0, 16, P)
    cb, sb_, rb = _rope_tables(P, 64, 8, 96)
    pad = ((0, 32), (0, 0))
    cb, sb_ = np.pad(cb, pad), np.pad(sb_, pad)
    i = np.arange(P)
    bo64 = (i[:, None] // 64 == i[None] // 64).astype(np.float32)
    ones = np.ones((P, P), np.float32)
    m01 = np.where(i[None] <= i[:, None], 0.0, NEG).astype(np.float32)
    m10 = np.where(i[None] >= i[:, None], 0.0, NEG).astype(np.float32)
    tab0 = dict(cosA=ca, sinA=sa, bo64=bo64, rot64=ra, ones=ones, cosB=cb, sinB=sb_, bo96=ones, rot96=rb,
                m01=m01, m10=m10)
    q = np.arange(X)[None]
    df, db = np.zeros((P, 4, X), np.float32), np.zeros((P, 4, X), np.float32)
    mf, mb = np.zeros((P, 2, X), np.float32), np.zeros((P, 2, X), np.float32)
    for kt in range(4):
        j = (kt % 2) * P + i[:, None]
        if kt < 2:
            df[:, kt] = db[:, kt] = np.abs(q - j)
            mf[:, kt], mb[:, kt] = j <= q, j >= q
        else:
            df[:, kt], db[:, kt] = X + q - j, X - q + j
    tab1 = dict(cosA=ca, sinA=sa, bo64=bo64, rot64=ra, ones=ones, df=df, db=db, mf=mf, mb=mb)
    return [np.concatenate([d[n].reshape(P, -1) for n in TAB[l]], axis=1) for l, d in enumerate((tab0, tab1))]


def kernel(x, c, ctx, c_ctx, ada_w, ada_b, norm1_w, norm2_w, ab_w_in, ab_w_o, a_q_norm, a_k_norm,
           a_sink, b_q_lora_norm, b_kv_lora_norm, b_w_uq, b_w_ukv, b_q_norm, b_k_norm, cd_w_in, cd_w_o,
           c_decay_fwd, c_decay_bwd, c_gn_w, d_q_norm, d_k_norm, peer_w_q, peer_keys, peer_u, peer_v):
    import concourse.bacc as _bacc
    from concourse.bass_utils import run_bass_kernel_spmd as _run

    f = np.asarray
    a = {}
    tokens = np.concatenate([f(x)[0], f(ctx)[0]], axis=0)
    a["x"] = tokens.reshape(T, KC, P).transpose(2, 1, 0)
    a["ada"] = f(ada_w).reshape(2, KC, P, MODS, P).transpose(0, 3, 2, 1, 4)
    r = np.arange
    pairs = np.concatenate([np.concatenate([r(j * 64, j * 64 + 64), r((j + 4) * 64, (j + 4) * 64 + 64)])
                            for j in range(4)])
    w = f(ab_w_in)[0]
    a["w0"] = _chunks(w, np.concatenate([pairs, r(512, 640), r(768, 1280), r(640, 768)]))
    a["kr"] = w[:, 1280:1312].reshape(1, KC, P, 32).transpose(0, 2, 1, 3)
    a["uq"] = f(b_w_uq)[0].reshape(2, P, 2, 384).transpose(2, 1, 0, 3)
    kv = f(b_w_ukv)[0].reshape(2, P, 8, 2, 64)
    a["ukvk"] = kv[:, :, :, 0].reshape(1, 2, P, 512).transpose(0, 2, 1, 3)
    a["ukvv"] = kv[:, :, :, 1].reshape(1, 2, P, 512).transpose(0, 2, 1, 3)
    w1 = f(cd_w_in)[0]
    a["w1"] = _chunks(w1, np.concatenate([r(0, 512), 1536 + pairs, r(2048, 2176), r(2176, 2304), r(1024, 1536)]))
    a["vr"] = w1[:, 512:1024].reshape(4, 2, P, 512).transpose(0, 2, 1, 3)
    every = r(D)
    a["wo"] = np.stack([_chunks(f(ab_w_o)[0][np.concatenate([pairs, 512 + r(512)])], every),
                        _chunks(f(cd_w_o)[0][np.concatenate([r(512), 512 + pairs])], every)])
    a["wq"] = f(peer_w_q).reshape(2, KC, P, 16, P).transpose(0, 3, 2, 1, 4)
    a["keys"] = f(peer_keys).reshape(2, 16, P, P).transpose(0, 3, 1, 2)
    a["ut"] = f(peer_u).reshape(2, P, P, KC, P).transpose(0, 2, 4, 3, 1)
    a["vt"] = f(peer_v).reshape(2, P, P, D).transpose(0, 2, 1, 3)
    tab0, tab1 = _tables()
    a["tab0"], a["tab1"] = tab0, tab1
    a["cst"] = np.stack([np.eye(P, dtype=np.float32),
                         np.tile(np.arange(P, dtype=np.float32), (P, 1))], axis=1)

    def cols(v):
        return f(v).reshape(-1, P).T

    def head(v):
        v = f(v).reshape(-1)
        return np.concatenate([v, v])[:, None] if v.size == 64 else np.pad(v, (0, P - v.size))[:, None]

    def wide(v):
        return np.tile(f(v).reshape(1, -1), (P, 1))

    cc = np.stack([cols(c), cols(c_ctx)], axis=2).reshape(P, 16)
    a["par"] = np.concatenate([
        cols(norm1_w), cols(norm2_w), cols(ada_b), head(a_q_norm), head(a_k_norm), cols(b_q_lora_norm),
        cols(b_kv_lora_norm), head(b_q_norm), head(b_k_norm), cols(c_gn_w), head(d_q_norm), head(d_k_norm),
        cc, wide(a_sink), wide(c_decay_fwd), wide(c_decay_bwd),
        np.full((P, 1), EPS, np.float32), np.ones((P, 1), np.float32)], axis=1)
    assert a["par"].shape[1] == NPR

    nc = _bacc.Bacc("TRN2", target_bir_lowering=False, num_devices=1)
    arrays, aps = {}, {}
    for name, v in a.items():
        v = np.ascontiguousarray(v)
        arrays["in_" + name] = v
        aps[name] = nc.dram_tensor("in_" + name, v.shape, F32, kind="ExternalInput").ap()
    out = nc.dram_tensor("out", (P, KC, X), F32, kind="ExternalOutput").ap()
    build(nc, aps, out)
    got = _run(nc, [arrays], core_ids=[0]).results[0]["out"]
    return np.ascontiguousarray(got.transpose(2, 1, 0).reshape(1, X, D))
```

```python
from contextlib import ExitStack

import numpy as np
import concourse.bass as bass
from concourse import mybir

F32 = mybir.dt.float32
F32R = mybir.dt.float32r
U32 = mybir.dt.uint32
ACT = mybir.ActivationFunctionType
ALU = mybir.AluOpType
AXX = mybir.AxisListType.X

P = 128
D = 1024
KC = D // P
X = 256
T = 512
GRID_W = 64
HD = 64
EPS = 1e-6
NEG = -1e30
LOWEST = -3.0e38
HEADS = 8
NSEL = 128
SLOTS = 4
GRP = 256
GRP_TILES = GRP // P
MODS = 6 * KC
BLOCKS = MODS // 4

PR = {}
_at = 0
for _name, _n in (("n1", 16), ("n2", 16), ("ada_b", 96), ("aq", 1), ("ak", 1), ("bql", 2), ("bkvl", 2),
                  ("bq", 1), ("bk", 1), ("gn", 4), ("dq", 1), ("dk", 1), ("c", 16), ("sink", 8),
                  ("decf", 4), ("decb", 4), ("eps", 1), ("one", 1)):
    PR[_name] = _at
    _at += _n
NPR = _at

TAB = [{}, {}]
TABW = [0, 0]
for _l, _spec in enumerate(((("cosA", 512), ("sinA", 512), ("bo64", 128), ("rot64", 128), ("ones", 128),
                             ("cosB", 512), ("sinB", 512), ("bo96", 128), ("rot96", 128),
                             ("m01", 128), ("m10", 128)),
                            (("cosA", 512), ("sinA", 512), ("bo64", 128), ("rot64", 128), ("ones", 128),
                             ("df", 1024), ("db", 1024), ("mf", 512), ("mb", 512)))):
    for _name, _n in _spec:
        TAB[_l][_name] = (TABW[_l], _n)
        TABW[_l] += _n


class Step:

    def __init__(self, eng, sem):
        self.eng, self.sem, self.n = eng, sem, 0

    def inc(self, ins):
        ins.then_inc(self.sem, 1)
        self.n = self.n + 1

    def wait(self):
        self.eng.wait_ge(self.sem, self.n)

    def do(self, ins):
        self.inc(ins)
        self.wait()


def build(nc, A, out):
    with ExitStack() as ctx:
        def sb(name, shape, dt=F32):
            return ctx.enter_context(nc.sbuf_tensor(name, shape, dt))

        def sem(name):
            return ctx.enter_context(nc.semaphore(name))

        sel = sb("sel", [P, 2, T])
        sel2 = sb("sel2", [P, T], mybir.dt.bfloat16)
        scr = sb("scr", [P, 2048])
        cst = sb("cst", [P, 2, P])
        par = sb("par", [P, NPR])
        cs = sb("cs", [P, KC, 2])
        mod = sb("mod", [P, 2, MODS, 2])
        gain = sb("gain", [P, 4, KC, 2])
        nsink = sb("nsink", [P, HEADS])
        hh = sb("hh", [P, KC, GRP], F32R)
        hl = sb("hl", [P, KC, GRP], F32R)
        uh = sb("uh", [P, D], F32R)
        ul = sb("ul", [P, D], F32R)
        vh = sb("vh", [P, D], F32R)
        vl = sb("vl", [P, D], F32R)
        wh = sb("wh", [P, 2, GRP], F32R)
        wl = sb("wl", [P, 2, GRP], F32R)
        ident, iota = cst[:, 0, :], cst[:, 1, :]
        oha = scr[:, 0:1024].rearrange("p (b t n) -> p b t n", b=2, t=4)
        ohb = scr[:, 1024:2048].rearrange("p (b t n) -> p b t n", b=2, t=4)
        gel = scr[:, 0:512].rearrange("p (b t) -> p b t", b=2)
        rows = scr[0:2, 0:1024].rearrange("p (b n) -> p b n", b=2)
        HT0, G0 = SLOTS * D, SLOTS * D + KC * X
        XT0 = HT0 + KC * T
        AR0 = XT0 + KC * T
        ROOM = 39424
        room = sb("room", [P, ROOM])
        ring = room[:, 0:HT0].rearrange("p (s n) -> p s n", s=SLOTS)
        ht = room[:, HT0:XT0].rearrange("p (s k t) -> p s k t", s=2, k=KC)
        xt = room[:, XT0:AR0].rearrange("p (k t) -> p k t", k=KC)
        gates = room[:, G0:G0 + P * GRP].rearrange("p (i t) -> p i t", t=GRP)
        arena = room[:, AR0:ROOM]
        ASIZE = ROOM - AR0
        ps = ctx.enter_context(nc.psum_tensor("ps", [P, 8, 512], F32))
        xt_dram = nc.dram_tensor("xt_wait", (P, KC, T), F32).ap()

        def carve(spec):
            at, got = 0, {}
            for name, dims in spec:
                n = int(np.prod(dims))
                v = arena[:, at:at + n]
                if len(dims) == 2:
                    v = v.rearrange("p (a b) -> p a b", a=dims[0])
                if len(dims) == 3:
                    v = v.rearrange("p (a b c) -> p a b c", a=dims[0], b=dims[1])
                got[name] = v
                at += n
            assert at <= ASIZE, at
            return got

        common = [("nrt", (T,)), ("zw", (2, T)), ("zsq", (2, T)), ("rt", (2, T)),
                  ("ri", (T,)), ("ta", (T,)), ("tb", (T,)), ("st", (6, 64)), ("on", (2, T))]
        m0 = carve(common + [("tab", (TABW[0],)), ("qa", (4, T)), ("ka", (T,)), ("va", (4, P)), ("qb", (8, T)), ("kb", (8, T)),
                             ("vb", (4, T)), ("oa", (8, T))])
        m1 = carve(common + [("tab", (TABW[1],)), ("qr", (2, X)), ("kr", (2, T)), ("qd", (4, X)), ("kd", (T,)), ("vr", (4, T)),
                             ("vd", (4, P)), ("sg", (4, X)), ("oa", (8, X)), ("dt", (4, 4, X)),
                             ("ret", (3 * 4 * X,)), ("lg", (16,))])
        ret = m1["ret"]
        m1["de"] = ret[:, 0:8 * X].rearrange("p (b t) -> p b t", b=2)
        m1["sd"] = ret[:, 4 * X:12 * X].rearrange("p (b k t) -> p b k t", b=2, k=4)
        m1["orr"] = ret[:, 0:4 * X].rearrange("p (h t) -> p h t", h=4)
        m1["osq"] = ret[:, 4 * X:8 * X].rearrange("p (h t) -> p h t", h=4)
        m1["ort"] = ret[:, 8 * X:12 * X]
        tk = carve([("qt", (16, T)), ("sc", (2, 16, P)), ("cd", (HEADS, 256)), ("eq", (P, 16)),
                    ("v", (16, 16)), ("if", (16, 16)), ("bv", (HEADS, 16)), ("pf", (2, P)),
                    ("g", (2, 3, P)), ("sm", (2, HEADS)), ("i", (16, 16)), ("pi", (3, P)), ("keys", (16, P))])
        keys = tk["keys"]
        iu = tk["i"].bitcast(U32)
        piu = tk["pi"].bitcast(U32)
        mix = [m0, m1]
        for m in mix:
            m["sq8"], m["nt"], m["nrb"] = m["zsq"], m["zw"], m["ta"]
            m["pr"], m["pts"] = m["zw"], m["zsq"]
        m0["lq"], m0["lkv"], m0["zk"], m0["zks"] = (m0["oa"][:, 2 * i:2 * i + 2, :] for i in range(4))

        def tab(l, name):
            a, n = TAB[l][name]
            return mix[l]["tab"][:, a:a + n]

        def pcol(name, i=0, n=1, rows=slice(0, P)):
            return par[rows, PR[name] + i:PR[name] + i + n]

        s_par = sem("s_par")
        s_x = sem("s_x")
        s_tab = [sem(f"s_tab{l}") for l in range(2)]
        s_key = sem("s_key")
        s_slot = [sem(f"s_slot{i}") for i in range(SLOTS)]
        s_cs = sem("s_cs")
        s_ada = sem("s_ada")
        s_adr = sem("s_adr")
        s_adt = sem("s_adt")
        s_mod = sem("s_mod")
        s_nsq = sem("s_nsq")
        s_nss = sem("s_nss")
        s_nrt = sem("s_nrt")
        s_nt = sem("s_nt")
        s_nh = sem("s_nh")
        s_xt = sem("s_xt")
        s_z = [sem(f"s_z{l}") for l in range(2)]
        s_zw = [sem(f"s_zw{l}") for l in range(2)]
        s_rx = [sem(f"s_rx{l}") for l in range(2)]
        s_rt = [sem(f"s_rt{l}") for l in range(2)]
        s_it = [sem(f"s_it{l}") for l in range(2)]
        s_s = [sem(f"s_s{l}") for l in range(2)]
        s_nm = [sem(f"s_nm{l}") for l in range(2)]
        s_p = [sem(f"s_p{l}") for l in range(2)]
        s_pt = [sem(f"s_pt{l}") for l in range(2)]
        s_pe = [sem(f"s_pe{l}") for l in range(2)]
        s_pv = [sem(f"s_pv{l}") for l in range(2)]
        s_se = sem("s_se")
        s_es = sem("s_es")
        s_on = [sem(f"s_on{l}") for l in range(2)]
        s_ot = [sem(f"s_ot{l}") for l in range(2)]
        s_oe = [sem(f"s_oe{l}") for l in range(2)]
        s_wo = sem("s_wo")
        s_q = sem("s_q")
        s_qe = sem("s_qe")
        s_sc = sem("s_sc")
        s_sce = sem("s_sce")
        s_best = sem("s_best")
        s_bexp = sem("s_bexp")
        s_tk = sem("s_tk")
        s_tt = sem("s_tt")
        s_sel = sem("s_sel")
        s_oh = sem("s_oh")
        s_g = sem("s_g")
        s_ge = sem("s_ge")
        s_spill = sem("s_spill")
        s_rel = sem("s_rel")
        s_hh = sem("s_hh")
        s_hl = sem("s_hl")
        s_uh = sem("s_uh")
        s_ul = sem("s_ul")
        s_vh = sem("s_vh")
        s_vl = sem("s_vl")
        s_a = sem("s_a")
        s_gel = sem("s_gel")
        s_w = sem("s_w")
        s_wh = sem("s_wh")
        s_wl = sem("s_wl")
        s_y = sem("s_y")
        s_ye = sem("s_ye")
        s_yt = sem("s_yt")
        s_ex = sem("s_ex")
        s_dt = sem("s_dt")
        s_rs = sem("s_rs")
        s_rd = sem("s_rd")
        s_ro = sem("s_ro")
        s_roe = sem("s_roe")
        s_mu = sem("s_mu")
        s_oc = sem("s_oc")
        s_osq = sem("s_osq")
        s_yr = sem("s_yr")
        s_out = sem("s_out")
        s_act = sem("s_act")
        s_dve = sem("s_dve")

        loads, freed = [], {}

        def load(key, src, freed_by):
            loads.append((key, src))
            freed[key] = freed_by

        blocks = [(l, b) for l in range(2) for b in range(BLOCKS)]
        sets = [range(0, 4), range(4, 10), range(10, 14), range(14, 18), range(18, 21), range(21, 24)]

        def load_ada(qs):
            for q in qs:
                l, b = blocks[q]
                for kk in range(4):
                    load(("ada", q, kk), A["ada"][l, b, kk].rearrange("p k m -> p (k m)"), (s_ada, 4 * q + kk + 1))

        def hk(k, a=0, b=T):
            if b - a == T:
                return ht[:, :, k, :]
            return ht[:, a // X, k, a % X:a % X + b - a]

        def item(kind, groups, rows=slice(0, P), n=T, **kw):
            return dict(kind=kind, groups=groups, rows=rows, n=n, **kw)

        def feat(key, rows=slice(0, P), cols=slice(0, P), n=T, w=P):
            return (rows, slice(0, n), [(key, (k, w, cols), hk(k, 0, n)) for k in range(KC)])

        items0 = []
        for j in range(4):
            items0.append(item("rope", [feat(("w0", j))], w=pcol("aq"), dest=m0["qa"][:, j, :], tb="A"))
        items0.append(item("rope", [feat(("w0", 4))], w=pcol("ak"), dest=m0["ka"], tb="A"))
        for name, c0, dst in (("bql", 5, "lq"), ("bkvl", 7, "lkv")):
            items0.append(item("lora0", [feat(("w0", c0))], w=pcol(name, 0), dest=m0[dst]))
            items0.append(item("lora1", [feat(("w0", c0 + 1))], w=pcol(name, 1), dest=m0[dst]))
        items0.append(item("kr", [feat(("kr", 0), rows=slice(64, 96), cols=slice(0, 32), w=32)],
                           rows=slice(64, 96), w=pcol("bk", rows=slice(64, 96))))
        items0.append(item("plain", [(slice(0, P), slice(t * P, t * P + P),
                                      [(("w0", 9), (k, P, None), hk(k, t * P, t * P + P)) for k in range(KC)])
                                     for t in range(4)], dest=m0["va"].rearrange("p a b -> p (a b)")))
        for h in range(HEADS):
            items0.append(item("rope", [(slice(0, 96), slice(0, T),
                                         [(("uq", h // 4), (k, 384, slice((h % 4) * 96, (h % 4) * 96 + 96)),
                                           m0["lq"][:, k, :]) for k in range(2)])],
                               rows=slice(0, 96), w=pcol("bq", rows=slice(0, 96)), dest=m0["qb"][0:96, h, :], tb="B"))
        for h in range(HEADS):
            items0.append(item("ropek", [(slice(0, 64), slice(0, T),
                                          [(("ukvk", 0), (k, 512, slice(h * 64, h * 64 + 64)), m0["lkv"][:, k, :])
                                           for k in range(2)])],
                               rows=slice(0, 96), w=pcol("bk", rows=slice(0, 64)), dest=m0["kb"][0:96, h, :], tb="B"))
        for t in range(4):
            items0.append(item("plain", [(slice(0, P), slice(0, T),
                                          [(("ukvv", 0), (k, 512, None), m0["lkv"][:, k, t * P:t * P + P])
                                           for k in range(2)])], dest=m0["vb"][:, t, :]))
        items1 = []
        for j in range(4):
            items1.append(item("rope", [feat(("w1", 4 + j), n=X)], n=X, w=pcol("dq"), dest=m1["qd"][:, j, :], tb="A"))
        items1.append(item("rope", [feat(("w1", 8))], w=pcol("dk"), dest=m1["kd"], tb="A"))
        for j in range(2):
            items1.append(item("rope0", [feat(("w1", j), n=X)], n=X, w=pcol("one"), dest=m1["qr"][:, j, :], tb="A"))
        for j in range(2):
            items1.append(item("rope0", [feat(("w1", 2 + j))], w=pcol("one"), dest=m1["kr"][:, j, :], tb="A"))
        items1.append(item("plain", [(slice(0, P), slice(t * P, t * P + P),
                                      [(("w1", 9), (k, P, None), hk(k, t * P, t * P + P)) for k in range(KC)])
                                     for t in range(4)], dest=m1["vd"].rearrange("p a b -> p (a b)")))
        for t in range(4):
            items1.append(item("plain", [(slice(0, P), slice(0, T),
                                          [(("vr", k // 2), (k % 2, 512, None), hk(k, t * P, t * P + P))
                                           for k in range(KC)])], dest=m1["vr"][:, t, :]))
        for j in range(4):
            items1.append(item("silu", [feat(("w1", 10 + j), n=X)], n=X, dest=m1["sg"][:, j, :]))
        items = [items0, items1]

        def has_rx(it):
            return it["kind"] in ("rope", "ropek", "rope0", "lora1")

        def has_norm(it):
            return it["kind"] in ("rope", "ropek", "lora1")

        rx_upto = [[sum(has_rx(i) for i in its[:c + 1]) for c in range(len(its))] for its in items]
        rt_upto = [[sum(has_norm(i) for i in its[:c + 1]) for c in range(len(its))] for its in items]

        def load_items(l):
            last = {}
            for c, it in enumerate(items[l]):
                for _, _, mms in it["groups"]:
                    for key, _, _ in mms:
                        last[key] = c
            seen = set()
            for it in items[l]:
                for _, _, mms in it["groups"]:
                    for key, _, _ in mms:
                        if key not in seen:
                            seen.add(key)
                            s = A[key[0]][key[1]].rearrange("p k m -> p (k m)")
                            load(key, s, (s_z[l], last[key] + 1))

        def heads(l):
            m, got = mix[l], []
            for kind in ("A", "B") if l == 0 else ("A",):
                for qt in range(4 if l == 0 else 2):
                    for h in range(HEADS):
                        ks, blk = (slice(0, T), range(4)) if qt < 2 else (slice(X, T), range(2, 4))
                        if kind == "A":
                            j, po = h % 4, 64 * (h // 4)
                            r = slice(po, po + 64)
                            qn, kn, vn = ("qa", "ka", "va") if l == 0 else ("qd", "kd", "vd")
                            q, k = m[qn][r, j, qt * P:qt * P + P], m[kn][r, ks]
                            v = [m[vn][:, b, po:po + 64] for b in blk]
                            sc = HD ** -0.5
                        else:
                            q, k = m["qb"][0:96, h, qt * P:qt * P + P], m["kb"][0:96, h, ks]
                            v = [m["vb"][:, b, h * 64:h * 64 + 64] for b in blk]
                            sc = 96 ** -0.5
                        mask = None
                        if l == 0 and kind == "A" and qt < 2:
                            mask = (1 - qt, tab(0, "m01" if qt == 0 else "m10"))
                        got.append(dict(q=q, k=k, v=v, nb=len(v), mask=mask, sc=float(sc), h=h,
                                        sink=l == 0 and kind == "A",
                                        dest=m["oa"][:, (4 if kind == "B" or l == 1 else 0):
                                                     (8 if kind == "B" or l == 1 else 4), qt * P:qt * P + P]))
            return got

        att = [heads(0), heads(1)]
        nq_cols = [T, X]
        wo_base = [0, 8]
        xt_base = {"wo0": 0, "peer0": 8, "wo1": 24, "peer1": 32}

        def load_wo(l):
            for m in range(KC):
                load(("wo", l, m), A["wo"][l, m].rearrange("p k m -> p (k m)"), (s_wo, wo_base[l] + m + 1))

        tiles = [4, 2]
        tile_base = [0, 4]
        groups = [(0, 1), (0, 0), (1, 0)]

        def load_peer(l):
            for m in range(16):
                load(("wq", l, m), A["wq"][l, m].rearrange("p k m -> p (k m)"), (s_q, 16 * l + m + 1))

        load_ada(sets[0])
        load_items(0)
        load_ada(sets[1])
        load_wo(0)
        load_peer(0)
        for st in sets[2:]:
            load_ada(st)
        loads.append(("experts", 0))
        loads.append(("experts", 1))
        load_items(1)
        load_wo(1)
        load_peer(1)
        loads.append(("experts", 2))
        slot_of, before, owner, count, pos = {}, {}, [None] * SLOTS, [0] * SLOTS, 0
        expert_count = {}
        for key, src in loads:
            if key == "experts":
                pos = 0
                expert_count[src] = list(count)
                before[("experts", src)] = list(owner)
                for s in range(SLOTS):
                    count[s] += P // 2
                    owner[s] = (s_ul if s % 2 == 0 else s_vl, 2 * (P * src + P - 1 + s // 2))
                continue
            slot_of[key] = (pos, count[pos])
            before[key] = owner[pos]
            owner[pos] = freed[key]
            count[pos] += 1
            pos = (pos + 1) % SLOTS

        def landed(eng, key):
            slot, n = slot_of[key]
            eng.wait_ge(s_slot[slot], 16 * (n + 1))
            return ring[:, slot, :]

        def tab_dst(l):
            return mix[l]["tab"][:, 0:TABW[l]]

        ys = arena[:, ASIZE - 2 * D:ASIZE].rearrange("p (t d) -> p t d", t=GRP_TILES)
        REUSE = (AR0 - G0 + GRP - 1) // GRP

        def group_xt(n):
            return [xt_base["peer0"], xt_base["peer0"] + KC, xt_base["peer1"]][n]

        def sc_view(b):
            return tk["sc"][:, b, :, :]

        block = ctx.enter_context(nc.Block())

        @block.sync
        def _(sp):
            sp.dma_start(cst[:, :, :], A["cst"]).then_inc(s_par, 16)
            sp.dma_start(par[:, :], A["par"]).then_inc(s_par, 16)
            for key, src in loads:
                if key == "experts":
                    n = src
                    l, g = groups[n]

                    def pair_load(i, j, first):
                        c = slice(j, j + 1) if first else bass.ds(i * 2 + j, 1)
                        u = A["ut"][l, c].rearrange("a p k m -> p (a k m)")
                        v = A["vt"][l, c].rearrange("a p d -> p (a d)")
                        for slot, src, parted in ((2 * j, u, s_ul), (2 * j + 1, v, s_vl)):
                            if first:
                                w = before[("experts", n)][slot]
                                sp.wait_ge(w[0], w[1])
                            else:
                                sp.wait_ge(parted, i * 4 + (2 * P * n + 2 * j - 2))
                            sp.dma_start(ring[:, slot, :], src).then_inc(s_slot[slot], 16)

                    for j in range(2):
                        pair_load(0, j, True)
                    with sp.Fori(1, P // 2) as i:
                        for j in range(2):
                            pair_load(i, j, False)
                    continue
                slot, n = slot_of[key]
                if before[key] is not None:
                    sp.wait_ge(before[key][0], before[key][1])
                sp.dma_start(ring[:, slot, 0:src.shape[-1]], src).then_inc(s_slot[slot], 16)
            sp.wait_ge(s_xt, xt_base["peer1"] + KC)
            sp.dma_start(out, xt[:, :, 0:X]).then_inc(s_out, 16)
            sp.wait_ge(s_out, 16)

        @block.gpsimd
        def _(pool):
            pool.dma_start(xt, A["x"]).then_inc(s_x, 16)
            pool.dma_start(tab_dst(0), A["tab0"]).then_inc(s_tab[0], 16)

            def spill(width):
                pool.dma_start(xt_dram[:, :, 0:width], xt[:, :, 0:width]).then_inc(s_spill, 16)

            def reload(n, half):
                if half == groups[n][1]:
                    pool.wait_ge(s_w, P * n + REUSE)
                c = slice(half * X, half * X + X)
                pool.dma_start(xt[:, :, c], xt_dram[:, :, c]).then_inc(s_rel, 16)

            pool.wait_ge(s_xt, xt_base["wo0"] + KC)
            pool.dma_start(keys, A["keys"][0]).then_inc(s_key, 16)
            spill(T)
            pool.wait_ge(s_spill, 16)
            reload(0, 1)
            pool.wait_ge(s_xt, xt_base["peer0"] + KC)
            pool.dma_start(xt_dram[:, :, X:T], xt[:, :, X:T]).then_inc(s_spill, 16)
            pool.wait_ge(s_spill, 32)
            reload(1, 0)
            reload(1, 1)
            pool.wait_ge(s_xt, xt_base["wo1"])
            pool.dma_start(tab_dst(1), A["tab1"]).then_inc(s_tab[1], 16)
            pool.wait_ge(s_xt, xt_base["peer1"])
            pool.dma_start(keys, A["keys"][1]).then_inc(s_key, 16)
            spill(X)
            pool.wait_ge(s_spill, 48)
            reload(2, 0)

        @block.tensor
        def _(pe):
            mm = pe.matmul

            def ada_mm(q, k):
                bank = 7 if q in sets[1] else 6 + q % 2
                if k == 0:
                    if q == 0:
                        pe.wait_ge(s_cs, 1)
                    elif q in sets[1] or q in (10, 11):
                        pe.wait_ge(s_adr, q)
                    elif q >= 2:
                        pe.wait_ge(s_adr, q - 1)
                w = landed(pe, ("ada", q, k // 2))
                last = mm(ps[0:2, bank, :], cs[:, k, :], w[:, (k % 2) * 512:(k % 2) * 512 + 512],
                          start=k == 0, stop=k == KC - 1)
                if k % 2:
                    last.then_inc(s_ada, 1)

            def ada_transpose(q):
                pe.wait_ge(s_adr, q + 1)
                n = next(i for i, st in enumerate(sets) if q in st)
                if n and q == sets[n][0]:
                    pe.wait_ge(s_mod, n)
                for j in range(4):
                    last = pe.transpose(ps[:, 2, 8 * q + 2 * j:8 * q + 2 * j + 2], rows[:, q % 2, j * P:j * P + P],
                                        ident[0:2, 0:2])
                last.then_inc(s_adt, 1)

            def modulation(n):
                for q in sets[n]:
                    for k in range(KC):
                        ada_mm(q, k)
                    if q != sets[n][0]:
                        ada_transpose(q - 1)
                ada_transpose(sets[n][-1])

            def norm(n):
                width = T if n < 3 else X
                pe.wait_ge(s_tab[n // 2], 16)
                for k in range(KC):
                    pe.wait_ge(s_nsq, KC * n + k + 1)
                    mm(ps[:, 6, 0:width], tab(n // 2, "ones"), mix[n // 2]["sq8"][:, k % 2, 0:width],
                       start=k == 0, stop=k == KC - 1).then_inc(s_nss, 1)

            def project(l, c):
                it = items[l][c]
                if c >= 3:
                    pe.wait_ge(s_zw[l], c - 2)
                if l == 0 and it["kind"] in ("rope", "ropek", "plain") and c >= 11:
                    pe.wait_ge(s_it[0], rx_upto[0][8])
                for rows, cols, mms in it["groups"]:
                    for i, (key, (k, w, wcols), act) in enumerate(mms):
                        wr = landed(pe, key)
                        if wcols is None:
                            lhs, rhs = act, wr[:, k * w:k * w + w]
                        else:
                            lhs, rhs = wr[:, k * w + wcols.start:k * w + wcols.stop], act
                        dst = ps[rows, c % 3, cols]
                        if len(rhs.shape) == 3:
                            dst = dst.rearrange("p (s t) -> p s t", s=2)
                        last = mm(dst, lhs, rhs, start=i == 0, stop=i == len(mms) - 1)
                last.then_inc(s_z[l], 1)

            def reduce_rotate(l, c):
                it, m = items[l][c], mix[l]
                if not has_rx(it):
                    return
                pe.wait_ge(s_zw[l], c + 1)
                if c == 0:
                    pe.wait_ge(s_tab[l], 16)
                if c >= 2 and rx_upto[l][c - 2]:
                    pe.wait_ge(s_it[l], rx_upto[l][c - 2])
                r, n = it["rows"], it["n"]
                if it["kind"] == "lora1":
                    mm(ps[:, 3 + c % 2, :], tab(l, "ones"), m["zsq"][:, (c - 1) % 2, :], start=True, stop=False)
                    mm(ps[:, 3 + c % 2, :], tab(l, "ones"), m["zsq"][:, c % 2, :], start=False, stop=True).then_inc(s_rx[l], 1)
                    return
                zw, zsq = (m["zk"], m["zks"]) if it["kind"] == "ropek" else (m["zw"], m["zsq"])
                w = 96 if it["tb"] == "B" else P
                bo, rot = ("bo96", "rot96") if it["tb"] == "B" else ("bo64", "rot64")
                if has_norm(it):
                    mm(ps[r, 3 + c % 2, 0:n], tab(l, bo)[r, 0:w], zsq[r, c % 2, 0:n], start=True, stop=True)
                mm(ps[r, 5 + c % 2, 0:n], tab(l, rot)[r, 0:w], zw[r, c % 2, 0:n], start=True,
                   stop=True).then_inc(s_rx[l], 1)

            def projections(l):
                pe.wait_ge(s_nh, KC * (2 * l + 1))
                project(l, 0)
                for c in range(len(items[l])):
                    if c + 1 < len(items[l]):
                        project(l, c + 1)
                    reduce_rotate(l, c)

            def scores(l, a):
                it = att[l][a]
                if a >= 2:
                    pe.wait_ge(s_p[l], a - 1)
                n = it["nb"] * P
                last = mm(ps[:, a % 2, 0:n], it["q"], it["k"], start=True, stop=it["mask"] is None)
                if it["mask"]:
                    b, mk = it["mask"]
                    last = mm(ps[:, a % 2, b * P:b * P + P], ident, mk, start=False, stop=True)
                last.then_inc(s_s[l], 1)

            def transpose_probs(l, a):
                it, m = att[l][a], mix[l]
                pe.wait_ge(s_p[l], a + 1)
                if a >= 2:
                    pe.wait_ge(s_pe[l], a - 1)
                for b in range(it["nb"]):
                    last = pe.transpose(ps[:, 3 + a % 2, b * P:b * P + P], m["pr"][:, a % 2, b * P:b * P + P], ident)
                last.then_inc(s_pt[l], 1)

            def values(l, a):
                it, m = att[l][a], mix[l]
                g = a // 8
                pe.wait_ge(s_pe[l], a + 1)
                if a % 8 == 0 and g >= 2:
                    pe.wait_ge(s_oe[l], g - 1)
                for b in range(it["nb"]):
                    last = mm(ps[:, 5 + g % 2, it["h"] * 64:it["h"] * 64 + 64], m["pts"][:, a % 2, b * P:b * P + P],
                              it["v"][b], start=b == 0, stop=b == it["nb"] - 1)
                last.then_inc(s_pv[l], 1)

            def transpose_out(l, g):
                pe.wait_ge(s_on[l], g + 1)
                for j in range(4):
                    last = pe.transpose(ps[:, 5 + g % 2, j * P:j * P + P], mix[l]["on"][:, g % 2, j * P:j * P + P], ident)
                last.then_inc(s_ot[l], 1)

            def attention(l):
                n = len(att[l])
                pe.wait_ge(s_zw[l], len(items[l]))
                pe.wait_ge(s_it[l], rx_upto[l][-1])
                if l == 1:
                    pe.wait_ge(s_yr, 1)
                scores(l, 0)
                for a in range(n):
                    if a + 1 < n:
                        scores(l, a + 1)
                    if l == 0 and a < 8 * len(sets[1]):
                        ada_mm(sets[1][a // 8], a % 8)
                    if l == 0 and a % 8 == 2 and 0 < a // 8 <= len(sets[1]):
                        ada_transpose(sets[1][a // 8 - 1])
                    if a >= 1:
                        values(l, a - 1)
                    transpose_probs(l, a)
                    if a % 8 == 2 and a > 8:
                        transpose_out(l, a // 8 - 1)
                values(l, n - 1)
                transpose_out(l, n // 8 - 1)

            def retention():
                pe.wait_ge(s_zw[1], len(items1))
                pe.wait_ge(s_it[1], rx_upto[1][-1])
                m = m1

                def rscores(h):
                    r = slice(64 * (h % 2), 64 * (h % 2) + 64)
                    for kt in range(4):
                        last = mm(ps[:, 2 * (h % 2) + kt // 2, (kt % 2) * X:(kt % 2) * X + X],
                                  m["kr"][r, h // 2, kt * P:kt * P + P], m["qr"][r, h // 2, :], start=True, stop=True)
                    last.then_inc(s_rs, 1)

                rscores(0)
                rscores(1)
                for h in range(4):
                    pe.wait_ge(s_rd, h + 1)
                    for kt in range(4):
                        last = mm(ps[:, 4 + h // 2, (h % 2) * X:(h % 2) * X + X], m["vr"][:, kt, h * P:h * P + P],
                                  m["sd"][:, h % 2, kt, :],
                                  start=kt == 0, stop=kt == 3)
                    last.then_inc(s_ro, 1)
                    if h + 2 < 4:
                        rscores(h + 2)
                pe.wait_ge(s_roe, 1)
                for b in range(2):
                    last = mm(ps[:, b, :], tab(1, "ones"), m["orr"][:, 2 * b:2 * b + 2, :].rearrange("p a b -> p (a b)"), start=True, stop=True)
                last.then_inc(s_mu, 1)
                pe.wait_ge(s_osq, 1)
                for b in range(2):
                    last = mm(ps[:, 2 + b, :], tab(1, "ones"), m["osq"][:, 2 * b:2 * b + 2, :].rearrange("p a b -> p (a b)"), start=True, stop=True)
                last.then_inc(s_mu, 1)

            def output(l):
                pe.wait_ge(s_oe[l], len(att[l]) // 8)
                if l == 0:
                    pe.wait_ge(s_mod, 2)
                n = nq_cols[l]
                for m in range(KC):
                    w = landed(pe, ("wo", l, m)).rearrange("p (k m) -> p k m", k=KC)
                    if m >= 3:
                        pe.wait_ge(s_xt, xt_base[f"wo{l}"] + m - 2)
                    for k in range(KC):
                        last = mm(ps[:, m % 3, 0:n], w[:, k, :], mix[l]["oa"][:, k, :], start=k == 0, stop=k == KC - 1)
                    last.then_inc(s_wo, 1)

            def queries(l):
                n = tiles[l] * P
                pe.wait_ge(s_nh, KC * (2 * l + 2))
                for m in range(16):
                    w = landed(pe, ("wq", l, m)).rearrange("p (k m) -> p k m", k=KC)
                    if m >= 3:
                        pe.wait_ge(s_qe, 16 * l + m - 2)
                    for k in range(KC):
                        rhs = hk(k, 0, n)
                        dst = ps[:, m % 3, 0:n]
                        if n == T:
                            dst = dst.rearrange("p (s t) -> p s t", s=2)
                        last = mm(dst, w[:, k, :], rhs, start=k == 0, stop=k == KC - 1)
                    last.then_inc(s_q, 1)
                pe.wait_ge(s_qe, 16 * l + 16)
                pe.wait_ge(s_key, 16 * (l + 1))

            def key_scores(l, t):
                for u in range(4):
                    q = (tile_base[l] + t) * 4 + u
                    if t * 4 + u >= 3:
                        pe.wait_ge(s_sce, q - 2)
                    for j in range(4):
                        hp = 4 * u + j
                        last = mm(ps[:, 3 + q % 3, j * P:j * P + P], tk["qt"][:, hp, t * P:t * P + P],
                                  keys[:, hp, :], start=True, stop=True)
                    last.then_inc(s_sc, 1)

            def select_transpose(l, t):
                n = tile_base[l] + t
                pe.wait_ge(s_tk, n + 1)
                if t >= 2:
                    pe.wait_ge(s_sel, n - 1)
                for j in range(3):
                    last = pe.transpose(ps[:, t % 2, j * P:j * P + P], tk["g"][:, t % 2, j, :], ident)
                last.then_inc(s_tt, 1)

            def selection(l):
                key_scores(l, 0)
                key_scores(l, 1)
                for t in range(tiles[l]):
                    if l == 0:
                        modulation(2 + t)
                    select_transpose(l, t)
                    if t + 2 < tiles[l]:
                        key_scores(l, t + 2)

            def gate_matrices(n):
                l, g = groups[n]
                pe.wait_ge(s_sel, tile_base[l] + tiles[l])
                if n == 1:
                    pe.wait_ge(s_xt, xt_base["peer0"] + KC)

                def steps(i, first):
                    for j in range(2):
                        pe.wait_ge(s_oh, i * 2 + (64 * n + j + 1))
                        if not first:
                            pe.wait_ge(s_ge, i * 2 + (64 * n + j - 1))
                        for t in range(4):
                            last = mm(ps[:, j, t * P:t * P + P], oha[:, j, t, :], ohb[:, j, t, :], start=True, stop=True)
                        last.then_inc(s_g, 1)

                steps(0, True)
                with pe.Fori(1, 32) as i:
                    steps(i, False)

            def experts(n):
                l, g = groups[n]
                cnt = expert_count[n]

                def up(i, j, first):
                    if not first:
                        pe.wait_ge(s_gel, i * 2 + (P * n + j - 1))
                    for half in range(2):
                        pe.wait_ge(s_ul, i * 4 + (2 * P * n + 2 * j + half + 1))
                        for k in range(4 * half, 4 * half + 4):
                            for p, (u, h) in enumerate(((uh, hh), (uh, hl), (ul, hh))):
                                last = mm(ps[:, 4 + j, 0:GRP], u[:, k * P:k * P + P], h[:, k, :],
                                          start=k == 0 and p == 0, stop=k == KC - 1 and p == 2)
                        last.then_inc(s_a, 1)

                def down(i, j, start, stop):
                    pe.wait_ge(s_wl, i * 2 + (P * n + j + 1))
                    for half in range(2):
                        c = slice(half * 512, half * 512 + 512)
                        pe.wait_ge(s_vl, i * 4 + (2 * P * n + 2 * j + half + 1))
                        for tt in range(GRP_TILES):
                            for p, (w, v) in enumerate(((wh, vh), (wh, vl), (wl, vh))):
                                last = mm(ps[:, 2 * tt + half, :], w[:, j, tt * P:tt * P + P], v[:, c],
                                          start=start and p == 0, stop=stop and p == 2)
                        last.then_inc(s_y, 1)

                pe.wait_ge(s_ge, 64 * (n + 1))
                pe.wait_ge(s_hl, n + 1)
                up(0, 0, True)
                up(0, 1, True)
                down(0, 0, True, False)
                with pe.Fori(1, P // 2) as i:
                    up(i, 0, False)
                    down(i - 1, 1, False, False)
                    up(i, 1, False)
                    down(i, 0, False, False)
                down(P // 2 - 1, 1, False, True)
                pe.wait_ge(s_ye, 2 * n + 2)
                for m in range(KC):
                    if m >= 2:
                        pe.wait_ge(s_xt, group_xt(n) + m - 1)
                    for tt in range(GRP_TILES):
                        last = pe.transpose(ps[:, 4 + m % 2, tt * P:tt * P + P], ys[:, tt, m * P:m * P + P], ident)
                    last.then_inc(s_yt, 1)

            pe.wait_ge(s_par, 32)
            modulation(0)
            norm(0)
            projections(0)
            attention(0)
            output(0)
            norm(1)
            queries(0)
            selection(0)
            for n in range(2):
                gate_matrices(n)
                experts(n)
            norm(2)
            projections(1)
            retention()
            attention(1)
            output(1)
            norm(3)
            queries(1)
            selection(1)
            gate_matrices(2)
            experts(2)

        @block.scalar
        def _(act):
            own = Step(act, s_act)
            af = act.activation

            def ada_row(q):
                act.wait_ge(s_ada, 4 * q + 4)
                if q >= 2:
                    act.wait_ge(s_adt, q - 1)
                bank = 7 if q in sets[1] else 6 + q % 2
                af(rows[:, q % 2, :], ps[0:2, bank, :], ACT.Copy).then_inc(s_adr, 1)

            def norm(n):
                width = T if n < 3 else X
                m, l, w = mix[n // 2], n // 2, n % 2
                for k in range(KC):
                    if n == 0:
                        act.wait_ge(s_x, 16)
                    else:
                        act.wait_ge(s_xt, {1: 0, 2: xt_base["peer0"] + KC, 3: xt_base["wo1"]}[n] + k + 1)
                    if KC * n + k >= 2:
                        act.wait_ge(s_nss, KC * n + k - 1)
                    af(m["sq8"][:, k % 2, 0:width], xt[:, k, 0:width], ACT.Square).then_inc(s_nsq, 1)
                act.wait_ge(s_nss, KC * n + KC)
                af(m["nrt"][:, 0:width], ps[:, 6, 0:width], ACT.Sqrt, bias=pcol("eps"), scale=1.0 / D).then_inc(s_nrt, 1)
                for k in range(KC):
                    act.wait_ge(s_nt, KC * n + k + 1)
                    for st in range(width // X):
                        last = af(ht[:, st, k, :], m["nt"][:, k % 2, st * X:st * X + X], ACT.Identity,
                                  bias=mod[:, l, 24 * w + k, st:st + 1])
                    last.then_inc(s_nh, 1)

            def projections(l):
                m = mix[l]

                def read(c):
                    it = items[l][c]
                    kind, r, n = it["kind"], it["rows"], it["n"]
                    z = ps[r, c % 3, 0:n]
                    act.wait_ge(s_z[l], c + 1)
                    if kind == "plain":
                        af(it["dest"], z, ACT.Copy).then_inc(s_zw[l], 1)
                        return
                    if kind == "silu":
                        af(it["dest"], z, ACT.Silu).then_inc(s_zw[l], 1)
                        return
                    if c >= 2:
                        b = c - 2
                        if kind != "kr" and items[l][b]["kind"] == "lora0":
                            b = c - 1
                        if rx_upto[l][b]:
                            act.wait_ge(s_rx[l], rx_upto[l][b])
                        if rx_upto[l][c - 2]:
                            act.wait_ge(s_it[l], rx_upto[l][c - 2])
                    if kind == "kr":
                        for b in range(2):
                            own.inc(af(m["zk"][r, b, :], z, ACT.Copy, scale=it["w"]))
                            last = af(m["zks"][r, b, :], z, ACT.Square)
                        last.then_inc(s_zw[l], 1)
                        return
                    if kind == "ropek":
                        r = slice(0, 64)
                        z = ps[r, c % 3, 0:n]
                        af(m["zk"][r, c % 2, 0:n], z, ACT.Copy, scale=it["w"])
                        af(m["zks"][r, c % 2, 0:n], z, ACT.Square).then_inc(s_zw[l], 1)
                        return
                    zw = m["zw"][r, c % 2, 0:n] if kind in ("rope", "rope0") else it["dest"][:, int(kind == "lora1"), :]
                    if kind == "rope0":
                        af(zw, z, ACT.Copy, scale=1.0).then_inc(s_zw[l], 1)
                        return
                    af(zw, z, ACT.Copy, scale=it["w"])
                    af(m["zsq"][r, c % 2, 0:n], z, ACT.Square).then_inc(s_zw[l], 1)

                def root(c):
                    it = items[l][c]
                    if not has_norm(it):
                        return
                    r, n = it["rows"], it["n"]
                    act.wait_ge(s_rx[l], rx_upto[l][c])
                    if c >= 2 and rx_upto[l][c - 2]:
                        act.wait_ge(s_it[l], rx_upto[l][c - 2])
                    dim = {"lora1": 256, "rope": 64, "ropek": 96}[it["kind"]]
                    if it["kind"] == "rope" and it["tb"] == "B":
                        dim = 96
                    af(m["rt"][r, c % 2, 0:n], ps[r, 3 + c % 2, 0:n], ACT.Sqrt, bias=pcol("eps", rows=r),
                       scale=1.0 / dim).then_inc(s_rt[l], 1)

                for c in range(len(items[l])):
                    read(c)
                    if c >= 1:
                        root(c - 1)
                root(len(items[l]) - 1)

            def attention(l):
                m = mix[l]

                def exps(a):
                    it = att[l][a]
                    n = it["nb"] * P
                    act.wait_ge(s_nm[l], a + 1)
                    if a >= 2:
                        act.wait_ge(s_pt[l], a - 1)
                    af(m["pr"][:, a % 2, 0:n], ps[:, a % 2, 0:n], ACT.Exp, bias=m["st"][:, 0, a:a + 1],
                       scale=it["sc"], accum_out=m["st"][:, 1, a:a + 1]).then_inc(s_p[l], 1)

                def evacuate(a):
                    n = att[l][a]["nb"] * P
                    act.wait_ge(s_pt[l], a + 1)
                    if a >= 2:
                        act.wait_ge(s_pv[l], a - 1)
                    af(m["pts"][:, a % 2, 0:n], ps[:, 3 + a % 2, 0:n], ACT.Copy).then_inc(s_pe[l], 1)

                def sinks(g):
                    act.wait_ge(s_se, g + 1)
                    c = slice(8 * g, 8 * g + 8)
                    af(m["st"][:, 3, c], m["st"][:, 2, c], ACT.Exp).then_inc(s_es, 1)

                def gather(g):
                    act.wait_ge(s_ot[l], g + 1)
                    af(att[l][8 * g]["dest"], ps[:, 5 + g % 2, :].rearrange("p (j q) -> p j q", j=4),
                       ACT.Copy).then_inc(s_oe[l], 1)

                for a in range(len(att[l])):
                    exps(a)
                    if a % 8 == 0 and a and att[l][a - 1]["sink"]:
                        sinks(a // 8 - 1)
                    if l == 0 and a % 8 == 0 and 0 < a // 8 <= len(sets[1]):
                        ada_row(sets[1][a // 8 - 1])
                    evacuate(a)
                    if a % 8 == 3 and a > 8:
                        gather(a // 8 - 1)
                gather(len(att[l]) // 8 - 1)

            def decays():
                m = m1
                act.wait_ge(s_tab[1], 16)
                own.do(af(m["lg"][:, 0:8], pcol("decf", 0, 8), ACT.Exp, scale=-1.0))
                own.do(af(m["lg"][:, 8:16], m["lg"][:, 0:8], ACT.Ln, bias=pcol("one")))
                own.do(af(m["lg"][:, 0:8], m["lg"][:, 8:16], ACT.Copy, scale=-1.0))
                for h in range(4):
                    if h >= 1:
                        act.wait_ge(s_dt, h)
                    af(m["de"][:, 0, :], tab(1, "df"), ACT.Exp, scale=m["lg"][:, h:h + 1])
                    af(m["de"][:, 1, :], tab(1, "db"), ACT.Exp, scale=m["lg"][:, 4 + h:5 + h]).then_inc(s_ex, 1)

            def retention():
                m = m1
                act.wait_ge(s_ro, 4)
                af(m["orr"].rearrange("p h t -> p (h t)"), ps[:, 4:6, :].rearrange("p a b -> p (a b)"),
                   ACT.Copy).then_inc(s_roe, 1)
                act.wait_ge(s_oc, 1)
                af(m["osq"].rearrange("p h t -> p (h t)"), m["orr"].rearrange("p h t -> p (h t)"),
                   ACT.Square).then_inc(s_osq, 1)
                act.wait_ge(s_mu, 2)
                af(m["ort"], ps[:, 2:4, :].rearrange("p a b -> p (a b)"), ACT.Sqrt, bias=pcol("eps"),
                   scale=1.0 / P).then_inc(s_osq, 1)

            def peer(l):
                n = tiles[l] * P
                for m in range(16):
                    act.wait_ge(s_q, 16 * l + m + 1)
                    af(tk["qt"][:, m, 0:n], ps[:, m % 3, 0:n], ACT.Copy).then_inc(s_qe, 1)

                def score_copy(t):
                    for u in range(4):
                        q = (tile_base[l] + t) * 4 + u
                        act.wait_ge(s_sc, q + 1)
                        af(sc_view(t % 2)[:, 4 * u:4 * u + 4, :].rearrange("p a b -> p (a b)"),
                           ps[:, 3 + q % 3, :], ACT.Copy).then_inc(s_sce, 1)

                score_copy(0)
                score_copy(1)
                for t in range(tiles[l]):
                    k = tile_base[l] + t
                    if l == 0:
                        for q in sets[2 + t]:
                            ada_row(q)
                    act.wait_ge(s_best, k + 1)
                    af(tk["bv"].rearrange("p h k -> p (h k)"), tk["bv"].rearrange("p h k -> p (h k)"),
                       ACT.Exp).then_inc(s_bexp, 1)
                    act.wait_ge(s_tt, k + 1)
                    af(sel[:, :, t * P:t * P + P], ps[:, t % 2, 0:2 * P].rearrange("p (a b) -> p a b", a=2), ACT.Copy)
                    af(sel2[:, t * P:t * P + P], ps[:, t % 2, 2 * P:3 * P], ACT.Copy).then_inc(s_sel, 1)
                    if t + 2 < tiles[l]:
                        score_copy(t + 2)

            def gate_matrices(n):
                l, g = groups[n]
                if n != 1:
                    act.wait_ge(s_tk, tile_base[l] + tiles[l])
                af(hh[:, :, :], ht[:, g, :, :], ACT.Copy).then_inc(s_hh, 1)
                act.wait_ge(s_spill, 16 * (n + 1))
                act.wait_ge(s_hl, n + 1)

                def steps(i):
                    for j in range(2):
                        act.wait_ge(s_g, i * 2 + (64 * n + j + 1))
                        af(gates[:, :, bass.ds(i * 8 + 4 * j, 4)] if not isinstance(i, int) else
                           gates[:, :, i * 8 + 4 * j:i * 8 + 4 * j + 4],
                           ps[:, j, :].rearrange("p (t i) -> p i t", t=4), ACT.Copy).then_inc(s_ge, 1)

                with act.Fori(0, 32) as i:
                    steps(i)

            def experts(n):
                act.wait_ge(s_g, 64 * (n + 1))
                cnt = expert_count[n]

                def up_part(i, j, first):
                    act.wait_ge(s_slot[2 * j], i * 16 + 16 * (cnt[2 * j] + 1))
                    for half in range(2):
                        c = slice(half * 512, half * 512 + 512)
                        if not first:
                            act.wait_ge(s_a, i * 4 + (2 * P * n + 2 * j + half - 1))
                        af(uh[:, c], ring[:, 2 * j, c], ACT.Copy).then_inc(s_uh, 1)

                def down_part(i, j, first):
                    act.wait_ge(s_slot[2 * j + 1], i * 16 + 16 * (cnt[2 * j + 1] + 1))
                    for half in range(2):
                        c = slice(half * 512, half * 512 + 512)
                        if not first:
                            act.wait_ge(s_y, i * 4 + (2 * P * n + 2 * j + half - 1))
                        af(vh[:, c], ring[:, 2 * j + 1, c], ACT.Copy).then_inc(s_vh, 1)

                def gelu(i, j, first):
                    act.wait_ge(s_a, i * 4 + (2 * P * n + 2 * j + 2))
                    if not first:
                        act.wait_ge(s_wl, i * 2 + (P * n + j - 1))
                    af(gel[:, j, :], ps[:, 4 + j, 0:GRP], ACT.Gelu_apprx_tanh).then_inc(s_gel, 1)

                def high(i, j, first):
                    act.wait_ge(s_w, i * 2 + (P * n + j + 1))
                    if not first:
                        act.wait_ge(s_y, i * 4 + (2 * P * n + 2 * j - 2))
                    af(wh[:, j, :], gel[:, j, :], ACT.Copy).then_inc(s_wh, 1)

                def both(i, j, first, last):
                    if not last:
                        up_part(i + j, 1 - j, False)
                    gelu(i, j, first)
                    high(i, j, first)
                    down_part(i, j, first and j == 0)

                up_part(0, 0, True)
                both(0, 0, True, False)
                both(0, 1, True, False)
                with act.Fori(1, P // 2 - 1) as i:
                    both(i, 0, False, False)
                    both(i, 1, False, False)
                both(P // 2 - 1, 0, False, False)
                both(P // 2 - 1, 1, False, True)
                act.wait_ge(s_y, 2 * P * (n + 1))
                for tt in range(GRP_TILES):
                    af(ys[:, tt, :], ps[:, 2 * tt:2 * tt + 2, :].rearrange("p a b -> p (a b)"), ACT.Copy).then_inc(s_ye, 1)

            act.wait_ge(s_par, 32)
            af(cs[:, :, :], pcol("c", 0, 16).rearrange("p (k s) -> p k s", s=2), ACT.Silu).then_inc(s_cs, 1)
            for q in sets[0]:
                ada_row(q)
            norm(0)
            projections(0)
            attention(0)
            norm(1)
            peer(0)
            for n in range(2):
                gate_matrices(n)
                experts(n)
            norm(2)
            decays()
            projections(1)
            retention()
            attention(1)
            norm(3)
            peer(1)
            gate_matrices(2)
            experts(2)

        @block.vector
        def _(dve):
            own = Step(dve, s_dve)
            tt, ts, stt = dve.tensor_tensor, dve.tensor_scalar, dve.scalar_tensor_tensor

            def modulation(n):
                dve.wait_ge(s_adt, sets[n][-1] + 1)
                todo = []
                for l in range(2):
                    qs = [q for q in sets[n] if blocks[q][0] == l]
                    if not qs:
                        continue
                    a, cnt = 4 * blocks[qs[0]][1], 4 * len(qs)
                    own.inc(tt(mod[:, l, a:a + cnt, :], ps[:, 2, 8 * qs[0]:8 * qs[0] + 2 * cnt].rearrange(
                        "p (m s) -> p m s", s=2),
                        pcol("ada_b", 48 * l + a, cnt).unsqueeze(2).broadcast_to([P, cnt, 2]), ALU.add))
                    for q in qs:
                        for w in range(2):
                            at = 4 * blocks[q][1] - (8 + 24 * w)
                            if at in (0, 4):
                                todo.append((l, w, at))
                own.wait()
                for l, w, at in todo:
                    own.inc(stt(out=gain[:, 2 * l + w, at:at + 4, :], in0=mod[:, l, 8 + 24 * w + at:12 + 24 * w + at, :],
                                scalar=1.0, op0=ALU.add, op1=ALU.mult,
                                in1=pcol("n2" if w else "n1", KC * l + at, 4).unsqueeze(2).broadcast_to([P, 4, 2])))
                own.wait()
                dve.sem_inc(s_mod, 1)

            def norm(n):
                width = T if n < 3 else X
                m = mix[n // 2]
                dve.wait_ge(s_nrt, n + 1)
                own.do(dve.reciprocal(m["nrb"][:, 0:width], m["nrt"][:, 0:width]))
                for k in range(KC):
                    if k >= 2:
                        dve.wait_ge(s_nh, KC * n + k - 1)
                    for st in range(width // X):
                        c = slice(st * X, st * X + X)
                        last = stt(out=m["nt"][:, k % 2, c], in0=xt[:, k, c], scalar=gain[:, n, k, st:st + 1],
                                   in1=m["nrb"][:, c], op0=ALU.mult, op1=ALU.mult)
                    last.then_inc(s_nt, 1)

            def projections(l):
                m = mix[l]
                for c, it in enumerate(items[l]):
                    if not has_rx(it):
                        continue
                    r, n = it["rows"], it["n"]
                    if it["kind"] == "lora1":
                        dve.wait_ge(s_rt[l], rt_upto[l][c])
                        own.do(dve.reciprocal(m["ri"], m["rt"][:, c % 2, :]))
                        own.inc(tt(it["dest"][:, 0, :], it["dest"][:, 0, :], m["ri"], ALU.mult))
                        tt(it["dest"][:, 1, :], it["dest"][:, 1, :], m["ri"], ALU.mult).then_inc(s_it[l], 1)
                        continue
                    zw = m["zk"] if it["kind"] == "ropek" else m["zw"]
                    dve.wait_ge(s_rx[l], rx_upto[l][c])
                    own.inc(tt(m["ta"][r, 0:n], zw[r, c % 2, 0:n], tab(l, "cos" + it["tb"])[r, 0:n], ALU.mult))
                    own.do(tt(m["tb"][r, 0:n], ps[r, 5 + c % 2, 0:n], tab(l, "sin" + it["tb"])[r, 0:n], ALU.mult))
                    if not has_norm(it):
                        tt(it["dest"], m["ta"][r, 0:n], m["tb"][r, 0:n], ALU.add).then_inc(s_it[l], 1)
                        dve.wait_ge(s_it[l], rx_upto[l][c])
                        continue
                    own.inc(tt(m["ta"][r, 0:n], m["ta"][r, 0:n], m["tb"][r, 0:n], ALU.add))
                    dve.wait_ge(s_rt[l], rt_upto[l][c])
                    own.do(dve.reciprocal(m["ri"][r, 0:n], m["rt"][r, c % 2, 0:n]))
                    tt(it["dest"], m["ta"][r, 0:n], m["ri"][r, 0:n], ALU.mult).then_inc(s_it[l], 1)
                    dve.wait_ge(s_it[l], rx_upto[l][c])

            def attention(l):
                m = mix[l]
                st = m["st"]

                def sink_terms(g):
                    c = slice(8 * g, 8 * g + 8)
                    tt(st[:, 2, c], st[:, 0, c], nsink[:, :], ALU.subtract).then_inc(s_se, 1)

                def normalise(g):
                    c = slice(8 * g, 8 * g + 8)
                    dve.wait_ge(s_pv[l], 8 * g + 8)
                    den = st[:, 1, c]
                    if att[l][8 * g]["sink"]:
                        dve.wait_ge(s_es, g + 1)
                        own.do(tt(st[:, 5, c], st[:, 1, c], st[:, 3, c], ALU.add))
                        den = st[:, 5, c]
                    own.do(dve.reciprocal(st[:, 4, c], den))
                    if g >= 2:
                        dve.wait_ge(s_ot[l], g - 1)
                    tt(m["on"][:, g % 2, :].rearrange("p (h d) -> p h d", h=HEADS),
                       ps[:, 5 + g % 2, :].rearrange("p (h d) -> p h d", h=HEADS),
                       st[:, 4, c].unsqueeze(2).broadcast_to([P, HEADS, 64]), ALU.mult).then_inc(s_on[l], 1)

                for a, it in enumerate(att[l]):
                    w = it["nb"] * P
                    dve.wait_ge(s_s[l], a + 1)
                    mx, nm = st[:, 5, a:a + 1], st[:, 0, a:a + 1]
                    own.do(dve.tensor_reduce(mx, ps[:, a % 2, 0:w], AXX, ALU.max))
                    if it["sink"]:
                        ts(nm, mx, -it["sc"], nsink[:, it["h"]:it["h"] + 1], ALU.mult, ALU.min).then_inc(s_nm[l], 1)
                    else:
                        ts(nm, mx, -it["sc"], None, ALU.mult).then_inc(s_nm[l], 1)
                    if a % 8 == 7 and it["sink"]:
                        dve.wait_ge(s_nm[l], a + 1)
                        sink_terms(a // 8)
                    if a % 8 == 1 and a > 8:
                        normalise(a // 8 - 1)
                normalise(len(att[l]) // 8 - 1)
                if l == 0:
                    modulation(1)

            def output(l):
                for m in range(KC):
                    dve.wait_ge(s_wo, wo_base[l] + m + 1)
                    for st in range(nq_cols[l] // X):
                        c = slice(st * X, st * X + X)
                        last = stt(out=xt[:, m, c], in0=ps[:, m % 3, c], scalar=mod[:, l, 16 + m, st:st + 1],
                                   in1=xt[:, m, c], op0=ALU.mult, op1=ALU.add)
                    last.then_inc(s_xt, 1)

            def decays():
                m = m1
                for h in range(4):
                    dve.wait_ge(s_ex, h + 1)
                    for b, name in enumerate(("mf", "mb")):
                        last = tt(m["de"][:, b, 0:512], m["de"][:, b, 0:512], tab(1, name), ALU.mult)
                        own.inc(last)
                    own.wait()
                    own.do(tt(m["dt"][:, h, :, :].rearrange("p a b -> p (a b)"), m["de"][:, 0, :], m["de"][:, 1, :], ALU.add))
                    dth = m["dt"][:, h, :, :].rearrange("p a b -> p (a b)")
                    ts(dth, dth, HD ** -0.5, None, ALU.mult).then_inc(s_dt, 1)

            def retention():
                m = m1
                dve.wait_ge(s_dt, 4)
                for h in range(4):
                    dve.wait_ge(s_rs, h + 1)
                    if h >= 2:
                        dve.wait_ge(s_ro, h - 1)
                    b = 2 * (h % 2)
                    tt(m["sd"][:, h % 2, :, :].rearrange("p a b -> p (a b)"),
                       ps[:, b:b + 2, :].rearrange("p a b -> p (a b)"),
                       m["dt"][:, h, :, :].rearrange("p a b -> p (a b)"), ALU.mult).then_inc(s_rd, 1)
                orr = m["orr"].rearrange("p h t -> p (h t)")
                dve.wait_ge(s_mu, 1)
                stt(out=orr, in0=ps[:, 0:2, :].rearrange("p a b -> p (a b)"), scalar=-1.0 / P, in1=orr,
                    op0=ALU.mult, op1=ALU.add).then_inc(s_oc, 1)
                dve.wait_ge(s_osq, 2)
                own.do(dve.reciprocal(m["ort"], m["ort"]))
                own.do(tt(orr, orr, m["ort"], ALU.mult))
                for h in range(4):
                    last = stt(out=m["oa"][:, h, :], in0=m["orr"][:, h, :], scalar=pcol("gn", h),
                               in1=m["sg"][:, h, :], op0=ALU.mult, op1=ALU.mult)
                    if h < 3:
                        own.inc(last)
                last.then_inc(s_yr, 1)

            def topk(l):
                v, f, bv, cd, eq, g3 = tk["v"], tk["if"], tk["bv"], tk["cd"], tk["eq"], tk["g"]
                for t in range(tiles[l]):
                    n = tile_base[l] + t
                    sc = sc_view(t % 2)
                    dve.wait_ge(s_sce, 4 * (n + 1))
                    for half in range(2):
                        s8 = slice(8 * half, 8 * half + 8)
                        for hp in range(16):
                            own.inc(dve.max(v[:, hp, s8], sc[:, hp, :]))
                        own.wait()
                        for hp in range(16):
                            own.inc(dve.max_index(iu[:, hp, s8], v[:, hp, s8], sc[:, hp, :]))
                        own.wait()
                        if half == 0:
                            for hp in range(16):
                                own.inc(dve.match_replace(sc[:, hp, :], v[:, hp, s8], sc[:, hp, :], LOWEST))
                            own.wait()
                    own.inc(dve.tensor_copy(f, iu))
                    vv = v.rearrange("p (h two) a -> p h two a", two=2)
                    own.do(tt(cd.rearrange("p h (a b) -> p h a b", a=16),
                              vv[:, :, 0, :].unsqueeze(3).broadcast_to([P, HEADS, 16, 16]),
                              vv[:, :, 1, :].unsqueeze(2).broadcast_to([P, HEADS, 16, 16]), ALU.add))
                    pi = piu[:, 0, :].rearrange("p (h k) -> p h k", h=HEADS)
                    for half in range(2):
                        s8 = slice(8 * half, 8 * half + 8)
                        for h in range(HEADS):
                            own.inc(dve.max(bv[:, h, s8], cd[:, h, :]))
                        own.wait()
                        for h in range(HEADS):
                            own.inc(dve.max_index(pi[:, h, s8], bv[:, h, s8], cd[:, h, :]))
                        own.wait()
                        if half == 0:
                            for h in range(HEADS):
                                own.inc(dve.match_replace(cd[:, h, :], bv[:, h, s8], cd[:, h, :], LOWEST))
                            own.wait()
                    mx = tk["sm"][:, 0, :]
                    own.do(dve.tensor_copy(mx, bv[:, :, 0]))
                    tt(bv, bv, mx.unsqueeze(2).broadcast_to([P, HEADS, 16]), ALU.subtract).then_inc(s_best, 1)
                    own.inc(ts(piu[:, 1, :], piu[:, 0, :], 4, None, ALU.logical_shift_right))
                    own.do(ts(piu[:, 2, :], piu[:, 0, :], 15, None, ALU.bitwise_and))
                    own.do(dve.tensor_copy(tk["pf"], piu[:, 1:3, :]))
                    if t >= 2:
                        dve.wait_ge(s_tt, n - 1)
                    ff = f.rearrange("p (h two) a -> p h two a", two=2)
                    for half in range(2):
                        own.do(tt(eq, tk["pf"][:, half, :].unsqueeze(2).broadcast_to([P, P, 16]),
                                  iota[:, 0:16].unsqueeze(1).broadcast_to([P, P, 16]), ALU.is_equal))
                        e4 = eq.rearrange("p (h k) a -> p h k a", h=HEADS)
                        own.do(tt(e4, e4, ff[:, :, half, :].unsqueeze(2).broadcast_to([P, HEADS, 16, 16]), ALU.mult))
                        own.do(dve.tensor_reduce(g3[:, t % 2, 1 + half, :], eq, AXX, ALU.add))
                    dve.wait_ge(s_bexp, n + 1)
                    own.do(dve.tensor_reduce(mx, bv, AXX, ALU.add))
                    own.do(dve.reciprocal(tk["sm"][:, 1, :], mx))
                    tt(g3[:, t % 2, 0, :].rearrange("p (h k) -> p h k", h=HEADS), bv,
                       tk["sm"][:, 1, :].unsqueeze(2).broadcast_to([P, HEADS, 16]), ALU.mult).then_inc(s_tk, 1)
                    dve.wait_ge(s_tk, n + 1)
                    if l == 0:
                        modulation(2 + t)

            def one_hots(n):
                l, g = groups[n]
                dve.wait_ge(s_hh, n + 1)
                tt(hl[:, :, :], ht[:, g, :, :], hh[:, :, :].bitcast(F32), ALU.subtract).then_inc(s_hl, 1)
                dve.wait_ge(s_sel, tile_base[l] + tiles[l])
                if n >= 1:
                    dve.wait_ge(s_y, 2 * P * n)

                def steps(i, first):
                    for j in range(2):
                        if not first:
                            dve.wait_ge(s_g, i * 2 + (64 * n + j - 1))
                        for t in range(4):
                            at = i * 8 + (g * GRP + 4 * j + t)
                            col = slice(at, at + 1) if isinstance(at, int) else bass.ds(at, 1)
                            ts(oha[:, j, t, :], iota, sel[:, 1, col], sel[:, 0, col], ALU.is_equal, ALU.mult)
                            last = ts(ohb[:, j, t, :], iota, sel2[:, col], None, ALU.is_equal)
                        last.then_inc(s_oh, 1)

                steps(0, True)
                with dve.Fori(1, 32) as i:
                    steps(i, False)

            def experts(n):
                dve.wait_ge(s_g, 64 * (n + 1))
                dve.wait_ge(s_ge, 64 * (n + 1))

                def low(dst, raw, high, sem):
                    tt(dst, raw, high.bitcast(F32), ALU.subtract).then_inc(sem, 1)

                def up_part(i, j):
                    for half in range(2):
                        c = slice(half * 512, half * 512 + 512)
                        dve.wait_ge(s_uh, i * 4 + (2 * P * n + 2 * j + half + 1))
                        low(ul[:, c], ring[:, 2 * j, c], uh[:, c], s_ul)

                def down_part(i, j):
                    for half in range(2):
                        c = slice(half * 512, half * 512 + 512)
                        dve.wait_ge(s_vh, i * 4 + (2 * P * n + 2 * j + half + 1))
                        low(vl[:, c], ring[:, 2 * j + 1, c], vh[:, c], s_vl)

                def weigh(i, j):
                    at = i * 2 + j
                    g = gates[:, at, :] if isinstance(at, int) else gates[:, bass.ds(at, 1), :].rearrange("p a t -> p (a t)")
                    dve.wait_ge(s_gel, i * 2 + (P * n + j + 1))
                    tt(gel[:, j, :], gel[:, j, :], g, ALU.mult).then_inc(s_w, 1)
                    dve.wait_ge(s_wh, i * 2 + (P * n + j + 1))
                    low(wl[:, j, :], gel[:, j, :], wh[:, j, :], s_wl)

                def both(i, j, last):
                    if not last:
                        up_part(i + j, 1 - j)
                    weigh(i, j)
                    down_part(i, j)

                up_part(0, 0)
                both(0, 0, False)
                both(0, 1, False)
                with dve.Fori(1, P // 2 - 1) as i:
                    both(i, 0, False)
                    both(i, 1, False)
                both(P // 2 - 1, 0, False)
                both(P // 2 - 1, 1, True)
                dve.wait_ge(s_rel, 16 * [1, 3, 4][n])
                l, g = groups[n]
                c = slice(g * GRP, g * GRP + GRP)
                for m in range(KC):
                    dve.wait_ge(s_yt, KC * n + m + 1)
                    stt(out=xt[:, m, c], in0=ps[:, 4 + m % 2, 0:GRP], scalar=mod[:, l, 40 + m, g:g + 1],
                        in1=xt[:, m, c], op0=ALU.mult, op1=ALU.add).then_inc(s_xt, 1)

            dve.wait_ge(s_par, 32)
            own.inc(ts(nsink[:, :], pcol("sink", 0, 8), -1.0, None, ALU.mult))
            modulation(0)
            norm(0)
            projections(0)
            attention(0)
            output(0)
            norm(1)
            topk(0)
            for n in range(2):
                one_hots(n)
                experts(n)
            norm(2)
            decays()
            projections(1)
            retention()
            attention(1)
            output(1)
            norm(3)
            topk(1)
            one_hots(2)
            experts(2)


def _chunks(w, cols):
    w = w[:, cols]
    k = w.shape[0] // P
    return np.ascontiguousarray(w.reshape(k, P, -1, P).transpose(2, 1, 0, 3))


def _rope_tables(head, start, half, rows):
    cos = np.ones((rows, T), np.float32)
    sin = np.zeros((rows, T), np.float32)
    rot = np.zeros((P, P), np.float32)
    t = np.arange(X)
    posn = [t // GRID_W, t % GRID_W]
    fr = (np.float32(10000.0) ** (-np.arange(half, dtype=np.float32) / np.float32(half))).astype(np.float32)
    for r in range(rows):
        f = r % head - start
        if f < 0:
            continue
        ang = posn[f // (2 * half)].astype(np.float32) * fr[f % half]
        low = f % (2 * half) < half
        cos[r, :X] = np.cos(ang)
        sin[r, :X] = -np.sin(ang) if low else np.sin(ang)
        rot[r + half if low else r - half, r] = 1.0
    return cos, sin, rot


def _tables():
    ca, sa, ra = _rope_tables(64, 0, 16, P)
    cb, sb_, rb = _rope_tables(P, 64, 8, 96)
    pad = ((0, 32), (0, 0))
    cb, sb_ = np.pad(cb, pad), np.pad(sb_, pad)
    i = np.arange(P)
    bo64 = (i[:, None] // 64 == i[None] // 64).astype(np.float32)
    ones = np.ones((P, P), np.float32)
    m01 = np.where(i[None] <= i[:, None], 0.0, NEG).astype(np.float32)
    m10 = np.where(i[None] >= i[:, None], 0.0, NEG).astype(np.float32)
    tab0 = dict(cosA=ca, sinA=sa, bo64=bo64, rot64=ra, ones=ones, cosB=cb, sinB=sb_, bo96=ones, rot96=rb,
                m01=m01, m10=m10)
    q = np.arange(X)[None]
    df, db = np.zeros((P, 4, X), np.float32), np.zeros((P, 4, X), np.float32)
    mf, mb = np.zeros((P, 2, X), np.float32), np.zeros((P, 2, X), np.float32)
    for kt in range(4):
        j = (kt % 2) * P + i[:, None]
        if kt < 2:
            df[:, kt] = db[:, kt] = np.abs(q - j)
            mf[:, kt], mb[:, kt] = j <= q, j >= q
        else:
            df[:, kt], db[:, kt] = X + q - j, X - q + j
    tab1 = dict(cosA=ca, sinA=sa, bo64=bo64, rot64=ra, ones=ones, df=df, db=db, mf=mf, mb=mb)
    return [np.concatenate([d[n].reshape(P, -1) for n in TAB[l]], axis=1) for l, d in enumerate((tab0, tab1))]


def kernel(x, c, ctx, c_ctx, ada_w, ada_b, norm1_w, norm2_w, ab_w_in, ab_w_o, a_q_norm, a_k_norm,
           a_sink, b_q_lora_norm, b_kv_lora_norm, b_w_uq, b_w_ukv, b_q_norm, b_k_norm, cd_w_in, cd_w_o,
           c_decay_fwd, c_decay_bwd, c_gn_w, d_q_norm, d_k_norm, peer_w_q, peer_keys, peer_u, peer_v):
    import concourse.bacc as _bacc
    from concourse.bass_utils import run_bass_kernel_spmd as _run

    f = np.asarray
    a = {}
    tokens = np.concatenate([f(x)[0], f(ctx)[0]], axis=0)
    a["x"] = tokens.reshape(T, KC, P).transpose(2, 1, 0)
    a["ada"] = f(ada_w).reshape(2, 4, 2, P, BLOCKS, 512).transpose(0, 4, 1, 3, 2, 5)
    r = np.arange
    pairs = np.concatenate([np.concatenate([r(j * 64, j * 64 + 64), r((j + 4) * 64, (j + 4) * 64 + 64)])
                            for j in range(4)])
    w = f(ab_w_in)[0]
    a["w0"] = _chunks(w, np.concatenate([pairs, r(512, 640), r(768, 1280), r(640, 768)]))
    a["kr"] = w[:, 1280:1312].reshape(1, KC, P, 32).transpose(0, 2, 1, 3)
    a["uq"] = f(b_w_uq)[0].reshape(2, P, 2, 384).transpose(2, 1, 0, 3)
    kv = f(b_w_ukv)[0].reshape(2, P, 8, 2, 64)
    a["ukvk"] = kv[:, :, :, 0].reshape(1, 2, P, 512).transpose(0, 2, 1, 3)
    a["ukvv"] = kv[:, :, :, 1].reshape(1, 2, P, 512).transpose(0, 2, 1, 3)
    w1 = f(cd_w_in)[0]
    a["w1"] = _chunks(w1, np.concatenate([r(0, 512), 1536 + pairs, r(2048, 2176), r(2176, 2304), r(1024, 1536)]))
    a["vr"] = w1[:, 512:1024].reshape(4, 2, P, 512).transpose(0, 2, 1, 3)
    every = r(D)
    a["wo"] = np.stack([_chunks(f(ab_w_o)[0], every),
                        _chunks(f(cd_w_o)[0], every)])
    a["wq"] = f(peer_w_q).reshape(2, KC, P, 16, P).transpose(0, 3, 2, 1, 4)
    a["keys"] = f(peer_keys).reshape(2, 16, P, P).transpose(0, 3, 1, 2)
    a["ut"] = f(peer_u).reshape(2, P, P, KC, P).transpose(0, 2, 4, 3, 1)
    a["vt"] = f(peer_v).reshape(2, P, P, D).transpose(0, 2, 1, 3)
    tab0, tab1 = _tables()
    a["tab0"], a["tab1"] = tab0, tab1
    a["cst"] = np.stack([np.eye(P, dtype=np.float32),
                         np.tile(np.arange(P, dtype=np.float32), (P, 1))], axis=1)

    def cols(v):
        return f(v).reshape(-1, P).T

    def head(v):
        v = f(v).reshape(-1)
        return np.concatenate([v, v])[:, None] if v.size == 64 else np.pad(v, (0, P - v.size))[:, None]

    def wide(v):
        return np.tile(f(v).reshape(1, -1), (P, 1))

    cc = np.stack([cols(c), cols(c_ctx)], axis=2).reshape(P, 16)
    a["par"] = np.concatenate([
        cols(norm1_w), cols(norm2_w), cols(ada_b), head(a_q_norm), head(a_k_norm), cols(b_q_lora_norm),
        cols(b_kv_lora_norm), head(b_q_norm), head(b_k_norm), cols(c_gn_w), head(d_q_norm), head(d_k_norm),
        cc, wide(a_sink), wide(c_decay_fwd), wide(c_decay_bwd),
        np.full((P, 1), EPS, np.float32), np.ones((P, 1), np.float32)], axis=1)
    assert a["par"].shape[1] == NPR

    nc = _bacc.Bacc("TRN2", target_bir_lowering=False, num_devices=1)
    arrays, aps = {}, {}
    for name, v in a.items():
        v = np.ascontiguousarray(v)
        arrays["in_" + name] = v
        aps[name] = nc.dram_tensor("in_" + name, v.shape, F32, kind="ExternalInput").ap()
    out = nc.dram_tensor("out", (P, KC, X), F32, kind="ExternalOutput").ap()
    build(nc, aps, out)
    got = _run(nc, [arrays], core_ids=[0]).results[0]["out"]
    return np.ascontiguousarray(got.transpose(2, 1, 0).reshape(1, X, D))
```

```python
from contextlib import ExitStack

import numpy as np
import concourse.bass as bass
from concourse import mybir

F32 = mybir.dt.float32
F32R = mybir.dt.float32r
BF16 = mybir.dt.bfloat16
U32 = mybir.dt.uint32
ACT = mybir.ActivationFunctionType
ALU = mybir.AluOpType
AXX = mybir.AxisListType.X

P = 128
D = 1024
KC = D // P
X = 256
T = 512
GRID_W = 64
HD = 64
EPS = 1e-6
NEG = -1e30
LOWEST = -3.0e38
HEADS = 8
NSEL = 128
SLOTS = 4
GRP = 256
GRP_TILES = GRP // P
MODS = 6 * KC
BLOCKS = MODS // 4

PR = {}
_at = 0
for _name, _n in (("n1", 16), ("n2", 16), ("ada_b", 96), ("aq", 1), ("ak", 1), ("bql", 2), ("bkvl", 2),
                  ("bq", 1), ("bk", 1), ("gn", 4), ("dq", 1), ("dk", 1), ("c", 16), ("sink", 8),
                  ("decf", 4), ("decb", 4), ("eps", 1), ("one", 1)):
    PR[_name] = _at
    _at += _n
NPR = _at

TAB = [{}, {}]
TABW = [0, 0]
for _l, _spec in enumerate(((("cosA", 512), ("sinA", 512), ("bo64", 128), ("rot64", 128), ("ones", 128),
                             ("cosB", 512), ("sinB", 512), ("bo96", 128), ("rot96", 128),
                             ("m01", 128), ("m10", 128)),
                            (("cosA", 512), ("sinA", 512), ("bo64", 128), ("rot64", 128), ("ones", 128),
                             ("df", 1024), ("db", 1024), ("mf", 512), ("mb", 512)))):
    for _name, _n in _spec:
        TAB[_l][_name] = (TABW[_l], _n)
        TABW[_l] += _n


class Step:

    def __init__(self, eng, sem):
        self.eng, self.sem, self.n = eng, sem, 0

    def inc(self, ins):
        ins.then_inc(self.sem, 1)
        self.n = self.n + 1

    def wait(self):
        self.eng.wait_ge(self.sem, self.n)

    def wait_upto(self, n):
        self.eng.wait_ge(self.sem, n)

    def do(self, ins):
        self.inc(ins)
        self.wait()


def build(nc, A, out):
    with ExitStack() as ctx:
        def sb(name, shape, dt=F32):
            return ctx.enter_context(nc.sbuf_tensor(name, shape, dt))

        def sem(name):
            return ctx.enter_context(nc.semaphore(name))

        sel = sb("sel", [P, T])
        selk = sb("selk", [P, 2, T], BF16)
        iob = sb("iob", [P, P, 4], BF16)
        scr = sb("scr", [P, 2048])
        cst = sb("cst", [P, 2, P])
        par = sb("par", [P, NPR])
        cs = sb("cs", [P, KC, 2])
        mod = sb("mod", [P, 2, MODS, 2])
        gain = sb("gain", [P, 4, KC, 2])
        nsink = sb("nsink", [P, HEADS])
        hh = sb("hh", [P, KC, GRP], F32R)
        hl = sb("hl", [P, KC, GRP], F32R)
        uh = sb("uh", [P, D], F32R)
        ul = sb("ul", [P, D], F32R)
        vh = sb("vh", [P, D], F32R)
        vl = sb("vl", [P, D], F32R)
        wh = sb("wh", [P, 2, GRP], F32R)
        wl = sb("wl", [P, 2, GRP], F32R)
        ident, iota = cst[:, 0, :], cst[:, 1, :]
        ohb = scr[:, 1024:2048].rearrange("p (b t n) -> p b t n", b=2, t=4)
        gel = scr[:, 0:512].rearrange("p (b t) -> p b t", b=2)
        rows = scr[0:2, 0:1024].rearrange("p (b n) -> p b n", b=2)
        HT0, G0 = SLOTS * D, SLOTS * D + KC * X
        XT0 = HT0 + KC * T
        AR0 = XT0 + KC * T
        OH0 = G0 + P * GRP
        ROOM = OH0 + 2 * D // 2
        room = sb("room", [P, ROOM])
        ring = room[:, 0:HT0].rearrange("p (s n) -> p s n", s=SLOTS)
        oha = [v.rearrange("p (t n) -> p t n", t=4)
               for v in (scr[:, 0:512], ring[:, 3, 0:512], scr[:, 512:1024], ring[:, 3, 512:1024])]
        ht = room[:, HT0:XT0].rearrange("p (s k t) -> p s k t", s=2, k=KC)
        xt = room[:, XT0:AR0].rearrange("p (k t) -> p k t", k=KC)
        gates = room[:, G0:G0 + P * GRP].rearrange("p (i t) -> p i t", t=GRP)
        eqb = room[:, OH0:ROOM].bitcast(BF16).rearrange("p (b w n t) -> p b w n t", b=2, w=2, t=4)
        arena = room[:, AR0:ROOM]
        ASIZE = ROOM - AR0
        ps = ctx.enter_context(nc.psum_tensor("ps", [P, 8, 512], F32))
        xt_dram = nc.dram_tensor("xt_wait", (P, KC, T), F32).ap()

        def carve(spec):
            at, got = 0, {}
            for name, dims in spec:
                n = int(np.prod(dims))
                v = arena[:, at:at + n]
                if len(dims) == 2:
                    v = v.rearrange("p (a b) -> p a b", a=dims[0])
                if len(dims) == 3:
                    v = v.rearrange("p (a b c) -> p a b c", a=dims[0], b=dims[1])
                got[name] = v
                at += n
            assert at <= ASIZE, at
            return got

        common = [("nrt", (T,)), ("zw", (2, T)), ("zsq", (2, T)), ("rt", (2, T)),
                  ("ri", (T,)), ("ta", (T,)), ("tb", (T,)), ("st", (6, 64)), ("on", (2, T))]
        m0 = carve(common + [("tab", (TABW[0],)), ("qa", (4, T)), ("ka", (T,)), ("va", (4, P)), ("qb", (8, T)), ("kb", (8, T)),
                             ("vb", (4, T)), ("oa", (8, T))])
        m1 = carve(common + [("tab", (TABW[1],)), ("qr", (2, X)), ("kr", (2, T)), ("qd", (4, X)), ("kd", (T,)), ("vr", (4, T)),
                             ("vd", (4, P)), ("sg", (4, X)), ("oa", (8, X)), ("dt", (4, 4, X)),
                             ("ret", (3 * 4 * X,)), ("lg", (16,))])
        ret = m1["ret"]
        m1["de"] = ret[:, 0:8 * X].rearrange("p (b t) -> p b t", b=2)
        m1["sd"] = ret[:, 4 * X:12 * X].rearrange("p (b k t) -> p b k t", b=2, k=4)
        m1["orr"] = ret[:, 0:4 * X].rearrange("p (h t) -> p h t", h=4)
        m1["osq"] = ret[:, 4 * X:8 * X].rearrange("p (h t) -> p h t", h=4)
        m1["ort"] = ret[:, 8 * X:12 * X]
        tk = carve([("qt", (3, T)), ("sc", (4, 16, P)), ("cd", (4, 256)), ("eq", (P, 8)),
                    ("v", (4, 16, 16)), ("i", (4, 16, 16)), ("if", (4, 16, 8)), ("bv", (4, HEADS, 16)),
                    ("pi", (4, P)), ("pm", (2, P)), ("pf", (2, P // 2)),
                    ("g", (2, 3, P)), ("mx", (32,)), ("rs", (32,)), ("keys", (16, P))])
        keys = tk["keys"]
        iu = tk["i"].bitcast(U32)
        piu = tk["pi"].bitcast(U32)
        pmu = tk["pm"].bitcast(U32)
        ifb = tk["if"].rearrange("p t h a -> p (t h a)").bitcast(BF16).rearrange("p (w t a h) -> p w t a h", w=2, t=4, a=16)
        pfb = tk["pf"].rearrange("p a b -> p (a b)").bitcast(BF16).rearrange("p (a b) -> p a b", a=2)
        eqk = tk["eq"].rearrange("p a b -> p (a b)").bitcast(BF16).rearrange("p (a s) -> p a s", a=16)
        mix = [m0, m1]
        for m in mix:
            m["sq8"], m["nt"], m["nrb"] = m["zsq"], m["zw"], m["ta"]
            m["pr"], m["pts"] = m["zw"], m["zsq"]
        m0["lq"], m0["lkv"], m0["zk"], m0["zks"] = (m0["oa"][:, 2 * i:2 * i + 2, :] for i in range(4))

        def tab(l, name):
            a, n = TAB[l][name]
            return mix[l]["tab"][:, a:a + n]

        def pcol(name, i=0, n=1, rows=slice(0, P)):
            return par[rows, PR[name] + i:PR[name] + i + n]

        s_par = sem("s_par")
        s_x = sem("s_x")
        s_tab = [sem(f"s_tab{l}") for l in range(2)]
        s_key = sem("s_key")
        s_slot = [sem(f"s_slot{i}") for i in range(SLOTS)]
        s_cs = sem("s_cs")
        s_ada = sem("s_ada")
        s_adr = sem("s_adr")
        s_adt = sem("s_adt")
        s_mod = sem("s_mod")
        s_nsq = sem("s_nsq")
        s_nss = sem("s_nss")
        s_nrt = sem("s_nrt")
        s_nt = sem("s_nt")
        s_nh = sem("s_nh")
        s_xt = sem("s_xt")
        s_z = [sem(f"s_z{l}") for l in range(2)]
        s_zw = [sem(f"s_zw{l}") for l in range(2)]
        s_rx = [sem(f"s_rx{l}") for l in range(2)]
        s_rt = [sem(f"s_rt{l}") for l in range(2)]
        s_it = [sem(f"s_it{l}") for l in range(2)]
        s_s = [sem(f"s_s{l}") for l in range(2)]
        s_nm = [sem(f"s_nm{l}") for l in range(2)]
        s_p = [sem(f"s_p{l}") for l in range(2)]
        s_pt = [sem(f"s_pt{l}") for l in range(2)]
        s_pe = [sem(f"s_pe{l}") for l in range(2)]
        s_pv = [sem(f"s_pv{l}") for l in range(2)]
        s_se = sem("s_se")
        s_es = sem("s_es")
        s_on = [sem(f"s_on{l}") for l in range(2)]
        s_ot = [sem(f"s_ot{l}") for l in range(2)]
        s_oe = [sem(f"s_oe{l}") for l in range(2)]
        s_wo = sem("s_wo")
        s_q = sem("s_q")
        s_qe = sem("s_qe")
        s_sc = sem("s_sc")
        s_sce = sem("s_sce")
        s_best = sem("s_best")
        s_bexp = sem("s_bexp")
        s_tk = sem("s_tk")
        s_tt = sem("s_tt")
        s_sel = sem("s_sel")
        s_oh = sem("s_oh")
        s_gwd = sem("s_gwd")
        s_gwp = sem("s_gwp")
        s_ob = sem("s_ob")
        s_g = sem("s_g")
        s_ge = sem("s_ge")
        s_spill = sem("s_spill")
        s_rel = sem("s_rel")
        s_hh = sem("s_hh")
        s_hl = sem("s_hl")
        s_uh = sem("s_uh")
        s_ul = sem("s_ul")
        s_vh = sem("s_vh")
        s_vl = sem("s_vl")
        s_a = sem("s_a")
        s_gel = sem("s_gel")
        s_w = sem("s_w")
        s_wh = sem("s_wh")
        s_wl = sem("s_wl")
        s_y = sem("s_y")
        s_ye = sem("s_ye")
        s_yt = sem("s_yt")
        s_ex = sem("s_ex")
        s_dt = sem("s_dt")
        s_rs = sem("s_rs")
        s_rd = sem("s_rd")
        s_ro = sem("s_ro")
        s_roe = sem("s_roe")
        s_mu = sem("s_mu")
        s_oc = sem("s_oc")
        s_osq = sem("s_osq")
        s_yr = sem("s_yr")
        s_out = sem("s_out")
        s_act = sem("s_act")
        s_dve = sem("s_dve")

        def norm_bank(n):
            return 6 if n else 5

        loads, freed, first_use, last_use = [], {}, {}, {}
        stage = [0]

        def load(key, src, freed_by, used=None):
            at = (stage[0], len(loads))
            first_use[key], last_use[key] = used or (at, at)
            loads.append((key, src))
            freed[key] = freed_by

        blocks = [(l, b) for l in range(2) for b in range(BLOCKS)]
        sets = [range(0, 4), range(4, 10), range(10, 14), range(14, 17), range(17, 20), range(20, 24)]
        after_query = {2: 10, 5: 11, 8: 12, 11: 13}
        LOWRANK = 11
        in_items = {}
        for b, q in enumerate(sets[1]):
            for at, ks in enumerate((range(0, 3), range(3, 6), range(6, 8))):
                in_items[LOWRANK + 3 * b + at] = (q, ks)

        def load_ada(qs):
            for q in qs:
                l, b = blocks[q]
                for kk in range(4):
                    load(("ada", q, kk), A["ada"][l, b, kk].rearrange("p k m -> p (k m)"), (s_ada, 4 * q + kk + 1))

        def hk(k, a=0, b=T):
            if b - a == T:
                return ht[:, :, k, :]
            return ht[:, a // X, k, a % X:a % X + b - a]

        def item(kind, groups, rows=slice(0, P), n=T, **kw):
            return dict(kind=kind, groups=groups, rows=rows, n=n, **kw)

        def feat(key, rows=slice(0, P), cols=slice(0, P), n=T, w=P):
            return (rows, slice(0, n), [(key, (k, w, cols), hk(k, 0, n)) for k in range(KC)])

        items0 = []
        for j in range(4):
            items0.append(item("rope", [feat(("w0", j))], w=pcol("aq"), dest=m0["qa"][:, j, :], tb="A"))
        items0.append(item("rope", [feat(("w0", 4))], w=pcol("ak"), dest=m0["ka"], tb="A"))
        for name, c0, dst in (("bql", 5, "lq"), ("bkvl", 7, "lkv")):
            items0.append(item("lora0", [feat(("w0", c0))], w=pcol(name, 0), dest=m0[dst]))
            items0.append(item("lora1", [feat(("w0", c0 + 1))], w=pcol(name, 1), dest=m0[dst]))
        items0.append(item("kr", [feat(("kr", 0), rows=slice(64, 96), cols=slice(0, 32), w=32)],
                           rows=slice(64, 96), w=pcol("bk", rows=slice(64, 96))))
        items0.append(item("plain", [(slice(0, P), slice(t * P, t * P + P),
                                      [(("w0", 9), (k, P, None), hk(k, t * P, t * P + P)) for k in range(KC)])
                                     for t in range(4)], dest=m0["va"].rearrange("p a b -> p (a b)")))
        for h in range(HEADS):
            items0.append(item("rope", [(slice(0, 96), slice(0, T),
                                         [(("uq", h // 4), (k, 384, slice((h % 4) * 96, (h % 4) * 96 + 96)),
                                           m0["lq"][:, k, :]) for k in range(2)])],
                               rows=slice(0, 96), w=pcol("bq", rows=slice(0, 96)), dest=m0["qb"][0:96, h, :], tb="B"))
        for h in range(HEADS):
            items0.append(item("ropek", [(slice(0, 64), slice(0, T),
                                          [(("ukvk", 0), (k, 512, slice(h * 64, h * 64 + 64)), m0["lkv"][:, k, :])
                                           for k in range(2)])],
                               rows=slice(0, 96), w=pcol("bk", rows=slice(0, 64)), dest=m0["kb"][0:96, h, :], tb="B"))
        for t in range(4):
            items0.append(item("plain", [(slice(0, P), slice(0, T),
                                          [(("ukvv", 0), (k, 512, None), m0["lkv"][:, k, t * P:t * P + P])
                                           for k in range(2)])], dest=m0["vb"][:, t, :]))
        items1 = []
        for j in range(4):
            items1.append(item("rope", [feat(("w1", 4 + j), n=X)], n=X, w=pcol("dq"), dest=m1["qd"][:, j, :], tb="A"))
        items1.append(item("rope", [feat(("w1", 8))], w=pcol("dk"), dest=m1["kd"], tb="A"))
        for j in range(2):
            items1.append(item("rope0", [feat(("w1", j), n=X)], n=X, w=pcol("one"), dest=m1["qr"][:, j, :], tb="A"))
        for j in range(2):
            items1.append(item("rope0", [feat(("w1", 2 + j))], w=pcol("one"), dest=m1["kr"][:, j, :], tb="A"))
        items1.append(item("plain", [(slice(0, P), slice(t * P, t * P + P),
                                      [(("w1", 9), (k, P, None), hk(k, t * P, t * P + P)) for k in range(KC)])
                                     for t in range(4)], dest=m1["vd"].rearrange("p a b -> p (a b)")))
        for t in range(4):
            items1.append(item("plain", [(slice(0, P), slice(0, T),
                                          [(("vr", k // 2), (k % 2, 512, None), hk(k, t * P, t * P + P))
                                           for k in range(KC)])], dest=m1["vr"][:, t, :]))
        for j in range(4):
            items1.append(item("silu", [feat(("w1", 10 + j), n=X)], n=X, dest=m1["sg"][:, j, :]))
        items = [items0, items1]

        def has_rx(it):
            return it["kind"] in ("rope", "ropek", "rope0", "lora1")

        def has_norm(it):
            return it["kind"] in ("rope", "ropek", "lora1")

        rx_upto = [[sum(has_rx(i) for i in its[:c + 1]) for c in range(len(its))] for its in items]
        rt_upto = [[sum(has_norm(i) for i in its[:c + 1]) for c in range(len(its))] for its in items]

        def load_items(l):
            last = {}
            for c, it in enumerate(items[l]):
                for _, _, mms in it["groups"]:
                    for key, _, _ in mms:
                        last[key] = c
            seen = set()
            stage[0] += 1
            for c, it in enumerate(items[l]):
                for _, _, mms in it["groups"]:
                    for key, _, _ in mms:
                        if key not in seen:
                            seen.add(key)
                            s = A[key[0]][key[1]].rearrange("p k m -> p (k m)")
                            load(key, s, (s_z[l], last[key] + 1), ((stage[0], c), (stage[0], last[key])))
                if l == 0 and c - 1 in in_items:
                    q, ks = in_items[c - 1]
                    for k in ks:
                        if ("ada", q, k // 2) not in seen:
                            seen.add(("ada", q, k // 2))
                            until = max(i for i in in_items if in_items[i][0] == q and
                                        (k // 2 * 2 in in_items[i][1] or k // 2 * 2 + 1 in in_items[i][1]))
                            load(("ada", q, k // 2), A["ada"][blocks[q][0], blocks[q][1], k // 2].rearrange(
                                "p k m -> p (k m)"), (s_ada, 4 * q + k // 2 + 1),
                                ((stage[0], c + 0.5), (stage[0], until + 1.5)))
            stage[0] += 1

        def heads(l):
            m, got = mix[l], []
            for kind in ("A", "B") if l == 0 else ("A",):
                for qt in range(4 if l == 0 else 2):
                    for h in range(HEADS):
                        ks, blk = (slice(0, T), range(4)) if qt < 2 else (slice(X, T), range(2, 4))
                        if kind == "A":
                            j, po = h % 4, 64 * (h // 4)
                            r = slice(po, po + 64)
                            qn, kn, vn = ("qa", "ka", "va") if l == 0 else ("qd", "kd", "vd")
                            q, k = m[qn][r, j, qt * P:qt * P + P], m[kn][r, ks]
                            v = [m[vn][:, b, po:po + 64] for b in blk]
                            sc = HD ** -0.5
                        else:
                            q, k = m["qb"][0:96, h, qt * P:qt * P + P], m["kb"][0:96, h, ks]
                            v = [m["vb"][:, b, h * 64:h * 64 + 64] for b in blk]
                            sc = 96 ** -0.5
                        mask = None
                        if l == 0 and kind == "A" and qt < 2:
                            mask = (1 - qt, tab(0, "m01" if qt == 0 else "m10"))
                        got.append(dict(q=q, k=k, v=v, nb=len(v), mask=mask, sc=float(sc), h=h,
                                        sink=l == 0 and kind == "A",
                                        dest=m["oa"][:, (4 if kind == "B" or l == 1 else 0):
                                                     (8 if kind == "B" or l == 1 else 4), qt * P:qt * P + P]))
            return got

        att = [heads(0), heads(1)]
        nq_cols = [T, X]
        wo_base = [0, 8]
        xt_base = {"wo0": 0, "peer0": 8, "wo1": 24, "peer1": 32}

        def load_wo(l):
            for m in range(KC):
                load(("wo", l, m), A["wo"][l, m].rearrange("p k m -> p (k m)"), (s_wo, wo_base[l] + m + 1))

        tiles = [4, 2]
        tile_base = [0, 4]
        groups = [(0, 1), (0, 0), (1, 0)]

        def load_peer(l):
            for m in range(16):
                load(("wq", l, m), A["wq"][l, m].rearrange("p k m -> p (k m)"), (s_q, 16 * l + m + 1))
                if l == 0 and m in after_query:
                    load_ada([after_query[m]])

        load_ada(sets[0])
        load_items(0)
        load_wo(0)
        load_peer(0)
        for st in sets[3:]:
            load_ada(st)
        loads.append(("experts", 0))
        loads.append(("experts", 1))
        load_items(1)
        load_wo(1)
        load_peer(1)
        loads.append(("experts", 2))
        slot_of, before, owner, count = {}, {}, [None] * SLOTS, [0] * SLOTS
        until = [(-1, s) for s in range(SLOTS)]
        expert_count = {}
        for key, src in loads:
            if key == "experts":
                expert_count[src] = list(count)
                before[("experts", src)] = list(owner)
                for s in range(SLOTS):
                    count[s] += P // 2
                    owner[s] = (s_ul if s % 2 == 0 else s_vl, 2 * (P * src + P - 1 + s // 2))
                continue
            s = min(range(SLOTS), key=lambda i: until[i])
            assert until[s] < first_use[key], key
            slot_of[key] = (s, count[s])
            before[key] = owner[s]
            owner[s] = freed[key]
            until[s] = last_use[key]
            count[s] += 1

        def landed(eng, key):
            slot, n = slot_of[key]
            eng.wait_ge(s_slot[slot], 16 * (n + 1))
            return ring[:, slot, :]

        def tab_dst(l):
            return mix[l]["tab"][:, 0:TABW[l]]

        ys = arena[:, ASIZE - 2 * D:ASIZE].rearrange("p (t d) -> p t d", t=GRP_TILES)
        REUSE = (AR0 - G0 + GRP - 1) // GRP

        def group_xt(n):
            return [xt_base["peer0"], xt_base["peer0"] + KC, xt_base["peer1"]][n]

        block = ctx.enter_context(nc.Block())

        @block.sync
        def _(sp):
            sp.dma_start(cst[:, :, :], A["cst"]).then_inc(s_par, 16)
            sp.dma_start(par[:, :], A["par"]).then_inc(s_par, 16)
            for key, src in loads:
                if key == "experts":
                    n = src
                    l, g = groups[n]

                    def pair_load(i, j, first):
                        c = slice(j, j + 1) if first else bass.ds(i * 2 + j, 1)
                        u = A["ut"][l, c].rearrange("a p k m -> p (a k m)")
                        v = A["vt"][l, c].rearrange("a p d -> p (a d)")
                        for slot, src, parted in ((2 * j, u, s_ul), (2 * j + 1, v, s_vl)):
                            if first:
                                w = before[("experts", n)][slot]
                                sp.wait_ge(w[0], w[1])
                                if slot == 3:
                                    sp.wait_ge(s_g, 64 * (n + 1))
                            else:
                                sp.wait_ge(parted, i * 4 + (2 * P * n + 2 * j - 2))
                            sp.dma_start(ring[:, slot, :], src).then_inc(s_slot[slot], 16)

                    for j in range(2):
                        pair_load(0, j, True)
                    with sp.Fori(1, P // 2) as i:
                        for j in range(2):
                            pair_load(i, j, False)
                    continue
                slot, n = slot_of[key]
                if before[key] is not None:
                    sp.wait_ge(before[key][0], before[key][1])
                sp.dma_start(ring[:, slot, 0:src.shape[-1]], src).then_inc(s_slot[slot], 16)
            sp.wait_ge(s_xt, xt_base["peer1"] + KC)
            sp.dma_start(out, xt[:, :, 0:X]).then_inc(s_out, 16)
            sp.wait_ge(s_out, 16)

        @block.gpsimd
        def _(pool):
            pool.dma_start(xt, A["x"]).then_inc(s_x, 16)
            pool.dma_start(tab_dst(0), A["tab0"]).then_inc(s_tab[0], 16)

            def spill(width):
                pool.dma_start(xt_dram[:, :, 0:width], xt[:, :, 0:width]).then_inc(s_spill, 16)

            def reload(n, half):
                if half == groups[n][1]:
                    pool.wait_ge(s_w, P * n + REUSE)
                c = slice(half * X, half * X + X)
                pool.dma_start(xt[:, :, c], xt_dram[:, :, c]).then_inc(s_rel, 16)

            def gate_odd(n):
                l, g = groups[n]

                def step(i, j, first):
                    at = i * 16 + (g * GRP + 4 * j)
                    cols = slice(at, at + 4) if isinstance(at, int) else bass.ds(at, 4)
                    pool.wait_ge(s_oh, i * 4 + (64 * n + j + 1))
                    if not first:
                        pool.wait_ge(s_g, i * 4 + (64 * n + j - 3))
                    pool.tensor_tensor(oha[j].rearrange("p t n -> p n t"), eqb[:, 1, 0],
                                       sel[:, cols].unsqueeze(1).broadcast_to([P, P, 4]),
                                       ALU.mult).then_inc(s_gwp, 1)

                pool.wait_ge(s_sel, tile_base[l] + tiles[l])
                w = before[("experts", n)][3]
                pool.wait_ge(w[0], w[1])
                step(0, 1, True)
                step(0, 3, True)
                with pool.Fori(1, 16) as i:
                    step(i, 1, False)
                    step(i, 3, False)

            pool.wait_ge(s_xt, xt_base["wo0"] + KC)
            pool.dma_start(keys, A["keys"][0]).then_inc(s_key, 16)
            spill(T)
            pool.wait_ge(s_spill, 16)
            gate_odd(0)
            reload(0, 1)
            pool.wait_ge(s_xt, xt_base["peer0"] + KC)
            pool.dma_start(xt_dram[:, :, X:T], xt[:, :, X:T]).then_inc(s_spill, 16)
            pool.wait_ge(s_spill, 32)
            gate_odd(1)
            reload(1, 0)
            reload(1, 1)
            pool.wait_ge(s_w, 2 * P)
            pool.dma_start(tab_dst(1), A["tab1"]).then_inc(s_tab[1], 16)
            pool.wait_ge(s_xt, xt_base["peer1"])
            pool.dma_start(keys, A["keys"][1]).then_inc(s_key, 16)
            spill(X)
            pool.wait_ge(s_spill, 48)
            gate_odd(2)
            reload(2, 0)

        @block.tensor
        def _(pe):
            mm = pe.matmul

            def ada_mm(q, k):
                bank = 7 if q in sets[1] else 6 + q % 2
                if k == 0:
                    if q == 0:
                        pe.wait_ge(s_cs, 1)
                    elif q in sets[1] or q in (10, 11):
                        pe.wait_ge(s_adr, q)
                    elif q >= 2:
                        pe.wait_ge(s_adr, q - 1)
                w = landed(pe, ("ada", q, k // 2))
                last = mm(ps[0:2, bank, :], cs[:, k, :], w[:, (k % 2) * 512:(k % 2) * 512 + 512],
                          start=k == 0, stop=k == KC - 1)
                if k % 2:
                    last.then_inc(s_ada, 1)

            def ada_transpose(q):
                pe.wait_ge(s_adr, q + 1)
                n = next(i for i, st in enumerate(sets) if q in st)
                if n and q == sets[n][0]:
                    pe.wait_ge(s_mod, n)
                for j in range(4):
                    last = pe.transpose(ps[:, 2, 8 * q + 2 * j:8 * q + 2 * j + 2], rows[:, q % 2, j * P:j * P + P],
                                        ident[0:2, 0:2])
                last.then_inc(s_adt, 1)

            def modulation(n):
                for q in sets[n]:
                    for k in range(KC):
                        ada_mm(q, k)
                    if q != sets[n][0]:
                        ada_transpose(q - 1)
                ada_transpose(sets[n][-1])

            def norm(n):
                width = T if n < 3 else X
                pe.wait_ge(s_tab[n // 2], 16)
                for k in range(KC):
                    pe.wait_ge(s_nsq, KC * n + k + 1)
                    mm(ps[:, norm_bank(n), 0:width], tab(n // 2, "ones"), mix[n // 2]["sq8"][:, k % 2, 0:width],
                       start=k == 0, stop=k == KC - 1).then_inc(s_nss, 1)

            def project(l, c):
                it = items[l][c]
                if c >= 2:
                    pe.wait_ge(s_zw[l], c - 1)
                if l == 0 and it["kind"] in ("rope", "ropek", "plain") and c >= 11:
                    pe.wait_ge(s_it[0], rx_upto[0][8])
                for rows, cols, mms in it["groups"]:
                    for i, (key, (k, w, wcols), act) in enumerate(mms):
                        if c == 0:
                            pe.wait_ge(s_nh, KC * 2 * l + k + 1)
                        wr = landed(pe, key)
                        if wcols is None:
                            lhs, rhs = act, wr[:, k * w:k * w + w]
                        else:
                            lhs, rhs = wr[:, k * w + wcols.start:k * w + wcols.stop], act
                        dst = ps[rows, c % 2, cols]
                        if len(rhs.shape) == 3:
                            dst = dst.rearrange("p (s t) -> p s t", s=2)
                        last = mm(dst, lhs, rhs, start=i == 0, stop=i == len(mms) - 1)
                last.then_inc(s_z[l], 1)

            def reduce_rotate(l, c):
                it, m = items[l][c], mix[l]
                if not has_rx(it):
                    return
                pe.wait_ge(s_zw[l], c + 1)
                if c == 0:
                    pe.wait_ge(s_tab[l], 16)
                if c >= 2 and rx_upto[l][c - 2]:
                    pe.wait_ge(s_it[l], rx_upto[l][c - 2])
                r, n = it["rows"], it["n"]
                if it["kind"] == "lora1":
                    mm(ps[:, 3 + c % 2, :], tab(l, "ones"), m["zsq"][:, (c - 1) % 2, :], start=True, stop=False)
                    mm(ps[:, 3 + c % 2, :], tab(l, "ones"), m["zsq"][:, c % 2, :], start=False, stop=True).then_inc(s_rx[l], 1)
                    return
                zw, zsq = (m["zk"], m["zks"]) if it["kind"] == "ropek" else (m["zw"], m["zsq"])
                w = 96 if it["tb"] == "B" else P
                bo, rot = ("bo96", "rot96") if it["tb"] == "B" else ("bo64", "rot64")
                if has_norm(it):
                    mm(ps[r, 3 + c % 2, 0:n], tab(l, bo)[r, 0:w], zsq[r, c % 2, 0:n], start=True, stop=True)
                mm(ps[r, 5 + c % 2, 0:n], tab(l, rot)[r, 0:w], zw[r, c % 2, 0:n], start=True,
                   stop=True).then_inc(s_rx[l], 1)

            def projections(l):
                project(l, 0)
                for c in range(len(items[l])):
                    if c + 1 < len(items[l]):
                        project(l, c + 1)
                    if l == 0 and c in in_items:
                        q, ks = in_items[c]
                        if ks[0] == 0 and q != sets[1][0]:
                            ada_transpose(q - 1)
                        for k in ks:
                            ada_mm(q, k)
                    reduce_rotate(l, c)
                if l == 0:
                    ada_transpose(sets[1][-1])

            def scores(l, a):
                it = att[l][a]
                if a >= 2:
                    pe.wait_ge(s_p[l], a - 1)
                n = it["nb"] * P
                last = mm(ps[:, a % 2, 0:n], it["q"], it["k"], start=True, stop=it["mask"] is None)
                if it["mask"]:
                    b, mk = it["mask"]
                    last = mm(ps[:, a % 2, b * P:b * P + P], ident, mk, start=False, stop=True)
                last.then_inc(s_s[l], 1)

            def transpose_probs(l, a):
                it, m = att[l][a], mix[l]
                pe.wait_ge(s_p[l], a + 1)
                if a >= 2:
                    pe.wait_ge(s_pe[l], a - 1)
                for b in range(it["nb"]):
                    last = pe.transpose(ps[:, 3 + a % 2, b * P:b * P + P], m["pr"][:, a % 2, b * P:b * P + P], ident)
                last.then_inc(s_pt[l], 1)

            def values(l, a):
                it, m = att[l][a], mix[l]
                g = a // 8
                pe.wait_ge(s_pe[l], a + 1)
                if a % 8 == 0 and g >= 2:
                    pe.wait_ge(s_oe[l], g - 1)
                if l == 1 and a == 8:
                    pe.wait_ge(s_osq, 2)
                for b in range(it["nb"]):
                    last = mm(ps[:, 5 + g % 2, it["h"] * 64:it["h"] * 64 + 64], m["pts"][:, a % 2, b * P:b * P + P],
                              it["v"][b], start=b == 0, stop=b == it["nb"] - 1)
                last.then_inc(s_pv[l], 1)

            def transpose_out(l, g):
                pe.wait_ge(s_on[l], g + 1)
                for j in range(4):
                    last = pe.transpose(ps[:, 5 + g % 2, j * P:j * P + P], mix[l]["on"][:, g % 2, j * P:j * P + P], ident)
                last.then_inc(s_ot[l], 1)

            def attention(l):
                n = len(att[l])
                pe.wait_ge(s_zw[l], len(items[l]))
                pe.wait_ge(s_it[l], rx_upto[l][-1])
                scores(l, 0)
                for a in range(n):
                    if a + 1 < n:
                        scores(l, a + 1)
                    if a >= 1:
                        values(l, a - 1)
                    transpose_probs(l, a)
                    if a % 8 == 2 and a > 8:
                        transpose_out(l, a // 8 - 1)
                    if l == 1 and a == 1:
                        retention_squares()
                values(l, n - 1)
                transpose_out(l, n // 8 - 1)

            def retention():
                pe.wait_ge(s_zw[1], len(items1))
                pe.wait_ge(s_it[1], rx_upto[1][-1])
                m = m1

                def rscores(h):
                    r = slice(64 * (h % 2), 64 * (h % 2) + 64)
                    for kt in range(4):
                        last = mm(ps[:, 2 * (h % 2) + kt // 2, (kt % 2) * X:(kt % 2) * X + X],
                                  m["kr"][r, h // 2, kt * P:kt * P + P], m["qr"][r, h // 2, :], start=True, stop=True)
                    last.then_inc(s_rs, 1)

                rscores(0)
                rscores(1)
                for h in range(4):
                    pe.wait_ge(s_rd, h + 1)
                    for kt in range(4):
                        last = mm(ps[:, 4 + h // 2, (h % 2) * X:(h % 2) * X + X], m["vr"][:, kt, h * P:h * P + P],
                                  m["sd"][:, h % 2, kt, :],
                                  start=kt == 0, stop=kt == 3)
                    last.then_inc(s_ro, 1)
                    if h + 2 < 4:
                        rscores(h + 2)
                pe.wait_ge(s_roe, 1)
                for b in range(2):
                    last = mm(ps[:, 6 + b, :], tab(1, "ones"), m["orr"][:, 2 * b:2 * b + 2, :].rearrange("p a b -> p (a b)"), start=True, stop=True)
                last.then_inc(s_mu, 1)

            def retention_squares():
                m = m1
                pe.wait_ge(s_osq, 1)
                for b in range(2):
                    last = mm(ps[:, 6 + b, :], tab(1, "ones"), m["osq"][:, 2 * b:2 * b + 2, :].rearrange("p a b -> p (a b)"), start=True, stop=True)
                last.then_inc(s_mu, 1)

            def output(l):
                pe.wait_ge(s_oe[l], len(att[l]) // 8)
                if l == 1:
                    pe.wait_ge(s_yr, 1)
                if l == 0:
                    pe.wait_ge(s_mod, 2)
                n = nq_cols[l]
                for m in range(KC):
                    w = landed(pe, ("wo", l, m)).rearrange("p (k m) -> p k m", k=KC)
                    if m >= 3:
                        pe.wait_ge(s_xt, xt_base[f"wo{l}"] + m - 2)
                    for k in range(KC):
                        last = mm(ps[:, m % 3, 0:n], w[:, k, :], mix[l]["oa"][:, k, :], start=k == 0, stop=k == KC - 1)
                    last.then_inc(s_wo, 1)

            def queries(l):
                n = tiles[l] * P

                def key_scores(m):
                    if m == 0:
                        pe.wait_ge(s_key, 16 * (l + 1))
                    pe.wait_ge(s_qe, 16 * l + m + 1)
                    if m >= 3:
                        pe.wait_ge(s_sce, 16 * l + m - 2)
                    for t in range(tiles[l]):
                        last = mm(ps[:, 3 + m % 3, t * P:t * P + P], tk["qt"][:, m % 3, t * P:t * P + P],
                                  keys[:, m, :], start=True, stop=True)
                    last.then_inc(s_sc, 1)

                for m in range(16):
                    w = landed(pe, ("wq", l, m)).rearrange("p (k m) -> p k m", k=KC)
                    if m >= 2:
                        pe.wait_ge(s_qe, 16 * l + m - 1)
                    for k in range(KC):
                        if m == 0:
                            pe.wait_ge(s_nh, KC * (2 * l + 1) + k + 1)
                        rhs = hk(k, 0, n)
                        dst = ps[:, m % 2, 0:n]
                        if n == T:
                            dst = dst.rearrange("p (s t) -> p s t", s=2)
                        last = mm(dst, w[:, k, :], rhs, start=k == 0, stop=k == KC - 1)
                    last.then_inc(s_q, 1)
                    if m >= 1:
                        key_scores(m - 1)
                    if l == 0 and m in after_query:
                        for k in range(KC):
                            ada_mm(after_query[m], k)
                    if l == 0 and m - 1 in after_query:
                        ada_transpose(after_query[m - 1])
                key_scores(15)
                pe.wait_ge(s_qe, 16 * l + 16)

            def select_transpose(l, t):
                n = tile_base[l] + t
                pe.wait_ge(s_tk, n + 1)
                if t >= 2:
                    pe.wait_ge(s_sel, n - 1)
                for j in range(3):
                    last = pe.transpose(ps[:, t % 2, j * P:j * P + P], tk["g"][:, t % 2, j, :], ident)
                last.then_inc(s_tt, 1)

            def selection(l):
                if l == 0:
                    modulation(3)
                    modulation(4)
                for t in range(tiles[l]):
                    select_transpose(l, t)
                    if l == 0 and t == 0:
                        modulation(5)

            def gate_matrices(n):
                l, g = groups[n]
                pe.wait_ge(s_sel, tile_base[l] + tiles[l])
                if n == 0:
                    pe.wait_ge(s_mod, len(sets))
                if n == 1:
                    pe.wait_ge(s_xt, xt_base["peer0"] + KC)

                def steps(i, first):
                    for j in range(4):
                        pe.wait_ge(s_gwp if j % 2 else s_gwd, i * 2 + (32 * n + j // 2 + 1))
                        pe.wait_ge(s_ob, i * 4 + (64 * n + j + 1))
                        if not first:
                            pe.wait_ge(s_ge, i * 4 + (64 * n + j - 3))
                        for t in range(4):
                            last = mm(ps[:, j, t * P:t * P + P], oha[j][:, t, :], ohb[:, j % 2, t, :],
                                      start=True, stop=True)
                        last.then_inc(s_g, 1)

                steps(0, True)
                with pe.Fori(1, 16) as i:
                    steps(i, False)

            def experts(n):
                l, g = groups[n]
                cnt = expert_count[n]

                def up(i, j, first):
                    if not first:
                        pe.wait_ge(s_gel, i * 2 + (P * n + j - 1))
                    for half in range(2):
                        pe.wait_ge(s_ul, i * 4 + (2 * P * n + 2 * j + half + 1))
                        for k in range(4 * half, 4 * half + 4):
                            for p, (u, h) in enumerate(((uh, hh), (uh, hl), (ul, hh))):
                                last = mm(ps[:, 4 + j, 0:GRP], u[:, k * P:k * P + P], h[:, k, :],
                                          start=k == 0 and p == 0, stop=k == KC - 1 and p == 2)
                        last.then_inc(s_a, 1)

                def down(i, j, start, stop):
                    pe.wait_ge(s_wl, i * 2 + (P * n + j + 1))
                    for half in range(2):
                        c = slice(half * 512, half * 512 + 512)
                        pe.wait_ge(s_vl, i * 4 + (2 * P * n + 2 * j + half + 1))
                        for tt in range(GRP_TILES):
                            for p, (w, v) in enumerate(((wh, vh), (wh, vl), (wl, vh))):
                                last = mm(ps[:, 2 * tt + half, :], w[:, j, tt * P:tt * P + P], v[:, c],
                                          start=start and p == 0, stop=stop and p == 2)
                        last.then_inc(s_y, 1)

                pe.wait_ge(s_ge, 64 * (n + 1))
                pe.wait_ge(s_hl, n + 1)
                up(0, 0, True)
                up(0, 1, True)
                down(0, 0, True, False)
                with pe.Fori(1, P // 2) as i:
                    up(i, 0, False)
                    down(i - 1, 1, False, False)
                    up(i, 1, False)
                    down(i, 0, False, False)
                down(P // 2 - 1, 1, False, True)
                pe.wait_ge(s_ye, 2 * n + 2)
                for m in range(KC):
                    if m >= 2:
                        pe.wait_ge(s_xt, group_xt(n) + m - 1)
                    for tt in range(GRP_TILES):
                        last = pe.transpose(ps[:, 4 + m % 2, tt * P:tt * P + P], ys[:, tt, m * P:m * P + P], ident)
                    last.then_inc(s_yt, 1)

            pe.wait_ge(s_par, 32)
            norm(0)
            modulation(0)
            projections(0)
            attention(0)
            output(0)
            norm(1)
            queries(0)
            selection(0)
            for n in range(2):
                gate_matrices(n)
                experts(n)
            norm(2)
            projections(1)
            retention()
            attention(1)
            output(1)
            norm(3)
            queries(1)
            selection(1)
            gate_matrices(2)
            experts(2)

        @block.scalar
        def _(act):
            own = Step(act, s_act)
            af = act.activation

            def ada_row(q):
                act.wait_ge(s_ada, 4 * q + 4)
                if q >= 2:
                    act.wait_ge(s_adt, q - 1)
                bank = 7 if q in sets[1] else 6 + q % 2
                af(rows[:, q % 2, :], ps[0:2, bank, :], ACT.Copy).then_inc(s_adr, 1)

            def squares(n):
                width = T if n < 3 else X
                m = mix[n // 2]
                for k in range(KC):
                    if n == 0:
                        act.wait_ge(s_x, 16)
                    else:
                        act.wait_ge(s_xt, {1: 0, 2: xt_base["peer0"] + KC, 3: xt_base["wo1"]}[n] + k + 1)
                    if KC * n + k >= 2:
                        act.wait_ge(s_nss, KC * n + k - 1)
                    af(m["sq8"][:, k % 2, 0:width], xt[:, k, 0:width], ACT.Square).then_inc(s_nsq, 1)
                act.wait_ge(s_nss, KC * n + KC)
                af(m["nrt"][:, 0:width], ps[:, norm_bank(n), 0:width], ACT.Sqrt, bias=pcol("eps"), scale=1.0 / D).then_inc(s_nrt, 1)

            def modulated(n):
                width = T if n < 3 else X
                m, l, w = mix[n // 2], n // 2, n % 2
                for k in range(KC):
                    act.wait_ge(s_nt, KC * n + k + 1)
                    for st in range(width // X):
                        last = af(ht[:, st, k, :], m["nt"][:, k % 2, st * X:st * X + X], ACT.Identity,
                                  bias=mod[:, l, 24 * w + k, st:st + 1])
                    last.then_inc(s_nh, 1)

            def decays(hs):
                m = m1
                if hs[0]:
                    return decay_exps(hs)
                own.do(af(m["lg"][:, 0:8], pcol("decf", 0, 8), ACT.Exp, scale=-1.0))
                own.do(af(m["lg"][:, 8:16], m["lg"][:, 0:8], ACT.Ln, bias=pcol("one")))
                own.do(af(m["lg"][:, 0:8], m["lg"][:, 8:16], ACT.Copy, scale=-1.0))
                decay_exps(hs)

            def decay_exps(hs):
                m = m1
                for h in hs:
                    if h >= 1:
                        act.wait_ge(s_dt, h)
                    af(m["de"][:, 0, :], tab(1, "df"), ACT.Exp, scale=m["lg"][:, h:h + 1])
                    af(m["de"][:, 1, :], tab(1, "db"), ACT.Exp, scale=m["lg"][:, 4 + h:5 + h]).then_inc(s_ex, 1)

            def projections(l):
                m = mix[l]

                def read(c):
                    it = items[l][c]
                    kind, r, n = it["kind"], it["rows"], it["n"]
                    z = ps[r, c % 2, 0:n]
                    act.wait_ge(s_z[l], c + 1)
                    if kind == "plain":
                        af(it["dest"], z, ACT.Copy).then_inc(s_zw[l], 1)
                        return
                    if kind == "silu":
                        af(it["dest"], z, ACT.Silu).then_inc(s_zw[l], 1)
                        return
                    if c >= 2:
                        b = c - 2
                        if kind != "kr" and items[l][b]["kind"] == "lora0":
                            b = c - 1
                        if rx_upto[l][b]:
                            act.wait_ge(s_rx[l], rx_upto[l][b])
                        if rx_upto[l][c - 2]:
                            act.wait_ge(s_it[l], rx_upto[l][c - 2])
                    if kind == "kr":
                        for b in range(2):
                            own.inc(af(m["zk"][r, b, :], z, ACT.Copy, scale=it["w"]))
                            last = af(m["zks"][r, b, :], z, ACT.Square)
                        last.then_inc(s_zw[l], 1)
                        return
                    if kind == "ropek":
                        r = slice(0, 64)
                        z = ps[r, c % 2, 0:n]
                        af(m["zk"][r, c % 2, 0:n], z, ACT.Copy, scale=it["w"])
                        af(m["zks"][r, c % 2, 0:n], z, ACT.Square).then_inc(s_zw[l], 1)
                        return
                    zw = m["zw"][r, c % 2, 0:n] if kind in ("rope", "rope0") else it["dest"][:, int(kind == "lora1"), :]
                    if kind == "rope0":
                        af(zw, z, ACT.Copy, scale=1.0).then_inc(s_zw[l], 1)
                        return
                    af(zw, z, ACT.Copy, scale=it["w"])
                    af(m["zsq"][r, c % 2, 0:n], z, ACT.Square).then_inc(s_zw[l], 1)

                def root(c):
                    it = items[l][c]
                    if not has_norm(it):
                        return
                    r, n = it["rows"], it["n"]
                    act.wait_ge(s_rx[l], rx_upto[l][c])
                    if c >= 2 and rx_upto[l][c - 2]:
                        act.wait_ge(s_it[l], rx_upto[l][c - 2])
                    dim = {"lora1": 256, "rope": 64, "ropek": 96}[it["kind"]]
                    if it["kind"] == "rope" and it["tb"] == "B":
                        dim = 96
                    af(m["rt"][r, c % 2, 0:n], ps[r, 3 + c % 2, 0:n], ACT.Sqrt, bias=pcol("eps", rows=r),
                       scale=1.0 / dim).then_inc(s_rt[l], 1)

                for c in range(len(items[l])):
                    read(c)
                    if l == 1 and items[l][c]["kind"] == "plain" and items[l][c - 1]["kind"] == "plain":
                        decays([c - 10])
                    if c >= 1:
                        root(c - 1)
                    if l == 0 and c in in_items and in_items[c][1][-1] == KC - 1:
                        ada_row(in_items[c][0])
                root(len(items[l]) - 1)

            def attention(l):
                m = mix[l]

                def exps(a):
                    it = att[l][a]
                    n = it["nb"] * P
                    act.wait_ge(s_nm[l], a + 1)
                    if a >= 2:
                        act.wait_ge(s_pt[l], a - 1)
                    af(m["pr"][:, a % 2, 0:n], ps[:, a % 2, 0:n], ACT.Exp, bias=m["st"][:, 0, a:a + 1],
                       scale=it["sc"], accum_out=m["st"][:, 1, a:a + 1]).then_inc(s_p[l], 1)

                def evacuate(a):
                    n = att[l][a]["nb"] * P
                    act.wait_ge(s_pt[l], a + 1)
                    if a >= 2:
                        act.wait_ge(s_pv[l], a - 1)
                    af(m["pts"][:, a % 2, 0:n], ps[:, 3 + a % 2, 0:n], ACT.Copy).then_inc(s_pe[l], 1)

                def sinks(g):
                    act.wait_ge(s_se, g + 1)
                    c = slice(8 * g, 8 * g + 8)
                    af(m["st"][:, 3, c], m["st"][:, 2, c], ACT.Exp).then_inc(s_es, 1)

                def gather(g):
                    act.wait_ge(s_ot[l], g + 1)
                    af(att[l][8 * g]["dest"], ps[:, 5 + g % 2, :].rearrange("p (j q) -> p j q", j=4),
                       ACT.Copy).then_inc(s_oe[l], 1)

                for a in range(len(att[l])):
                    exps(a)
                    if a % 8 == 0 and a and att[l][a - 1]["sink"]:
                        sinks(a // 8 - 1)
                    evacuate(a)
                    if l == 1 and a == 2:
                        retention_root()
                    if a % 8 == 3 and a > 8:
                        gather(a // 8 - 1)
                gather(len(att[l]) // 8 - 1)

            def retention():
                m = m1
                act.wait_ge(s_ro, 4)
                af(m["orr"].rearrange("p h t -> p (h t)"), ps[:, 4:6, :].rearrange("p a b -> p (a b)"),
                   ACT.Copy).then_inc(s_roe, 1)
                act.wait_ge(s_oc, 1)
                af(m["osq"].rearrange("p h t -> p (h t)"), m["orr"].rearrange("p h t -> p (h t)"),
                   ACT.Square).then_inc(s_osq, 1)

            def retention_root():
                m = m1
                act.wait_ge(s_mu, 2)
                af(m["ort"], ps[:, 6:8, :].rearrange("p a b -> p (a b)"), ACT.Sqrt, bias=pcol("eps"),
                   scale=1.0 / P).then_inc(s_osq, 1)

            def peer(l):
                n = tiles[l] * P

                def score_copy(m):
                    act.wait_ge(s_sc, 16 * l + m + 1)
                    af(tk["sc"][:, 0:tiles[l], m, :], ps[:, 3 + m % 3, 0:n].rearrange("p (t n) -> p t n", n=P),
                       ACT.Copy).then_inc(s_sce, 1)

                for m in range(16):
                    act.wait_ge(s_q, 16 * l + m + 1)
                    if m >= 3:
                        act.wait_ge(s_sc, 16 * l + m - 2)
                    af(tk["qt"][:, m % 3, 0:n], ps[:, m % 2, 0:n], ACT.Copy).then_inc(s_qe, 1)
                    if m >= 1:
                        score_copy(m - 1)
                    if l == 0 and m - 1 in after_query:
                        ada_row(after_query[m - 1])
                score_copy(15)
                if l == 0:
                    for q in sets[3]:
                        ada_row(q)
                act.wait_ge(s_best, l + 1)
                bv = tk["bv"][:, 0:tiles[l]].rearrange("p t h k -> p (t h k)")
                af(bv, bv, ACT.Exp).then_inc(s_bexp, 1)
                if l == 0:
                    for q in sets[4]:
                        ada_row(q)
                for t in range(tiles[l]):
                    k = tile_base[l] + t
                    if l == 0 and t == 1:
                        for q in sets[5]:
                            ada_row(q)
                    act.wait_ge(s_tt, k + 1)
                    af(sel[:, t * P:t * P + P], ps[:, t % 2, 0:P], ACT.Copy)
                    af(selk[:, :, t * P:t * P + P], ps[:, t % 2, P:3 * P].rearrange("p (a b) -> p a b", a=2),
                       ACT.Copy).then_inc(s_sel, 1)

            def gate_matrices(n):
                l, g = groups[n]
                if n != 1:
                    act.wait_ge(s_tk, tile_base[l] + tiles[l])
                af(hh[:, :, :], ht[:, g, :, :], ACT.Copy).then_inc(s_hh, 1)
                act.wait_ge(s_spill, 16 * (n + 1))
                act.wait_ge(s_hl, n + 1)

                def convert(i, j, first):
                    act.wait_ge(s_oh, i * 4 + (64 * n + j + 1))
                    if not first:
                        act.wait_ge(s_g, i * 4 + (64 * n + j - 1))
                    af(ohb[:, j % 2, :, :].rearrange("p t n -> p n t"), eqb[:, j % 2, 1, :, :],
                       ACT.Copy).then_inc(s_ob, 1)

                def evacuate(i, j):
                    act.wait_ge(s_g, i * 4 + (64 * n + j + 1))
                    at = i * 16 + 4 * j
                    to = gates[:, :, at:at + 4] if isinstance(at, int) else gates[:, :, bass.ds(at, 4)]
                    af(to, ps[:, j, :].rearrange("p (t i) -> p i t", t=4), ACT.Copy).then_inc(s_ge, 1)

                for j in range(4):
                    convert(0, j, j < 2)
                    if j >= 2:
                        evacuate(0, j - 2)
                with act.Fori(1, 16) as i:
                    for j in range(4):
                        convert(i, j, False)
                        evacuate(i - (j < 2), (j - 2) % 4)
                evacuate(15, 2)
                evacuate(15, 3)

            def experts(n):
                act.wait_ge(s_g, 64 * (n + 1))
                cnt = expert_count[n]

                def up_part(i, j, first):
                    act.wait_ge(s_slot[2 * j], i * 16 + 16 * (cnt[2 * j] + 1))
                    for half in range(2):
                        c = slice(half * 512, half * 512 + 512)
                        if not first:
                            act.wait_ge(s_a, i * 4 + (2 * P * n + 2 * j + half - 1))
                        af(uh[:, c], ring[:, 2 * j, c], ACT.Copy).then_inc(s_uh, 1)

                def down_part(i, j, first):
                    act.wait_ge(s_slot[2 * j + 1], i * 16 + 16 * (cnt[2 * j + 1] + 1))
                    for half in range(2):
                        c = slice(half * 512, half * 512 + 512)
                        if not first:
                            act.wait_ge(s_y, i * 4 + (2 * P * n + 2 * j + half - 1))
                        af(vh[:, c], ring[:, 2 * j + 1, c], ACT.Copy).then_inc(s_vh, 1)

                def gelu(i, j, first):
                    act.wait_ge(s_a, i * 4 + (2 * P * n + 2 * j + 2))
                    if not first:
                        act.wait_ge(s_wl, i * 2 + (P * n + j - 1))
                    af(gel[:, j, :], ps[:, 4 + j, 0:GRP], ACT.Gelu_apprx_tanh).then_inc(s_gel, 1)

                def high(i, j, first):
                    act.wait_ge(s_w, i * 2 + (P * n + j + 1))
                    if not first:
                        act.wait_ge(s_y, i * 4 + (2 * P * n + 2 * j - 2))
                    af(wh[:, j, :], gel[:, j, :], ACT.Copy).then_inc(s_wh, 1)

                def both(i, j, first, last):
                    if not last:
                        up_part(i + j, 1 - j, False)
                    gelu(i, j, first)
                    high(i, j, first)
                    down_part(i, j, first and j == 0)

                up_part(0, 0, True)
                both(0, 0, True, False)
                both(0, 1, True, False)
                with act.Fori(1, P // 2 - 1) as i:
                    both(i, 0, False, False)
                    both(i, 1, False, False)
                both(P // 2 - 1, 0, False, False)
                both(P // 2 - 1, 1, False, True)
                act.wait_ge(s_y, 2 * P * (n + 1))
                for tt in range(GRP_TILES):
                    af(ys[:, tt, :], ps[:, 2 * tt:2 * tt + 2, :].rearrange("p a b -> p (a b)"), ACT.Copy).then_inc(s_ye, 1)

            act.wait_ge(s_par, 32)
            af(cs[:, :, :], pcol("c", 0, 16).rearrange("p (k s) -> p k s", s=2), ACT.Silu).then_inc(s_cs, 1)
            squares(0)
            for q in sets[0]:
                ada_row(q)
            modulated(0)
            projections(0)
            attention(0)
            squares(1)
            modulated(1)
            peer(0)
            for n in range(2):
                gate_matrices(n)
                experts(n)
            squares(2)
            modulated(2)
            projections(1)
            retention()
            attention(1)
            squares(3)
            modulated(3)
            peer(1)
            gate_matrices(2)
            experts(2)

        @block.vector
        def _(dve):
            own = Step(dve, s_dve)
            tt, ts, stt = dve.tensor_tensor, dve.tensor_scalar, dve.scalar_tensor_tensor

            def modulation(n):
                dve.wait_ge(s_adt, sets[n][-1] + 1)
                todo = []
                for l in range(2):
                    qs = [q for q in sets[n] if blocks[q][0] == l]
                    if not qs:
                        continue
                    a, cnt = 4 * blocks[qs[0]][1], 4 * len(qs)
                    own.inc(tt(mod[:, l, a:a + cnt, :], ps[:, 2, 8 * qs[0]:8 * qs[0] + 2 * cnt].rearrange(
                        "p (m s) -> p m s", s=2),
                        pcol("ada_b", 48 * l + a, cnt).unsqueeze(2).broadcast_to([P, cnt, 2]), ALU.add))
                    for q in qs:
                        for w in range(2):
                            at = 4 * blocks[q][1] - (8 + 24 * w)
                            if at in (0, 4):
                                todo.append((l, w, at))
                own.wait()
                for l, w, at in todo:
                    own.inc(stt(out=gain[:, 2 * l + w, at:at + 4, :], in0=mod[:, l, 8 + 24 * w + at:12 + 24 * w + at, :],
                                scalar=1.0, op0=ALU.add, op1=ALU.mult,
                                in1=pcol("n2" if w else "n1", KC * l + at, 4).unsqueeze(2).broadcast_to([P, 4, 2])))
                own.wait()
                dve.sem_inc(s_mod, 1)

            def inverse_root(n):
                width = T if n < 3 else X
                m = mix[n // 2]
                dve.wait_ge(s_nrt, n + 1)
                own.do(dve.reciprocal(m["nrb"][:, 0:width], m["nrt"][:, 0:width]))

            def norm(n):
                width = T if n < 3 else X
                m = mix[n // 2]
                for k in range(KC):
                    if k >= 2:
                        dve.wait_ge(s_nh, KC * n + k - 1)
                    for st in range(width // X):
                        c = slice(st * X, st * X + X)
                        last = stt(out=m["nt"][:, k % 2, c], in0=xt[:, k, c], scalar=gain[:, n, k, st:st + 1],
                                   in1=m["nrb"][:, c], op0=ALU.mult, op1=ALU.mult)
                    last.then_inc(s_nt, 1)

            def projections(l):
                m = mix[l]
                for c, it in enumerate(items[l]):
                    if not has_rx(it):
                        continue
                    r, n = it["rows"], it["n"]
                    if it["kind"] == "lora1":
                        dve.wait_ge(s_rt[l], rt_upto[l][c])
                        own.do(dve.reciprocal(m["ri"], m["rt"][:, c % 2, :]))
                        own.inc(tt(it["dest"][:, 0, :], it["dest"][:, 0, :], m["ri"], ALU.mult))
                        tt(it["dest"][:, 1, :], it["dest"][:, 1, :], m["ri"], ALU.mult).then_inc(s_it[l], 1)
                        continue
                    zw = m["zk"] if it["kind"] == "ropek" else m["zw"]
                    dve.wait_ge(s_rx[l], rx_upto[l][c])
                    own.inc(tt(m["ta"][r, 0:n], zw[r, c % 2, 0:n], tab(l, "cos" + it["tb"])[r, 0:n], ALU.mult))
                    own.do(tt(m["tb"][r, 0:n], ps[r, 5 + c % 2, 0:n], tab(l, "sin" + it["tb"])[r, 0:n], ALU.mult))
                    if not has_norm(it):
                        tt(it["dest"], m["ta"][r, 0:n], m["tb"][r, 0:n], ALU.add).then_inc(s_it[l], 1)
                        dve.wait_ge(s_it[l], rx_upto[l][c])
                        continue
                    own.inc(tt(m["ta"][r, 0:n], m["ta"][r, 0:n], m["tb"][r, 0:n], ALU.add))
                    dve.wait_ge(s_rt[l], rt_upto[l][c])
                    own.do(dve.reciprocal(m["ri"][r, 0:n], m["rt"][r, c % 2, 0:n]))
                    tt(it["dest"], m["ta"][r, 0:n], m["ri"][r, 0:n], ALU.mult).then_inc(s_it[l], 1)
                    dve.wait_ge(s_it[l], rx_upto[l][c])

            def attention(l):
                m = mix[l]
                st = m["st"]

                def sink_terms(g):
                    c = slice(8 * g, 8 * g + 8)
                    tt(st[:, 2, c], st[:, 0, c], nsink[:, :], ALU.subtract).then_inc(s_se, 1)

                def normalise(g):
                    c = slice(8 * g, 8 * g + 8)
                    dve.wait_ge(s_pv[l], 8 * g + 8)
                    den = st[:, 1, c]
                    if att[l][8 * g]["sink"]:
                        dve.wait_ge(s_es, g + 1)
                        own.do(tt(st[:, 5, c], st[:, 1, c], st[:, 3, c], ALU.add))
                        den = st[:, 5, c]
                    own.do(dve.reciprocal(st[:, 4, c], den))
                    if g >= 2:
                        dve.wait_ge(s_ot[l], g - 1)
                    tt(m["on"][:, g % 2, :].rearrange("p (h d) -> p h d", h=HEADS),
                       ps[:, 5 + g % 2, :].rearrange("p (h d) -> p h d", h=HEADS),
                       st[:, 4, c].unsqueeze(2).broadcast_to([P, HEADS, 64]), ALU.mult).then_inc(s_on[l], 1)

                for a, it in enumerate(att[l]):
                    w = it["nb"] * P
                    dve.wait_ge(s_s[l], a + 1)
                    mx, nm = st[:, 5, a:a + 1], st[:, 0, a:a + 1]
                    own.do(dve.tensor_reduce(mx, ps[:, a % 2, 0:w], AXX, ALU.max))
                    if it["sink"]:
                        ts(nm, mx, -it["sc"], nsink[:, it["h"]:it["h"] + 1], ALU.mult, ALU.min).then_inc(s_nm[l], 1)
                    else:
                        ts(nm, mx, -it["sc"], None, ALU.mult).then_inc(s_nm[l], 1)
                    if a % 8 == 7 and it["sink"]:
                        dve.wait_ge(s_nm[l], a + 1)
                        sink_terms(a // 8)
                    if a % 8 == 1 and a > 8:
                        normalise(a // 8 - 1)
                    if l == 1 and a in (4, 6, 8):
                        retention_scale(a // 2 - 2)
                normalise(len(att[l]) // 8 - 1)

            def output(l):
                for m in range(KC):
                    dve.wait_ge(s_wo, wo_base[l] + m + 1)
                    for st in range(nq_cols[l] // X):
                        c = slice(st * X, st * X + X)
                        last = stt(out=xt[:, m, c], in0=ps[:, m % 3, c], scalar=mod[:, l, 16 + m, st:st + 1],
                                   in1=xt[:, m, c], op0=ALU.mult, op1=ALU.add)
                    last.then_inc(s_xt, 1)

            def decays():
                m = m1
                for h in range(4):
                    dve.wait_ge(s_ex, h + 1)
                    for b, name in enumerate(("mf", "mb")):
                        last = tt(m["de"][:, b, 0:512], m["de"][:, b, 0:512], tab(1, name), ALU.mult)
                        own.inc(last)
                    own.wait()
                    own.do(tt(m["dt"][:, h, :, :].rearrange("p a b -> p (a b)"), m["de"][:, 0, :], m["de"][:, 1, :], ALU.add))
                    dth = m["dt"][:, h, :, :].rearrange("p a b -> p (a b)")
                    ts(dth, dth, HD ** -0.5, None, ALU.mult).then_inc(s_dt, 1)

            def retention():
                m = m1
                dve.wait_ge(s_dt, 4)
                for h in range(4):
                    dve.wait_ge(s_rs, h + 1)
                    if h >= 2:
                        dve.wait_ge(s_ro, h - 1)
                    b = 2 * (h % 2)
                    tt(m["sd"][:, h % 2, :, :].rearrange("p a b -> p (a b)"),
                       ps[:, b:b + 2, :].rearrange("p a b -> p (a b)"),
                       m["dt"][:, h, :, :].rearrange("p a b -> p (a b)"), ALU.mult).then_inc(s_rd, 1)
                orr = m["orr"].rearrange("p h t -> p (h t)")
                dve.wait_ge(s_mu, 1)
                stt(out=orr, in0=ps[:, 6:8, :].rearrange("p a b -> p (a b)"), scalar=-1.0 / P, in1=orr,
                    op0=ALU.mult, op1=ALU.add).then_inc(s_oc, 1)

            def retention_scale(part):
                m = m1
                orr = m["orr"].rearrange("p h t -> p (h t)")
                if part < 2:
                    dve.wait_ge(s_osq, 2)
                    half = m["ort"][:, part * 512:part * 512 + 512]
                    own.inc(dve.reciprocal(half, half))
                    return
                own.wait()
                own.do(tt(orr, orr, m["ort"], ALU.mult))
                for h in range(4):
                    last = stt(out=m["oa"][:, h, :], in0=m["orr"][:, h, :], scalar=pcol("gn", h),
                               in1=m["sg"][:, h, :], op0=ALU.mult, op1=ALU.mult)
                    if h < 3:
                        own.inc(last)
                last.then_inc(s_yr, 1)

            def topk(l):
                v, bv, cd, sc, g3, nt = tk["v"], tk["bv"], tk["cd"], tk["sc"], tk["g"], tiles[l]

                def best16(rows):
                    lanes, done = [rows[0::2], rows[1::2]], [0, 0]
                    for step in range(5):
                        s8 = slice(8 * (step // 3), 8 * (step // 3) + 8)
                        for x in range(2):
                            if step:
                                own.wait_upto(done[x])
                            for vals, idx, data in lanes[x]:
                                if step % 3 == 0:
                                    own.inc(dve.max(vals[:, s8], data))
                                elif step % 3 == 1:
                                    own.inc(dve.max_index(idx[:, s8], vals[:, s8], data))
                                else:
                                    own.inc(dve.match_replace(data, vals[:, s8], data, LOWEST))
                            done[x] = own.n
                    own.wait()

                def sums(h):
                    return [(bv[:, t, h, :], piu[:, t, h * 16:h * 16 + 16], cd[:, t, :]) for t in range(nt)]

                for m in range(16):
                    dve.wait_ge(s_sce, 16 * l + m + 1)
                    h = m // 2
                    best16([(v[:, t, m, :], iu[:, t, m, :], sc[:, t, m, :]) for t in range(nt)] +
                           (sums(h - 1) if m % 2 == 0 and h else []))
                    if m % 2:
                        own.do(tt(cd[:, 0:nt].rearrange("p t (a b) -> p t a b", a=16),
                                  v[:, 0:nt, m - 1, :].unsqueeze(3).broadcast_to([P, nt, 16, 16]),
                                  v[:, 0:nt, m, :].unsqueeze(2).broadcast_to([P, nt, 16, 16]), ALU.add))
                best16(sums(HEADS - 1))
                for two in range(2):
                    own.inc(dve.tensor_copy(ifb[:, two, 0:nt].rearrange("p t a h -> p t h a"),
                                            iu[:, 0:nt].rearrange("p t (h two) a -> p two t h a", two=2)[:, two]))
                bvr = bv[:, 0:nt].rearrange("p t h k -> p (t h) k")
                own.do(dve.tensor_copy(tk["mx"][:, 0:8 * nt], bvr[:, :, 0]))
                tt(bvr, bvr, tk["mx"][:, 0:8 * nt].unsqueeze(2).broadcast_to([P, 8 * nt, 16]),
                   ALU.subtract).then_inc(s_best, 1)
                if l == 0:
                    modulation(2)
                for t in range(nt):
                    n = tile_base[l] + t
                    own.inc(ts(pmu[:, 0, :], piu[:, t, :], 4, None, ALU.logical_shift_right))
                    own.do(ts(pmu[:, 1, :], piu[:, t, :], 15, None, ALU.bitwise_and))
                    for half in range(2):
                        own.inc(dve.tensor_copy(pfb[:, half, :].rearrange("p (k h) -> p k h", h=HEADS),
                                                pmu[:, half, :].rearrange("p (h k) -> p k h", h=HEADS)))
                    own.wait()
                    if t >= 2:
                        dve.wait_ge(s_tt, n - 1)
                    for half in range(2):
                        own.do(tt(eqk.rearrange("p a (s q) -> p a s q", q=4),
                                  pfb[:, half, :].rearrange("p (s q) -> p s q", q=4).unsqueeze(1).broadcast_to([P, 16, 32, 4]),
                                  iob[:, 0:16, :].unsqueeze(2).broadcast_to([P, 16, 32, 4]), ALU.is_equal))
                        e4 = eqk.rearrange("p a (k h) -> p a k h", h=HEADS)
                        own.do(tt(e4, e4, ifb[:, half, t].unsqueeze(2).broadcast_to([P, 16, 16, HEADS]), ALU.mult))
                        for w in (8, 4):
                            own.do(tt(eqk[:, 0:w], eqk[:, 0:w], eqk[:, w:2 * w], ALU.add))
                        own.do(dve.tensor_reduce(g3[:, t % 2, 1 + half, :], eqk[:, 0:4].rearrange("p a s -> p s a"),
                                                 AXX, ALU.add))
                    if t == 0:
                        dve.wait_ge(s_bexp, l + 1)
                        own.do(dve.tensor_reduce(tk["mx"][:, 0:8 * nt], bvr, AXX, ALU.add))
                        own.do(dve.reciprocal(tk["rs"][:, 0:8 * nt], tk["mx"][:, 0:8 * nt]))
                    tt(g3[:, t % 2, 0, :].rearrange("p (k h) -> p h k", h=HEADS), bv[:, t],
                       tk["rs"][:, 8 * t:8 * t + 8].unsqueeze(2).broadcast_to([P, HEADS, 16]), ALU.mult).then_inc(s_tk, 1)
                    dve.wait_ge(s_tk, n + 1)
                    if l == 0 and t:
                        modulation(2 + t)

            def one_hots(n):
                l, g = groups[n]
                dve.wait_ge(s_hh, n + 1)
                tt(hl[:, :, :], ht[:, g, :, :], hh[:, :, :].bitcast(F32), ALU.subtract).then_inc(s_hl, 1)
                dve.wait_ge(s_sel, tile_base[l] + tiles[l])
                if n >= 1:
                    dve.wait_ge(s_y, 2 * P * n)

                def columns(i, j):
                    at = i * 16 + (g * GRP + 4 * j)
                    return slice(at, at + 4) if isinstance(at, int) else bass.ds(at, 4)

                def compare(i, j, first):
                    if not first:
                        dve.wait_ge(s_gwp if j % 2 else s_gwd, i * 2 + (32 * n + j // 2))
                        dve.wait_ge(s_ob, i * 4 + (64 * n + j - 1))
                    tt(eqb[:, j % 2], iob[:, :, :].unsqueeze(1).broadcast_to([P, 2, P, 4]),
                       selk[:, :, columns(i, j)].unsqueeze(2).broadcast_to([P, 2, P, 4]),
                       ALU.is_equal).then_inc(s_oh, 1)

                def gate(i, j, first):
                    dve.wait_ge(s_oh, i * 4 + (64 * n + j + 1))
                    if not first:
                        dve.wait_ge(s_g, i * 4 + (64 * n + j - 3))
                    tt(oha[j].rearrange("p t n -> p n t"), eqb[:, 0, 0],
                       sel[:, columns(i, j)].unsqueeze(1).broadcast_to([P, P, 4]), ALU.mult).then_inc(s_gwd, 1)

                def steps(i, first):
                    for j in (0, 2):
                        compare(i, j, first and j == 0)
                        compare(i, j + 1, first and j == 0)
                        gate(i, j, first)

                steps(0, True)
                with dve.Fori(1, 16) as i:
                    steps(i, False)

            def experts(n):
                dve.wait_ge(s_g, 64 * (n + 1))
                dve.wait_ge(s_ge, 64 * (n + 1))

                def low(dst, raw, high, sem):
                    tt(dst, raw, high.bitcast(F32), ALU.subtract).then_inc(sem, 1)

                def up_part(i, j):
                    for half in range(2):
                        c = slice(half * 512, half * 512 + 512)
                        dve.wait_ge(s_uh, i * 4 + (2 * P * n + 2 * j + half + 1))
                        low(ul[:, c], ring[:, 2 * j, c], uh[:, c], s_ul)

                def down_part(i, j):
                    for half in range(2):
                        c = slice(half * 512, half * 512 + 512)
                        dve.wait_ge(s_vh, i * 4 + (2 * P * n + 2 * j + half + 1))
                        low(vl[:, c], ring[:, 2 * j + 1, c], vh[:, c], s_vl)

                def weigh(i, j):
                    at = i * 2 + j
                    g = gates[:, at, :] if isinstance(at, int) else gates[:, bass.ds(at, 1), :].rearrange("p a t -> p (a t)")
                    dve.wait_ge(s_gel, i * 2 + (P * n + j + 1))
                    tt(gel[:, j, :], gel[:, j, :], g, ALU.mult).then_inc(s_w, 1)
                    dve.wait_ge(s_wh, i * 2 + (P * n + j + 1))
                    low(wl[:, j, :], gel[:, j, :], wh[:, j, :], s_wl)

                def both(i, j, last):
                    if not last:
                        up_part(i + j, 1 - j)
                    weigh(i, j)
                    down_part(i, j)

                up_part(0, 0)
                both(0, 0, False)
                both(0, 1, False)
                with dve.Fori(1, P // 2 - 1) as i:
                    both(i, 0, False)
                    both(i, 1, False)
                both(P // 2 - 1, 0, False)
                both(P // 2 - 1, 1, True)
                dve.wait_ge(s_rel, 16 * [1, 3, 4][n])
                l, g = groups[n]
                c = slice(g * GRP, g * GRP + GRP)
                for m in range(KC):
                    dve.wait_ge(s_yt, KC * n + m + 1)
                    stt(out=xt[:, m, c], in0=ps[:, 4 + m % 2, 0:GRP], scalar=mod[:, l, 40 + m, g:g + 1],
                        in1=xt[:, m, c], op0=ALU.mult, op1=ALU.add).then_inc(s_xt, 1)

            dve.wait_ge(s_par, 32)
            own.inc(dve.tensor_copy(iob[:, :, :], iota.unsqueeze(2).broadcast_to([P, P, 4])))
            own.inc(ts(nsink[:, :], pcol("sink", 0, 8), -1.0, None, ALU.mult))
            inverse_root(0)
            modulation(0)
            norm(0)
            projections(0)
            modulation(1)
            attention(0)
            output(0)
            inverse_root(1)
            norm(1)
            topk(0)
            for n in range(2):
                one_hots(n)
                experts(n)
            inverse_root(2)
            norm(2)
            projections(1)
            decays()
            retention()
            attention(1)
            output(1)
            inverse_root(3)
            norm(3)
            topk(1)
            one_hots(2)
            experts(2)


def _chunks(w, cols):
    w = w[:, cols]
    k = w.shape[0] // P
    return np.ascontiguousarray(w.reshape(k, P, -1, P).transpose(2, 1, 0, 3))


def _rope_tables(head, start, half, rows):
    cos = np.ones((rows, T), np.float32)
    sin = np.zeros((rows, T), np.float32)
    rot = np.zeros((P, P), np.float32)
    t = np.arange(X)
    posn = [t // GRID_W, t % GRID_W]
    fr = (np.float32(10000.0) ** (-np.arange(half, dtype=np.float32) / np.float32(half))).astype(np.float32)
    for r in range(rows):
        f = r % head - start
        if f < 0:
            continue
        ang = posn[f // (2 * half)].astype(np.float32) * fr[f % half]
        low = f % (2 * half) < half
        cos[r, :X] = np.cos(ang)
        sin[r, :X] = -np.sin(ang) if low else np.sin(ang)
        rot[r + half if low else r - half, r] = 1.0
    return cos, sin, rot


def _tables():
    ca, sa, ra = _rope_tables(64, 0, 16, P)
    cb, sb_, rb = _rope_tables(P, 64, 8, 96)
    pad = ((0, 32), (0, 0))
    cb, sb_ = np.pad(cb, pad), np.pad(sb_, pad)
    i = np.arange(P)
    bo64 = (i[:, None] // 64 == i[None] // 64).astype(np.float32)
    ones = np.ones((P, P), np.float32)
    m01 = np.where(i[None] <= i[:, None], 0.0, NEG).astype(np.float32)
    m10 = np.where(i[None] >= i[:, None], 0.0, NEG).astype(np.float32)
    tab0 = dict(cosA=ca, sinA=sa, bo64=bo64, rot64=ra, ones=ones, cosB=cb, sinB=sb_, bo96=ones, rot96=rb,
                m01=m01, m10=m10)
    q = np.arange(X)[None]
    df, db = np.zeros((P, 4, X), np.float32), np.zeros((P, 4, X), np.float32)
    mf, mb = np.zeros((P, 2, X), np.float32), np.zeros((P, 2, X), np.float32)
    for kt in range(4):
        j = (kt % 2) * P + i[:, None]
        if kt < 2:
            df[:, kt] = db[:, kt] = np.abs(q - j)
            mf[:, kt], mb[:, kt] = j <= q, j >= q
        else:
            df[:, kt], db[:, kt] = X + q - j, X - q + j
    tab1 = dict(cosA=ca, sinA=sa, bo64=bo64, rot64=ra, ones=ones, df=df, db=db, mf=mf, mb=mb)
    return [np.concatenate([d[n].reshape(P, -1) for n in TAB[l]], axis=1) for l, d in enumerate((tab0, tab1))]


def kernel(x, c, ctx, c_ctx, ada_w, ada_b, norm1_w, norm2_w, ab_w_in, ab_w_o, a_q_norm, a_k_norm,
           a_sink, b_q_lora_norm, b_kv_lora_norm, b_w_uq, b_w_ukv, b_q_norm, b_k_norm, cd_w_in, cd_w_o,
           c_decay_fwd, c_decay_bwd, c_gn_w, d_q_norm, d_k_norm, peer_w_q, peer_keys, peer_u, peer_v):
    import concourse.bacc as _bacc
    from concourse.bass_utils import run_bass_kernel_spmd as _run

    f = np.asarray
    a = {}
    tokens = np.concatenate([f(x)[0], f(ctx)[0]], axis=0)
    a["x"] = tokens.reshape(T, KC, P).transpose(2, 1, 0)
    a["ada"] = f(ada_w).reshape(2, 4, 2, P, BLOCKS, 512).transpose(0, 4, 1, 3, 2, 5)
    r = np.arange
    pairs = np.concatenate([np.concatenate([r(j * 64, j * 64 + 64), r((j + 4) * 64, (j + 4) * 64 + 64)])
                            for j in range(4)])
    w = f(ab_w_in)[0]
    a["w0"] = _chunks(w, np.concatenate([pairs, r(512, 640), r(768, 1280), r(640, 768)]))
    a["kr"] = w[:, 1280:1312].reshape(1, KC, P, 32).transpose(0, 2, 1, 3)
    a["uq"] = f(b_w_uq)[0].reshape(2, P, 2, 384).transpose(2, 1, 0, 3)
    kv = f(b_w_ukv)[0].reshape(2, P, 8, 2, 64)
    a["ukvk"] = kv[:, :, :, 0].reshape(1, 2, P, 512).transpose(0, 2, 1, 3)
    a["ukvv"] = kv[:, :, :, 1].reshape(1, 2, P, 512).transpose(0, 2, 1, 3)
    w1 = f(cd_w_in)[0]
    a["w1"] = _chunks(w1, np.concatenate([r(0, 512), 1536 + pairs, r(2048, 2176), r(2176, 2304), r(1024, 1536)]))
    a["vr"] = w1[:, 512:1024].reshape(4, 2, P, 512).transpose(0, 2, 1, 3)
    every = r(D)
    a["wo"] = np.stack([_chunks(f(ab_w_o)[0], every),
                        _chunks(f(cd_w_o)[0], every)])
    a["wq"] = f(peer_w_q).reshape(2, KC, P, 16, P).transpose(0, 3, 2, 1, 4)
    a["keys"] = f(peer_keys).reshape(2, 16, P, P).transpose(0, 3, 1, 2)
    a["ut"] = f(peer_u).reshape(2, P, P, KC, P).transpose(0, 2, 4, 3, 1)
    a["vt"] = f(peer_v).reshape(2, P, P, D).transpose(0, 2, 1, 3)
    tab0, tab1 = _tables()
    a["tab0"], a["tab1"] = tab0, tab1
    a["cst"] = np.stack([np.eye(P, dtype=np.float32),
                         np.tile(np.arange(P, dtype=np.float32), (P, 1))], axis=1)

    def cols(v):
        return f(v).reshape(-1, P).T

    def head(v):
        v = f(v).reshape(-1)
        return np.concatenate([v, v])[:, None] if v.size == 64 else np.pad(v, (0, P - v.size))[:, None]

    def wide(v):
        return np.tile(f(v).reshape(1, -1), (P, 1))

    cc = np.stack([cols(c), cols(c_ctx)], axis=2).reshape(P, 16)
    a["par"] = np.concatenate([
        cols(norm1_w), cols(norm2_w), cols(ada_b), head(a_q_norm), head(a_k_norm), cols(b_q_lora_norm),
        cols(b_kv_lora_norm), head(b_q_norm), head(b_k_norm), cols(c_gn_w), head(d_q_norm), head(d_k_norm),
        cc, wide(a_sink), wide(c_decay_fwd), wide(c_decay_bwd),
        np.full((P, 1), EPS, np.float32), np.ones((P, 1), np.float32)], axis=1)
    assert a["par"].shape[1] == NPR

    nc = _bacc.Bacc("TRN2", target_bir_lowering=False, num_devices=1)
    arrays, aps = {}, {}
    for name, v in a.items():
        v = np.ascontiguousarray(v)
        arrays["in_" + name] = v
        aps[name] = nc.dram_tensor("in_" + name, v.shape, F32, kind="ExternalInput").ap()
    out = nc.dram_tensor("out", (P, KC, X), F32, kind="ExternalOutput").ap()
    build(nc, aps, out)
    got = _run(nc, [arrays], core_ids=[0]).results[0]["out"]
    return np.ascontiguousarray(got.transpose(2, 1, 0).reshape(1, X, D))
```
